# Optimizing a Trainium2 kernel written in Bass

```python
import math
import jax, jax.numpy as jnp
from jax import lax
import numpy as np

D_MODEL = 1024
BATCH = 1
SEQ = 256
DEPTH = 2

N_MIXERS = 2
N_SSM_LAYERS = (DEPTH + 1) // 2
N_ATT_LAYERS = DEPTH // 2
SSM_WIDTH = D_MODEL // 2
SSM_CH = 16
SSM_GROUPS = SSM_WIDTH // SSM_CH
SSM_STATE = 64
DT_MIN, DT_MAX = 1e-3, 1e-1
HEAD_DIM = 64
N_HEADS = D_MODEL // HEAD_DIM
N_KV_HEADS = N_HEADS // 4
KV_GROUP = N_HEADS // N_KV_HEADS
IDX_HEADS = max(4, D_MODEL // 128)
IDX_DIM = 64
TOPK_MAX = 256
Q_BLOCK = 128
ROPE_THETA = 10000.0
ATT_SPLITS = (N_HEADS * HEAD_DIM, N_KV_HEADS * HEAD_DIM, N_KV_HEADS * HEAD_DIM,
              IDX_HEADS * IDX_DIM, IDX_DIM, IDX_HEADS)
ATT_IN_COLS = sum(ATT_SPLITS)
D_FF = 4 * D_MODEL
NORM_EPS = 1e-6


def rms_norm(x, g):
    xf = x.astype(jnp.float32)
    y = xf * lax.rsqrt(jnp.mean(xf * xf, axis=-1, keepdims=True) + NORM_EPS)
    return (y * g.astype(jnp.float32)).astype(x.dtype)

def rope_tables(seq_len, dim, dtype):
    half = dim // 2
    inv_freq = ROPE_THETA ** (-jnp.arange(half, dtype=jnp.float32) * 2.0 / dim)
    ang = jnp.arange(seq_len, dtype=jnp.float32)[:, None] * inv_freq[None, :]
    cos = jnp.concatenate([jnp.cos(ang), jnp.cos(ang)], axis=-1)
    sin = jnp.concatenate([jnp.sin(ang), jnp.sin(ang)], axis=-1)
    return cos.astype(dtype), sin.astype(dtype)

def apply_rope(x, cos, sin):
    half = x.shape[-1] // 2
    rot = jnp.concatenate([-x[..., half:], x[..., :half]], axis=-1)
    return x * cos[None, :, None, :] + rot * sin[None, :, None, :]

def s5_mixer(h, w_in, lam_re, lam_im, log_dt, b_re, b_im, c_re, c_im, d_skip, w_glu, w_out):
    bsz, seq, _ = h.shape
    dt_ = h.dtype
    u = (h @ w_in).reshape(bsz, seq, SSM_GROUPS, SSM_CH)
    lr = lam_re.astype(jnp.float32); li = lam_im.astype(jnp.float32)
    dt = jnp.exp(log_dt.astype(jnp.float32))[:, None]
    mag = jnp.exp(lr * dt)
    abar_re = mag * jnp.cos(li * dt)
    abar_im = mag * jnp.sin(li * dt)
    den = lr * lr + li * li
    nr = abar_re - 1.0
    ni = abar_im
    fr = (nr * lr + ni * li) / den
    fi = (ni * lr - nr * li) / den
    br = b_re.astype(jnp.float32); bi = b_im.astype(jnp.float32)
    bbar_re = (fr[..., None] * br - fi[..., None] * bi).astype(dt_)
    bbar_im = (fr[..., None] * bi + fi[..., None] * br).astype(dt_)
    bu_re = jnp.einsum('bsgc,gpc->bsgp', u, bbar_re)
    bu_im = jnp.einsum('bsgc,gpc->bsgp', u, bbar_im)
    a_re = jnp.broadcast_to(abar_re.astype(dt_), bu_re.shape)
    a_im = jnp.broadcast_to(abar_im.astype(dt_), bu_im.shape)

    def combine(left, right):
        a1r, a1i, b1r, b1i = left
        a2r, a2i, b2r, b2i = right
        return (a2r * a1r - a2i * a1i,
                a2r * a1i + a2i * a1r,
                a2r * b1r - a2i * b1i + b2r,
                a2r * b1i + a2i * b1r + b2i)

    _, _, xs_re, xs_im = lax.associative_scan(combine, (a_re, a_im, bu_re, bu_im), axis=1)
    y = (jnp.einsum('bsgp,gcp->bsgc', xs_re, c_re)
         - jnp.einsum('bsgp,gcp->bsgc', xs_im, c_im)
         + d_skip[None, None] * u)
    z = jax.nn.gelu(y.reshape(bsz, seq, SSM_WIDTH))
    z = z * jax.nn.sigmoid(z @ w_glu)
    return z @ w_out

def dsa_mixer(h, w_in, w_out):
    bsz, seq, _ = h.shape
    dt_ = h.dtype
    proj = h @ w_in
    offs = np.cumsum(ATT_SPLITS)[:-1].tolist()
    q, k, v, qi, ki, wi = jnp.split(proj, offs, axis=-1)
    cos, sin = rope_tables(seq, HEAD_DIM, dt_)
    q = apply_rope(q.reshape(bsz, seq, N_HEADS, HEAD_DIM), cos, sin)
    k = apply_rope(k.reshape(bsz, seq, N_KV_HEADS, HEAD_DIM), cos, sin)
    v = v.reshape(bsz, seq, N_KV_HEADS, HEAD_DIM)
    qi = apply_rope(qi.reshape(bsz, seq, IDX_HEADS, IDX_DIM), cos, sin)
    ki = apply_rope(ki[:, :, None, :], cos, sin)[:, :, 0, :]
    wi = wi * (IDX_HEADS ** -0.5 * IDX_DIM ** -0.5)

    k_sel = min(TOPK_MAX, seq // 4)
    n_blk = seq // Q_BLOCK
    to_blocks = lambda a: jnp.swapaxes(a.reshape((bsz, n_blk, Q_BLOCK) + a.shape[2:]), 0, 1)
    q_b, qi_b, wi_b = to_blocks(q), to_blocks(qi), to_blocks(wi)
    starts = jnp.arange(n_blk, dtype=jnp.int32) * Q_BLOCK
    key_pos = jnp.arange(seq, dtype=jnp.int32)
    b_idx = jnp.arange(bsz)[:, None, None]
    scale = HEAD_DIM ** -0.5

    def block(args):
        q_blk, qi_blk, wi_blk, t0 = args
        t = t0 + jnp.arange(Q_BLOCK, dtype=jnp.int32)
        rel = jax.nn.relu(jnp.einsum('bthd,bsd->bths', qi_blk, ki).astype(jnp.float32))
        score = jnp.einsum('bths,bth->bts', rel, wi_blk.astype(jnp.float32))
        causal = key_pos[None, :] <= t[:, None]
        score = jnp.where(causal[None], score, -jnp.inf)
        _, idx = lax.top_k(score, k_sel)
        kg = k[b_idx, idx]
        vg = v[b_idx, idx]
        qg = q_blk.reshape(bsz, Q_BLOCK, N_KV_HEADS, KV_GROUP, HEAD_DIM)
        att = jnp.einsum('btngd,btknd->btngk', qg, kg).astype(jnp.float32) * scale
        valid = idx <= t[None, :, None]
        att = jnp.where(valid[:, :, None, None, :], att, -jnp.inf)
        p = jax.nn.softmax(att, axis=-1).astype(dt_)
        o = jnp.einsum('btngk,btknd->btngd', p, vg)
        return o.reshape(bsz, Q_BLOCK, N_HEADS * HEAD_DIM)

    out = lax.map(block, (q_b, qi_b, wi_b, starts))
    out = jnp.swapaxes(out, 0, 1).reshape(bsz, seq, N_HEADS * HEAD_DIM)
    return out @ w_out

def sq_relu_mlp(h, w1, w2):
    a = jax.nn.relu(h @ w1)
    return (a * a) @ w2

def first_inputs(seed: int = 0) -> dict:
    key = jax.random.key(seed)
    ks = jax.random.split(key, 20)
    nA, nB = N_SSM_LAYERS, N_ATT_LAYERS
    G, P, C, E = SSM_GROUPS, SSM_STATE, SSM_CH, SSM_WIDTH
    nrm = lambda k, shape, fan: jax.random.normal(k, shape, jnp.float32) * (fan ** -0.5)
    x = jax.random.normal(ks[0], (BATCH, SEQ, D_MODEL), jnp.float32)
    norm_g = 1.0 + 0.01 * jax.random.normal(ks[1], (DEPTH, 4, D_MODEL), jnp.float32)
    mlp_w1 = nrm(ks[2], (DEPTH, D_MODEL, D_FF), D_MODEL)
    mlp_w2 = nrm(ks[3], (DEPTH, D_FF, D_MODEL), D_FF)
    ssm_w_in = nrm(ks[4], (nA, D_MODEL, E), D_MODEL)
    n_idx = jnp.arange(P, dtype=jnp.float32)
    ssm_lam_re = -0.5 + 0.01 * jax.random.normal(ks[5], (nA, G, P), jnp.float32)
    ssm_lam_im = math.pi * n_idx[None, None, :] + 0.01 * jax.random.normal(ks[6], (nA, G, P), jnp.float32)
    ssm_log_dt = jax.random.uniform(ks[7], (nA, G), jnp.float32, math.log(DT_MIN), math.log(DT_MAX))
    ssm_b_re = nrm(ks[8], (nA, G, P, C), 2 * C)
    ssm_b_im = nrm(ks[9], (nA, G, P, C), 2 * C)
    ssm_c_re = nrm(ks[10], (nA, G, C, P), 2 * P)
    ssm_c_im = nrm(ks[11], (nA, G, C, P), 2 * P)
    ssm_d = jax.random.normal(ks[12], (nA, G, C), jnp.float32)
    ssm_w_glu = nrm(ks[13], (nA, E, E), E)
    ssm_w_out = nrm(ks[14], (nA, E, D_MODEL), E)
    att_w_in = nrm(ks[15], (nB, D_MODEL, ATT_IN_COLS), D_MODEL)
    att_w_out = nrm(ks[16], (nB, N_HEADS * HEAD_DIM, D_MODEL), N_HEADS * HEAD_DIM)
    return {"x": x, "norm_g": norm_g, "mlp_w1": mlp_w1, "mlp_w2": mlp_w2,
            "ssm_w_in": ssm_w_in, "ssm_lam_re": ssm_lam_re, "ssm_lam_im": ssm_lam_im,
            "ssm_log_dt": ssm_log_dt, "ssm_b_re": ssm_b_re, "ssm_b_im": ssm_b_im,
            "ssm_c_re": ssm_c_re, "ssm_c_im": ssm_c_im, "ssm_d": ssm_d,
            "ssm_w_glu": ssm_w_glu, "ssm_w_out": ssm_w_out,
            "att_w_in": att_w_in, "att_w_out": att_w_out}

def first_block(x, norm_g, mlp_w1, mlp_w2, ssm_w_in, ssm_lam_re, ssm_lam_im, ssm_log_dt,
              ssm_b_re, ssm_b_im, ssm_c_re, ssm_c_im, ssm_d, ssm_w_glu, ssm_w_out,
              att_w_in, att_w_out):
    h = x
    for i in range(DEPTH):
        j = i // N_MIXERS
        pre = rms_norm(h, norm_g[i, 0])
        if i % N_MIXERS == 0:
            mix = s5_mixer(pre, ssm_w_in[j], ssm_lam_re[j], ssm_lam_im[j], ssm_log_dt[j],
                           ssm_b_re[j], ssm_b_im[j], ssm_c_re[j], ssm_c_im[j], ssm_d[j],
                           ssm_w_glu[j], ssm_w_out[j])
        else:
            mix = dsa_mixer(pre, att_w_in[j], att_w_out[j])
        h = h + rms_norm(mix, norm_g[i, 1])
        ff = sq_relu_mlp(rms_norm(h, norm_g[i, 2]), mlp_w1[i], mlp_w2[i])
        h = h + rms_norm(ff, norm_g[i, 3])
    return h


DEPTH_2 = 1

SSD_EXPAND = 2
D_INNER = SSD_EXPAND * D_MODEL
SSD_HEAD_DIM = 64
SSD_HEADS = D_INNER // SSD_HEAD_DIM
SSD_GROUPS = 8
D_STATE = 128
SSD_CONV = 4
SSD_CHUNK = 128
SSD_CONV_DIM = D_INNER + 2 * SSD_GROUPS * D_STATE
SSD_NORM_GROUP = D_INNER // SSD_GROUPS
ATTN_WINDOWS = (128, 512, 2048)
ATTN_DILATIONS = (1, 4, 16)
ATTN_N_GROUPS = 3
ATTN_HEADS_PER_GROUP = 8
ATTN_HEAD_DIM = 64
ATTN_BLOCK = 128
ATTN_WIDTH = ATTN_N_GROUPS * ATTN_HEADS_PER_GROUP * ATTN_HEAD_DIM
ATTN_OUT = ATTN_HEADS_PER_GROUP * ATTN_HEAD_DIM
D_FF_2 = 2816
FFN_CONV = 3
EPS = 1e-6
IN_WIDTHS = (D_INNER, SSD_CONV_DIM, SSD_HEADS, ATTN_WIDTH, ATTN_WIDTH, ATTN_WIDTH, D_MODEL, D_MODEL)
IN_SPLITS = tuple(sum(IN_WIDTHS[:i + 1]) for i in range(len(IN_WIDTHS) - 1))
D_IN_PROJ = sum(IN_WIDTHS)


def rms_norm_2(x, g):
    xf = x.astype(jnp.float32)
    y = xf * lax.rsqrt(jnp.mean(xf * xf, axis=-1, keepdims=True) + EPS)
    return (y * g.astype(jnp.float32)).astype(x.dtype)

def causal_dwconv(x, w, bias):
    K = w.shape[0]
    s = x.shape[1]
    xp = jnp.pad(x, ((0, 0), (K - 1, 0), (0, 0)))
    out = bias
    for i in range(K):
        out = out + xp[:, i:i + s] * w[i]
    return out

def ssd_chunked(xs, dt, A, Bm, Cm):
    b, s, H, P = xs.shape
    G, N = Bm.shape[2], Bm.shape[3]
    K = H // G
    Q = SSD_CHUNK
    c = s // Q
    X = (xs * dt[..., None]).reshape(b, c, Q, G, K, P)
    a = (dt * A).reshape(b, c, Q, G, K).transpose(0, 1, 3, 4, 2)
    a_cs = jnp.cumsum(a, axis=-1)
    Bc = Bm.reshape(b, c, Q, G, N)
    Cc = Cm.reshape(b, c, Q, G, N)
    causal = jnp.tril(jnp.ones((Q, Q), dtype=bool))
    seg = a_cs[..., :, None] - a_cs[..., None, :]
    Ldec = jnp.exp(jnp.where(causal, seg, -jnp.inf))
    CB = jnp.einsum('bclgn,bcsgn->bcgls', Cc, Bc)
    y_diag = jnp.einsum('bcgkls,bcsgkp->bclgkp', CB[:, :, :, None] * Ldec, X)
    decay_states = jnp.exp(a_cs[..., -1:] - a_cs)
    states = jnp.einsum('bclgn,bcgkl,bclgkp->bcgkpn', Bc, decay_states, X)
    chunk_decay = jnp.exp(a_cs[..., -1])

    def step(carry, inp):
        st, dec = inp
        return carry * dec[..., None, None] + st, carry

    init = jnp.zeros((b, G, K, P, N), jnp.float32)
    _, prev = lax.scan(step, init, (jnp.moveaxis(states, 1, 0), jnp.moveaxis(chunk_decay, 1, 0)))
    prev = jnp.moveaxis(prev, 0, 1)
    y_off = jnp.einsum('bclgn,bcgkpn,bcgkl->bclgkp', Cc, prev, jnp.exp(a_cs))
    return (y_diag + y_off).reshape(b, s, H, P)

def ssd_branch(z, xbc, dt_raw, conv_w, conv_b, dt_bias, a_log, d_skip, norm_g):
    b, s, _ = z.shape
    f32 = jnp.float32
    xbc = jax.nn.silu(causal_dwconv(xbc, conv_w, conv_b))
    xs, Bm, Cm = jnp.split(xbc, (D_INNER, D_INNER + SSD_GROUPS * D_STATE), axis=-1)
    xs = xs.reshape(b, s, SSD_HEADS, SSD_HEAD_DIM).astype(f32)
    Bm = Bm.reshape(b, s, SSD_GROUPS, D_STATE).astype(f32)
    Cm = Cm.reshape(b, s, SSD_GROUPS, D_STATE).astype(f32)
    dt = jax.nn.softplus(dt_raw.astype(f32) + dt_bias.astype(f32))
    A = -jnp.exp(a_log.astype(f32))
    y = ssd_chunked(xs, dt, A, Bm, Cm) + d_skip.astype(f32)[:, None] * xs
    y = y.reshape(b, s, D_INNER) * jax.nn.silu(z.astype(f32))
    y = rms_norm_2(y.reshape(b, s, SSD_GROUPS, SSD_NORM_GROUP), norm_g.reshape(SSD_GROUPS, SSD_NORM_GROUP))
    return y.reshape(b, s, D_INNER).astype(z.dtype)

def dilated_window_attention(q, k, v, dil, n_back):
    b, s, h, hd = q.shape
    L = s // dil
    nb = -(-L // ATTN_BLOCK)
    Lp = nb * ATTN_BLOCK

    def to_sub(t):
        t = t.reshape(b, L, dil, h, hd).transpose(0, 2, 1, 3, 4).reshape(b * dil, L, h, hd)
        t = jnp.pad(t, ((0, 0), (0, Lp - L), (0, 0), (0, 0)))
        return t.reshape(b * dil, nb, ATTN_BLOCK, h, hd)

    def with_prev(t):
        prev = jnp.pad(t, ((0, 0), (1, 0), (0, 0), (0, 0), (0, 0)))[:, :-1]
        return jnp.concatenate([prev, t], axis=2)

    qb = to_sub(q)
    kc = with_prev(to_sub(k))
    vc = with_prev(to_sub(v))
    scores = jnp.einsum('znqhd,znkhd->znhqk', qb, kc) * (hd ** -0.5)
    qi = jnp.arange(ATTN_BLOCK)[:, None]
    ki = jnp.arange(2 * ATTN_BLOCK)[None, :]
    dist = ATTN_BLOCK + qi - ki
    band = (dist >= 0) & (dist <= n_back)
    key_pos = (jnp.arange(nb)[:, None, None] - 1) * ATTN_BLOCK + ki[None]
    mask = band[None] & (key_pos >= 0)
    scores = jnp.where(mask[None, :, None], scores, -jnp.inf)
    m = jnp.max(scores, axis=-1, keepdims=True)
    p = jnp.exp(scores - m)
    den = jnp.sum(p, axis=-1, keepdims=True)
    o = jnp.einsum('znhqk,znkhd->znqhd', p / den, vc)
    lse = (m + jnp.log(den))[..., 0]
    o = o.reshape(b, dil, Lp, h, hd)[:, :, :L].transpose(0, 2, 1, 3, 4).reshape(b, s, h, hd)
    lse = lse.transpose(0, 1, 3, 2).reshape(b, dil, Lp, h)[:, :, :L].transpose(0, 2, 1, 3).reshape(b, s, h)
    return o, lse

def attn_branch(q, k, v, q_norm_g, k_norm_g):
    b, s, _ = q.shape
    f32 = jnp.float32
    shp = (b, s, ATTN_N_GROUPS, ATTN_HEADS_PER_GROUP, ATTN_HEAD_DIM)
    qn = rms_norm_2(q.reshape(shp), q_norm_g).astype(f32)
    kn = rms_norm_2(k.reshape(shp), k_norm_g).astype(f32)
    vv = v.reshape(shp).astype(f32)
    outs, lses = [], []
    for gi in range(ATTN_N_GROUPS):
        o, lse = dilated_window_attention(qn[:, :, gi], kn[:, :, gi], vv[:, :, gi],
                                          ATTN_DILATIONS[gi], ATTN_WINDOWS[gi] // ATTN_DILATIONS[gi])
        outs.append(o)
        lses.append(lse)
    wts = jax.nn.softmax(jnp.stack(lses, axis=0), axis=0)
    o = jnp.einsum('gbsh,gbshd->bshd', wts, jnp.stack(outs, axis=0))
    return o.reshape(b, s, ATTN_OUT).astype(q.dtype)

def second_inputs(seed: int = 0) -> dict:
    key = jax.random.key(seed)
    ks = jax.random.split(key, 20)
    f32 = jnp.float32

    def dense(k, shape, fan_in):
        return jax.random.normal(k, shape, f32) * fan_in ** -0.5

    def gain(k, shape):
        return 1.0 + 0.05 * jax.random.normal(k, shape, f32)

    x = jax.random.normal(ks[0], (BATCH, SEQ, D_MODEL), f32)
    norm1_g = gain(ks[1], (DEPTH_2, D_MODEL))
    w_in = dense(ks[2], (DEPTH_2, D_MODEL, D_IN_PROJ), D_MODEL)
    ssd_conv_w = dense(ks[3], (DEPTH_2, SSD_CONV, SSD_CONV_DIM), SSD_CONV)
    ssd_conv_b = 0.02 * jax.random.normal(ks[4], (DEPTH_2, SSD_CONV_DIM), f32)
    dt0 = jnp.exp(jax.random.uniform(ks[5], (DEPTH_2, SSD_HEADS), f32, math.log(1e-3), math.log(1e-1)))
    dt_bias = dt0 + jnp.log(-jnp.expm1(-dt0))
    a_log = jnp.log(jax.random.uniform(ks[6], (DEPTH_2, SSD_HEADS), f32, 1.0, 16.0))
    d_skip = 1.0 + 0.1 * jax.random.normal(ks[7], (DEPTH_2, SSD_HEADS), f32)
    ssd_norm_g = gain(ks[8], (DEPTH_2, D_INNER))
    w_ssd_proj = dense(ks[9], (DEPTH_2, D_INNER, D_MODEL), D_INNER)
    q_norm_g = gain(ks[10], (DEPTH_2, ATTN_HEAD_DIM))
    k_norm_g = gain(ks[11], (DEPTH_2, ATTN_HEAD_DIM))
    w_attn_proj = dense(ks[12], (DEPTH_2, ATTN_OUT, D_MODEL), ATTN_OUT)
    w_out = dense(ks[13], (DEPTH_2, D_MODEL, D_MODEL), D_MODEL)
    norm2_g = gain(ks[14], (DEPTH_2, D_MODEL))
    w_up = dense(ks[15], (DEPTH_2, D_MODEL, 2 * D_FF_2), D_MODEL)
    ffn_conv_w = dense(ks[16], (DEPTH_2, FFN_CONV, 2 * D_FF_2), FFN_CONV)
    ffn_conv_b = 0.02 * jax.random.normal(ks[17], (DEPTH_2, 2 * D_FF_2), f32)
    w_down = dense(ks[18], (DEPTH_2, D_FF_2, D_MODEL), D_FF_2)
    return {'x': x, 'norm1_g': norm1_g, 'w_in': w_in, 'ssd_conv_w': ssd_conv_w, 'ssd_conv_b': ssd_conv_b,
            'dt_bias': dt_bias, 'a_log': a_log, 'd_skip': d_skip, 'ssd_norm_g': ssd_norm_g,
            'w_ssd_proj': w_ssd_proj, 'q_norm_g': q_norm_g, 'k_norm_g': k_norm_g,
            'w_attn_proj': w_attn_proj, 'w_out': w_out, 'norm2_g': norm2_g, 'w_up': w_up,
            'ffn_conv_w': ffn_conv_w, 'ffn_conv_b': ffn_conv_b, 'w_down': w_down}

def second_block(x, norm1_g, w_in, ssd_conv_w, ssd_conv_b, dt_bias, a_log, d_skip, ssd_norm_g,
              w_ssd_proj, q_norm_g, k_norm_g, w_attn_proj, w_out, norm2_g, w_up,
              ffn_conv_w, ffn_conv_b, w_down):
    for l in range(DEPTH_2):
        h = rms_norm_2(x, norm1_g[l])
        proj = h @ w_in[l]
        z, xbc, dt_raw, q, k, v, g_ssd, g_attn = jnp.split(proj, IN_SPLITS, axis=-1)
        y_ssd = ssd_branch(z, xbc, dt_raw, ssd_conv_w[l], ssd_conv_b[l], dt_bias[l], a_log[l],
                           d_skip[l], ssd_norm_g[l])
        y_attn = attn_branch(q, k, v, q_norm_g[l], k_norm_g[l])
        merged = (jax.nn.sigmoid(g_ssd) * (y_ssd @ w_ssd_proj[l])
                  + jax.nn.sigmoid(g_attn) * (y_attn @ w_attn_proj[l]))
        x = x + merged @ w_out[l]
        h2 = rms_norm_2(x, norm2_g[l])
        u = causal_dwconv(h2 @ w_up[l], ffn_conv_w[l], ffn_conv_b[l])
        u_gate, u_val = jnp.split(u, 2, axis=-1)
        x = x + (jax.nn.silu(u_gate) * u_val) @ w_down[l]
    return x


def setup_inputs(seed=0):
    out = dict(first_inputs(seed))
    for name, value in second_inputs(seed + 1).items():
        if name != "x":
            out[name + "_2"] = value
    return out


def reference(
    x, norm_g, mlp_w1, mlp_w2, ssm_w_in, ssm_lam_re, ssm_lam_im, ssm_log_dt, ssm_b_re, ssm_b_im,
    ssm_c_re, ssm_c_im, ssm_d, ssm_w_glu, ssm_w_out, att_w_in, att_w_out, norm1_g_2, w_in_2,
    ssd_conv_w_2, ssd_conv_b_2, dt_bias_2, a_log_2, d_skip_2, ssd_norm_g_2, w_ssd_proj_2,
    q_norm_g_2, k_norm_g_2, w_attn_proj_2, w_out_2, norm2_g_2, w_up_2, ffn_conv_w_2,
    ffn_conv_b_2, w_down_2,
):
    x = first_block(
        x, norm_g, mlp_w1, mlp_w2, ssm_w_in, ssm_lam_re, ssm_lam_im, ssm_log_dt, ssm_b_re,
        ssm_b_im, ssm_c_re, ssm_c_im, ssm_d, ssm_w_glu, ssm_w_out, att_w_in, att_w_out,
    )
    return second_block(
        x, norm1_g_2, w_in_2, ssd_conv_w_2, ssd_conv_b_2, dt_bias_2, a_log_2, d_skip_2,
        ssd_norm_g_2, w_ssd_proj_2, q_norm_g_2, k_norm_g_2, w_attn_proj_2, w_out_2, norm2_g_2,
        w_up_2, ffn_conv_w_2, ffn_conv_b_2, w_down_2,
    )


_drawn_inputs = setup_inputs


def setup_inputs(seed=0):
    import zlib

    import numpy as np

    out = dict(_drawn_inputs(seed))
    spreads = {}
    factors = {'ssm_lam_re': 49.958,
     'norm1_g_2': 2.832,
     'ssd_conv_b_2': 8.0,
     'd_skip_2': 21.654,
     'ssd_norm_g_2': 4.318,
     'q_norm_g_2': 8.0,
     'k_norm_g_2': 8.0,
     'norm2_g_2': 3.214,
     'ffn_conv_b_2': 8.0}
    for name, (base, spread) in spreads.items():
        noise = np.random.default_rng([zlib.crc32(name.encode()), seed]).standard_normal(out[name].shape)
        drawn = base * np.exp(spread * noise) if base else spread * noise
        out[name] = __import__('jax').numpy.asarray(drawn.astype(out[name].dtype))
    for name, factor in factors.items():
        out[name] = (out[name] * factor).astype(out[name].dtype)
    return out
```

```python
import concourse.bass as bass
from concourse import mybir
from contextlib import ExitStack

import numpy as np

F32 = mybir.dt.float32
F32R = mybir.dt.float32r
BF16 = mybir.dt.bfloat16
I32 = mybir.dt.int32
ALU = mybir.AluOpType
ACT = mybir.ActivationFunctionType
AXIS = mybir.AxisListType

P = 128
SEQ = 256
TB = SEQ // P
D = 1024
KD = D // P
EPS = 1e-6
NEG = -1e30
TAKEN = -3e38

GROUPS, CH, STATE, E5 = 32, 16, 64, 512
ST = GROUPS * STATE // P
DFF = 4 * D
MC = DFF // 256
NH, NKV, HD, IH, TOPK = 16, 4, 64, 8, 64
QW, KW, IW = NH * HD, NKV * HD, IH * HD
VOFF, QIOFF = QW + KW, QW + 2 * KW
KIOFF = QIOFF + IW
WIOFF = KIOFF + HD
ATT_COLS = WIOFF + IH
ATT_TAIL = ATT_COLS - 4 * 512
DIN, SG, SH, DSTATE = 2048, 8, 32, 128
ZOFF, XSOFF = 0, DIN
BOFF = XSOFF + DIN
COFF = BOFF + SG * DSTATE
DTOFF = COFF + SG * DSTATE
AW = 3 * 8 * 64
Q2OFF = DTOFF + SH
K2OFF, V2OFF = Q2OFF + AW, Q2OFF + 2 * AW
GATEOFF = Q2OFF + 3 * AW
DFF2 = 2816
FC = DFF2 // P

C_ID, C_UU, C_GT, C_NEGT, C_CAUS, C_DIL, C_COS, C_SIN, C_SEL, C_PAR = (
    0, 128, 384, 512, 640, 768, 1536, 1664, 1792, 1920)
C_END = 1924
R_NG, R_N1, R_N2, R_SN, R_D, R_LR = 0, 64, 72, 80, 96, 100
R_CB, R_FB, R_LI, R_QG, R_KG = 0, 32, 76, 92, 93
ROWS = [116, 128, 94, 88, 44]
N_PARAM = 24
JOBS1 = [(0, h0, 4) for h0 in (0, 1, 8, 9)] + [(1, h0, 2) for h0 in (0, 1, 4, 5, 8, 9, 12, 13)]
IJOBS = [(0, h0, 4) for h0 in (0, 1)] + [(1, h0, 2) for h0 in (0, 1, 4, 5)]
JOBS2 = [(2 * pr + hh, tb) for pr in range(4) for tb in range(TB) for hh in range(2)]
G_WX, G_WB, G_WC, G_BX, G_BB, G_BC, G_NG, G_D, G_DT, G_A, G_NB, G_END = 0, 8, 12, 16, 18, 19, 20, 22, 24, 32, 40, 52
P_ATT, P_B2, P_SSD, P_WOUT2 = 37, 82, 111, 143


class Ring:

    def __init__(self):
        self.n, self.uses, self.off = 0, [0] * 4, 0

    def next(self):
        s, k, n = self.n % 4, self.uses[self.n % 4] + self.off, self.n + self.off * 4
        self.n += 1
        self.uses[s] += 1
        return s, k, n

    def enter(self, i, per_slot):
        self.off, self.per = i * per_slot, per_slot

    def leave(self, turns):
        self.off = 0
        self.n += 4 * self.per * (turns - 1)
        self.uses = [u + self.per * (turns - 1) for u in self.uses]


class Steps:

    def __init__(self, eng, sem):
        self.eng, self.sem, self.n, self.off = eng, sem, 0, 0

    def link(self, ins):
        ins.then_inc(self.sem, 1)
        self.n += 1
        self.eng.wait_ge(self.sem, self.off + self.n)

    def enter(self, i, per):
        self.off, self.start, self.per = i * per, self.n, per

    def leave(self, turns):
        assert self.n - self.start == self.per, (self.n - self.start, self.per)
        self.n += self.per * (turns - 1)
        self.off = 0


def build(nc, ins, out):
    ctx = ExitStack()
    with ctx:
        def sb(name, shape, dt=F32):
            return ctx.enter_context(nc.sbuf_tensor(name, shape, dt))

        sems = {}

        def S(name):
            if name not in sems:
                sems[name] = ctx.enter_context(nc.semaphore(name))
            return sems[name]

        raw = sb("raw", [P, 2, 2048])
        HI = sb("HI", [P, 4, 2048], F32R)
        LO = sb("LO", [P, 4, 2048], F32R)
        XH = sb("XH", [P, KD, SEQ], F32R)
        XL = sb("XL", [P, KD, SEQ], F32R)
        HH = sb("HH", [P, 2, 2, SEQ], F32R)
        HL = sb("HL", [P, 2, 2, SEQ], F32R)
        OH = HH[:, :, :, :].rearrange("p a b t -> p (a b) t")
        OL = HL[:, :, :, :].rearrange("p a b t -> p (a b) t")
        cst = sb("cst", [P, C_END])
        cols = sb("cols", [P, 5, P])
        gpall = sb("gpall", [P, SG, G_END])
        gp = sb("gp", [P, 2, G_END])
        fpall = sb("fpall", [P, FC, 8])
        fp = sb("fp", [P, 2, 8])
        h = sb("h", [P, TB, D])
        y = sb("y", [P, TB, D])
        gbc = sb("gbc", [P, 2, D])
        zero_bf = sb("zero_bf", [P, 512], BF16)
        id_bf = sb("id_bf", [P, P], BF16)
        neg_bf = sb("neg_bf", [P, P], BF16)
        ones = sb("ones", [P, P])
        ssq = sb("ssq", [P, 2])
        nv = sb("nv", [P, 2])
        nt = sb("nt", [P, 2])
        rstd = sb("rstd", [P, 2])
        arena = sb("arena", [P, 15520])
        acc = ctx.enter_context(nc.psum_tensor("acc", [P, TB, D], F32))
        wk = ctx.enter_context(nc.psum_tensor("wk", [P, 4, 512], F32))
        accf = acc[:, :, :].rearrange("p a n -> p (a n)")

        def carve(at, *shape):
            n = int(np.prod(shape))
            v = arena[:, at:at + n]
            if len(shape) == 2:
                return v.rearrange("p (a b) -> p a b", a=shape[0])
            if len(shape) == 3:
                return v.rearrange("p (a b c) -> p a b c", a=shape[0], b=shape[1])
            return v

        ident = cst[:, C_ID:C_ID + P]
        cosT = cst[:, C_COS:C_COS + 128].rearrange("p (b d) -> p b d", b=TB)
        sinT = cst[:, C_SIN:C_SIN + 128].rearrange("p (b d) -> p b d", b=TB)
        dilm = cst[:, C_DIL:C_DIL + 768].rearrange("p (g n) -> p g n", g=3)

        def pcol(block, r):
            return cols[:, block, r:r + 1]

        def gain(layer, which, k):
            return pcol(0, R_NG + (layer * 4 + which) * 8 + k)

        e_tab = carve(0, ST, 2, SEQ)
        s5 = 8192
        uT = carve(s5, 4, SEQ)
        rows = carve(s5 + 1024, 5, P)
        rotA = carve(s5 + 1024, 2, SEQ)
        rotB = carve(s5 + 1536, 2, SEQ)
        zz = carve(s5 + 2048, 2, 2, SEQ)
        rotC = carve(s5 + 3072, 2, SEQ)
        rotD = carve(s5 + 3584, 2, SEQ)
        xs5 = carve(s5 + 4096, 2, 2, SEQ)
        bt5 = carve(s5 + 5120, 2, 4, P)
        ct5 = carve(s5 + 6144, 2, 4, P)
        sm5 = carve(s5 + 7168, 10, 16)
        bpad = carve(s5 + 2048, 2, 16, 32)
        cpad = carve(s5 + 3072, 2, 4, P)
        braw = carve(s5 + 4096, 2, 16, 16)
        craw = carve(s5 + 4608, 2, 4, 64)
        bq = carve(s5 + 1664, 16, 16)
        etmp = y[:, :, :].rearrange("p b n -> p (b n)")
        yv = carve(0, 4, SEQ)
        gt5 = carve(2048, 4, SEQ)
        zf = y[:, 0, :].rearrange("p (q t) -> p q t", q=4)
        z2f = y[:, 1, :].rearrange("p (q t) -> p q t", q=4)
        pair = sb("pair", [2, 32])
        pairb = sb("pairb", [P, 32])
        alog = sb("alog", [P, SH])
        dtb = sb("dtb", [P, SH])

        relu_b = carve(0, 2, 512)
        sq_b = carve(1024, 2, 512)
        pj = carve(0, TB, ATT_COLS)
        qT1 = carve(4240, 8, SEQ)
        kT1 = carve(6288, 4, SEQ)
        qiT = carve(7312, 4, SEQ)
        kiT = carve(8336, SEQ)
        rope1 = carve(8592, 1280)
        rope2 = carve(9872, 1280)
        roped = carve(11152, TB, 2176)
        rel = carve(8592, 2, 512)
        score = carve(9616, TB, SEQ)
        left = carve(10128, TB, SEQ)
        keep = carve(10640, TB, SEQ)
        p1 = carve(11152, 3, 512)
        pT1 = carve(12688, 2, 512)
        qk2 = carve(0, TB, AW)
        v2 = carve(3072, TB, AW)
        qT2 = carve(6144, 12, SEQ)
        kT2 = carve(9216, 12, SEQ)
        p2 = carve(0, 2, 768)
        pT2 = carve(1536, 2, 768)
        g_ssd = carve(12288, TB, D)
        dt_tok = carve(14336, TB, SH)
        a_tok = carve(14400, TB, SH)
        sp1 = carve(14464, TB, SH)
        sp2 = carve(14528, TB, SH)
        sp3 = carve(14592, TB, SH)
        hv2 = carve(14656, 24)
        ht2 = carve(14680, 24)
        hr2 = carve(14704, 24)
        zc = carve(0, 2, 2, SEQ)
        zt = carve(1024, 2, 2, SEQ)
        xpad = carve(2048, 2, 260)
        xconv = carve(2568, 2, SEQ)
        xtanh = carve(3080, 2, SEQ)
        xsc = carve(3592, 2, 2, SEQ)
        bcpad = carve(4616, 2, 260)
        bconv = carve(5136, 2, SEQ)
        btanh = carve(5648, 2, SEQ)
        bcc = carve(6160, 2, 2, SEQ)
        Lm = carve(7184, 4, 384)
        Xt = carve(8720, TB, SEQ)
        cbs = carve(9232, 384)
        yz = carve(9616, 2, 2, SEQ)
        sq2 = carve(10640, 2, SEQ)
        gv_ = carve(11152, SEQ)
        gt_ = carve(11408, SEQ)
        gr_ = carve(11664, SEQ)
        yn = carve(14900, 2, SEQ)
        fpad = carve(0, 2, 2, 260)
        fconv = carve(1040, 2, 2, SEQ)
        ftanh = carve(2064, 2, SEQ)
        fhid = carve(2576, 2, SEQ)
        wkf = wk[:, :, :].rearrange("p b n -> p (b n)")
        yf = y[:, :, :].rearrange("p b n -> p (b n)")
        small = sb("small", [P, 2, 4, 4])
        top8 = sb("top8", [P, 8])
        wi_s = sb("wi_s", [P, TB, IH])

        block = ctx.enter_context(nc.Block())

        def kview(w):
            return w.rearrange("(k p) n -> p k n", p=P)

        w1 = [kview(ins["mlp_w1"][l]) for l in range(2)]
        w2 = [kview(ins["mlp_w2"][l]) for l in range(2)]
        sw_in, sw_glu, sw_out = (kview(ins[n][0]) for n in ("ssm_w_in", "ssm_w_glu", "ssm_w_out"))
        aw_in, aw_out = kview(ins["att_w_in"][0]), kview(ins["att_w_out"][0])
        w_in2, w_ssd, w_atp, w_out2, w_up, w_dn = (
            kview(ins[n][0]) for n in ("w_in_2", "w_ssd_proj_2", "w_attn_proj_2", "w_out_2", "w_up_2", "w_down_2"))

        @block.sync
        def _(sp):
            ring = Ring()

            def load(a, b, shape):
                first = ring.n < 2
                s, k, _ = ring.next()
                if not first:
                    if s >= 2:
                        sp.wait_ge(S(f"lo_ready{s - 2}"), k + 1)
                    else:
                        sp.wait_ge(S(f"lo_ready{s + 2}"), k)
                half, n = shape
                for i, src in enumerate((a, b)):
                    dst = raw[:, s % 2, i * half * n:(i + 1) * half * n]
                    sp.dma_start(dst.rearrange("p (k n) -> p k n", n=n), src).then_inc(S(f"loaded{s}"), 16)

            def up(w, c0):
                cs = bass.ds(c0, 256)
                load(w[:, 0:4, cs], w[:, 4:8, cs], (4, 256))

            def chunk4(w, c0):
                for kk in (0, 4):
                    cs = bass.ds(c0, 512)
                    load(w[:, kk:kk + 2, cs], w[:, kk + 2:kk + 4, cs], (2, 512))

            def down(w, k0):
                load(w[:, bass.ds(k0, 1), :], w[:, bass.ds(k0 + 1, 1), :], (1, 1024))

            def narrow(w, c0, n):
                load(w[:, 0:4, c0:c0 + n], w[:, 4:8, c0:c0 + n], (4, n))

            up(sw_in, 0)
            up(sw_in, 256)
            load(sw_glu[:, 0:2, :], sw_glu[:, 2:4, :], (2, 512))
            down(sw_out, 0)
            down(sw_out, 2)

            def mlp(layer):
                up(w1[layer], 0)
                with sp.Fori(0, (MC - 2) // 2) as i:
                    ring.enter(i, 1)
                    up(w1[layer], i * 512 + 256)
                    down(w2[layer], i * 4)
                    up(w1[layer], i * 512 + 512)
                    down(w2[layer], i * 4 + 2)
                ring.leave((MC - 2) // 2)
                up(w1[layer], (MC - 1) * 256)
                down(w2[layer], 2 * MC - 4)
                down(w2[layer], 2 * MC - 2)

            mlp(0)
            for c in range(4):
                chunk4(aw_in, 512 * c)
            narrow(aw_in, 2048, ATT_TAIL)
            for k in range(0, KD, 2):
                down(aw_out, k)
            mlp(1)
            narrow(w_in2, DTOFF, SH)
            for off in (Q2OFF, V2OFF, K2OFF):
                for c in range(3):
                    chunk4(w_in2, off + 512 * c)
            for c in range(8):
                up(w_in2, GATEOFF + 256 * c)
            down(w_atp, 0)
            down(w_atp, 2)

            def ssd_step(g, with_out):
                up(w_in2, g * 256 + ZOFF)
                up(w_in2, g * 256 + XSOFF)
                if with_out:
                    down(w_ssd, g * 2 - 4)
                load(w_in2[:, :, bass.ds(g * P + BOFF, P)], w_in2[:, :, bass.ds(g * P + COFF, P)], (8, P))

            ssd_step(0, False)
            ssd_step(1, False)
            with sp.Fori(0, 3) as i:
                ring.enter(i, 2)
                ssd_step(i * 2 + 2, True)
                ssd_step(i * 2 + 3, True)
            ring.leave(3)
            down(w_ssd, 12)
            down(w_ssd, 14)
            for k in range(0, KD, 2):
                down(w_out2, k)

            def gate_val(c):
                load(w_up[:, :, bass.ds(c * P, P)], w_up[:, :, bass.ds(c * P + DFF2, P)], (8, P))

            def down1(c):
                load(w_dn[:, bass.ds(c, 1), 0:512], w_dn[:, bass.ds(c, 1), 512:1024], (1, 512))

            gate_val(0)
            with sp.Fori(0, (FC - 2) // 2) as i:
                ring.enter(i, 1)
                gate_val(i * 2 + 1)
                down1(i * 2)
                gate_val(i * 2 + 2)
                down1(i * 2 + 1)
            ring.leave((FC - 2) // 2)
            gate_val(FC - 1)
            down1(FC - 2)
            down1(FC - 1)
            sp.wait_ge(S("out_ready"), 1)
            sp.dma_start(out[0].rearrange("(b p) n -> p b n", p=P), y[:, :, :]).then_inc(S("out_stored"), 16)
            sp.wait_ge(S("out_stored"), 16)

        SMALL = {P_ATT + 8: 8 * ATT_TAIL, P_B2: 8 * SH}

        def size(n):
            if n >= P_WOUT2 + 4:
                m = n - P_WOUT2 - 4
                return 1024 if (m in (42, 43) or (m % 2 == 0 and 2 <= m < 42)) else 2048
            return SMALL.get(n, 2048)

        def low_part(eng, ring, mine, n):
            s, k, _ = ring.next()
            if s % 2 == mine:
                eng.wait_ge(S(f"hi_ready{s}"), k + 1)
                eng.tensor_tensor(LO[:, s, 0:n], raw[:, s % 2, 0:n], HI[:, s, 0:n].bitcast(F32),
                                  ALU.subtract).then_inc(S(f"lo_ready{s}"), 1)

        @block.gpsimd
        def _(pool):
            ring = Ring()
            steps = Steps(pool, S("pool_step"))
            nc.gpsimd.memset(ones[:, :], 1.0).then_inc(S("ones_set"), 1)

            def upto(n):
                while ring.n <= n:
                    low_part(nc.gpsimd, ring, 0, size(ring.n))

            def loop(turns, per, first):
                with pool.Fori(0, turns) as i:
                    ring.enter(i, per)
                    for j in range(4 * per):
                        low_part(nc.gpsimd, ring, 0, size(first + j))
                ring.leave(turns)

            upto(3)
            for i in range(ST):
                pool.wait_ge(S("z5_ready"), i + 1)
                nc.gpsimd.tensor_tensor(rotD[:, 0, :], zz[:, i % 2, 0, :], e_tab[:, i, 1, :], ALU.mult)
                steps.link(nc.gpsimd.tensor_tensor(rotD[:, 1, :], zz[:, i % 2, 1, :], e_tab[:, i, 0, :], ALU.mult))
                if i >= 2:
                    pool.wait_ge(S("x5_used"), i - 1)
                nc.gpsimd.tensor_tensor(xs5[:, i % 2, 1, :], rotD[:, 0, :], rotD[:, 1, :],
                                        ALU.add).then_inc(S("xi5_ready"), 1)
                pool.wait_ge(S("xi5_ready"), i + 1)
            upto(5)
            loop(7, 1, 6)
            upto(P_ATT + 13)
            loop(7, 1, P_ATT + 14)
            upto(P_SSD + 5)
            loop(3, 2, P_SSD + 6)
            upto(P_WOUT2 + 4)
            loop(10, 1, P_WOUT2 + 5)
            upto(P_WOUT2 + 4 + 43)

        @block.tensor
        def _(pe):
            ring = Ring()
            mm = nc.tensor.matmul

            def arrived():
                s, k, _ = ring.next()
                pe.wait_ge(S(f"lo_ready{s}"), k + 1)
                return s

            def used(ins):
                ins.then_inc(S("piece_done"), 1)

            def three(o, lh, ll, rh, rl, start, stop, skip=False):
                mm(o, lh, rh, start=start, stop=False, skip_group_check=skip)
                mm(o, lh, rl, start=False, stop=False, skip_group_check=skip)
                return mm(o, ll, rh, start=False, stop=stop, skip_group_check=skip)

            def ch_major(s, bank, paired=False):
                for j in range(2):
                    for k in range(KD):
                        w = (j * KD + k) * P if paired else k * 256 + j * P
                        last = three(wk[:, bank, j * SEQ:(j + 1) * SEQ], HI[:, s, w:w + P], LO[:, s, w:w + P],
                                     XH[:, k, :], XL[:, k, :], k == 0, k == KD - 1)
                return last

            def tok_major(s, outs, k0, kt, n, start, stop, xh=XH, xl=XL, skip=False):
                for tb in range(TB):
                    for k in range(kt):
                        ts = slice(tb * P, (tb + 1) * P)
                        last = three(outs(tb), xh[:, k0 + k, ts], xl[:, k0 + k, ts], HI[:, s, k * n:(k + 1) * n],
                                     LO[:, s, k * n:(k + 1) * n], start and k == 0, stop and k == kt - 1, skip)
                return last

            def clear_acc():
                for q in range(4):
                    mm(accf[:, q * 512:(q + 1) * 512], zero_bf[:, 0:P], zero_bf[:, :], start=True, stop=False,
                       skip_group_check=True)

            def down(s, tiles, last_group, kt=2):
                for tb in range(TB):
                    ts = slice(tb * P, (tb + 1) * P)
                    for kk in range(kt):
                        xh, xl = tiles(kk)
                        stop = last_group and kk == kt - 1
                        for lhs, w, end in ((xh, HI, False), (xh, LO, False), (xl, HI, stop)):
                            for n in range(2):
                                c = kk * 1024 + n * 512
                                last = mm(acc[:, tb, n * 512:(n + 1) * 512], lhs[:, ts], w[:, s, c:c + 512],
                                          start=False, stop=end, skip_group_check=True)
                return last

            def norm_transpose(n):
                pe.wait_ge(S("y_ready"), n + 1)
                for b in range(4):
                    for kk in range(2):
                        for tb in range(TB):
                            k = 2 * b + kk
                            last = nc.tensor.transpose(wk[:, b, kk * SEQ + tb * P:kk * SEQ + (tb + 1) * P],
                                                       y[:, tb, k * P:(k + 1) * P], ident)
                    last.then_inc(S("xT_psum"), 1)

            def xT_wait(n):
                pe.wait_ge(S("xT_lo"), 4 * n + 4)

            pe.wait_ge(S("params_in"), 16 * N_PARAM)
            pe.wait_ge(S("consts_in"), 16)
            for r, n in enumerate(ROWS[:4]):
                nc.tensor.transpose(wk[:, 0, r * P:r * P + n], rows[0:n, r, :], ident[0:n, 0:n])
            nc.tensor.transpose(wk[:, 1, 0:ROWS[4]], rows[0:ROWS[4], 4, :], ident[0:ROWS[4], 0:ROWS[4]])
            mm(wk[:, 1, P:P + 32], cst[0:2, C_SEL:C_SEL + P], pair[0:2, :], start=True, stop=True)\
                .then_inc(S("cols_psum"), 1)
            pe.wait_ge(S("cpad_ready"), 1)
            for r in range(2):
                for q in range(4):
                    last = nc.tensor.transpose(wk[:, 2 + r, q * P:(q + 1) * P], cpad[:, r, q, :], ident)
            last.then_inc(S("ct_psum"), 1)
            pe.wait_ge(S("cols_ready"), 1)
            pe.wait_ge(S("ct_ready"), 1)
            norm_transpose(0)
            xT_wait(0)
            for b in range(2):
                s = arrived()
                last = ch_major(s, b)
                used(last)
            pe.wait_ge(S("bpad_ready"), 1)
            for r in range(2):
                for q in range(4):
                    last = nc.tensor.transpose(wk[:, 2 + r, q * P:(q + 1) * P],
                                               bpad[:, r, 4 * q:4 * q + 4, :].rearrange("p a b -> p (a b)"), ident)
            last.then_inc(S("bt_psum"), 1)
            pe.wait_ge(S("bt_ready"), 1)
            pe.wait_ge(S("u_ready"), 2)

            def drive(i):
                q, j = i // 4, i % 4
                js = slice(32 * j, 32 * j + 32)
                if i >= 4:
                    pe.wait_ge(S("bu_read"), i - 3)
                for r in range(2):
                    last = mm(wk[:, i % 4, r * SEQ:(r + 1) * SEQ], bt5[js, r, q, :], uT[js, q, :],
                              start=True, stop=True)
                last.then_inc(S("bu_psum"), 1)

            for i in range(4):
                drive(i)
            for i in range(ST):
                q, j = i // 4, i % 4
                js = slice(32 * j, 32 * j + 32)
                pe.wait_ge(S("xr5_ready"), i + 1)
                pe.wait_ge(S("xi5_ready"), i + 1)
                for r in range(2):
                    last = mm(accf[js, q * 512:q * 512 + SEQ], ct5[:, r, q, js], xs5[:, i % 2, r, :],
                              start=(r == 0), stop=(r == 1))
                last.then_inc(S("x5_used"), 1)
                if i + 4 < ST:
                    drive(i + 4)
            pe.wait_ge(S("z_lo"), 4)
            s = arrived()
            for b in range(2):
                for j in range(2):
                    for k in range(4):
                        w = k * 512 + (2 * b + j) * P
                        last = three(wk[:, b, j * SEQ:(j + 1) * SEQ], HI[:, s, w:w + P], LO[:, s, w:w + P],
                                     XH[:, k, :], XL[:, k, :], k == 0, k == 3)
                if b == 0:
                    last.then_inc(S("glu_psum"), 1)
            used(last)
            pe.wait_ge(S("z2_lo"), 2)
            clear_acc()
            for p in range(2):
                s = arrived()
                used(down(s, lambda kk: (XH[:, 4 + 2 * p + kk, :], XL[:, 4 + 2 * p + kk, :]), p == 1))

            def mlp(layer):
                norm_transpose(1 + 2 * layer)
                xT_wait(1 + 2 * layer)
                base = layer * MC

                def mlp_up(c, par):
                    if not (isinstance(c, int) and c + base < 2):
                        pe.wait_ge(S("hid_read"), c + base - 1)
                    s = arrived()
                    used(ch_major(s, par))

                def mlp_down(c, par, end=False):
                    pe.wait_ge(S("hid_lo"), c + base + 1)
                    s = arrived()
                    used(down(s, lambda kk: (HH[:, par, kk, :], HL[:, par, kk, :]), end))

                mlp_up(0, 0)
                clear_acc()
                with pe.Fori(0, (MC - 2) // 2) as i:
                    ring.enter(i, 1)
                    mlp_up(i * 2 + 1, 1)
                    mlp_down(i * 2, 0)
                    mlp_up(i * 2 + 2, 0)
                    mlp_down(i * 2 + 1, 1)
                ring.leave((MC - 2) // 2)
                mlp_up(MC - 1, 1)
                mlp_down(MC - 2, 0)
                mlp_down(MC - 1, 1, True)

            mlp(0)

            norm_transpose(2)
            xT_wait(2)
            for c in range(4):
                if c >= 2:
                    pe.wait_ge(S("pj_read"), c - 1)
                for half in range(2):
                    s = arrived()
                    last = tok_major(s, lambda tb: wk[:, 2 * (c % 2) + tb, :], 4 * half, 4, 512, half == 0, half == 1)
                    used(last)
            pe.wait_ge(S("pj_read"), 3)
            s = arrived()
            used(tok_major(s, lambda tb: wk[:, tb, 0:ATT_TAIL], 0, KD, ATT_TAIL, True, True))
            for tb in range(TB):
                pe.wait_ge(S("rope_ready"), tb + 1)
                for job in range(5):
                    n = 5 * tb + job
                    if n >= 4:
                        pe.wait_ge(S("qkT_read"), n - 3)
                    else:
                        pe.wait_ge(S("pj_read"), 5)
                    for b in range(1 if job == 4 else 4):
                        c = (job * 4 + b) * P
                        last = nc.tensor.transpose(wk[:, n % 4, b * P:(b + 1) * P], roped[:, tb, c:c + P], ident)
                    last.then_inc(S("qkT_psum"), 1)
            pe.wait_ge(S("qkT_read"), 10)

            for job, (tb, h0, nh) in enumerate(IJOBS):
                if job >= 4:
                    pe.wait_ge(S("rel_read"), job - 3)
                K = P * (tb + 1)
                for b in range(nh):
                    hd = h0 + 2 * b
                    hs = slice(64 * (hd % 2), 64 * (hd % 2) + 64)
                    last = mm(wk[:, job % 4, b * K:(b + 1) * K], qiT[hs, hd // 2, tb * P:(tb + 1) * P],
                              kiT[hs, 0:K], start=True, stop=True)
                last.then_inc(S("rel_psum"), 1)

            def scores1(n):
                tb, h0, nh = JOBS1[n]
                K = P * (tb + 1)
                if n >= 4:
                    pe.wait_ge(S("s1_read"), n - 3)
                else:
                    pe.wait_ge(S("rel_read"), 6)
                for b in range(nh):
                    hd = h0 + 2 * b
                    hs = slice(64 * (hd % 2), 64 * (hd % 2) + 64)
                    last = mm(wk[:, n % 4, b * K:(b + 1) * K], qT1[hs, hd // 2, tb * P:(tb + 1) * P],
                              kT1[hs, hd // 4, 0:K], start=True, stop=True)
                last.then_inc(S("s1_psum"), 1)

            def weighted1(n):
                tb, h0, nh = JOBS1[n]
                pe.wait_ge(S("p1_ready"), n + 1)
                if n >= 2:
                    pe.wait_ge(S("pT1_ready"), n - 1)
                for b in range(4):
                    last = nc.tensor.transpose(accf[:, (n % 2) * 512 + b * P:(n % 2) * 512 + (b + 1) * P],
                                               p1[:, n % 3, b * P:(b + 1) * P], ident)
                last.then_inc(S("pT1_psum"), 1)
                pe.wait_ge(S("pT1_ready"), n + 1)
                if n >= 2:
                    pe.wait_ge(S("o1_lo"), n - 1)
                for b in range(nh):
                    hd = h0 + 2 * b
                    o = 1024 + (n % 2) * 512 + b * P
                    for kb in range(tb + 1):
                        last = mm(accf[64 * (hd % 2):64 * (hd % 2) + 64, o:o + P],
                                  pj[:, kb, VOFF + (hd // 4) * 64:VOFF + (hd // 4) * 64 + 64],
                                  pT1[:, n % 2, (b * (tb + 1) + kb) * P:(b * (tb + 1) + kb + 1) * P],
                                  start=(kb == 0), stop=(kb == tb))
                last.then_inc(S("o1_psum"), 1)

            scores1(0)
            scores1(1)
            for n in range(len(JOBS1)):
                if n + 2 < len(JOBS1):
                    scores1(n + 2)
                weighted1(n)
            pe.wait_ge(S("o1_lo"), len(JOBS1))
            clear_acc()
            for p in range(4):
                s = arrived()
                used(down(s, lambda kk: (XH[:, 2 * p + kk, :], XL[:, 2 * p + kk, :]), p == 3))

            mlp(1)

            norm_transpose(4)
            xT_wait(4)
            s = arrived()
            used(tok_major(s, lambda tb: wk[:, tb, 0:SH], 0, KD, SH, True, True))

            def qk_transpose(which):
                for tb in range(TB):
                    for t in range(3):
                        n = which * 6 + tb * 3 + t
                        if n == 0 or n == 6:
                            pe.wait_ge(S("qk2_ready"), which + 1)
                        if n >= 2:
                            pe.wait_ge(S("qkT2_read"), n - 1)
                        for b in range(4):
                            c = (t * 4 + b) * P
                            last = nc.tensor.transpose(accf[:, (n % 2) * 512 + b * P:(n % 2) * 512 + (b + 1) * P],
                                                       qk2[:, tb, c:c + P], ident)
                        last.then_inc(S("qkT2_psum"), 1)

            for c in range(9):
                if c == 0:
                    pe.wait_ge(S("dt_read"), 1)
                elif c >= 2:
                    pe.wait_ge(S("qkv2_read"), c - 1)
                for half in range(2):
                    s = arrived()
                    last = tok_major(s, lambda tb: wk[:, 2 * (c % 2) + tb, :], 4 * half, 4, 512, half == 0, half == 1)
                    used(last)
                if c == 5:
                    qk_transpose(0)
            pe.wait_ge(S("a_ready"), 1)
            UU, GT = cst[:, C_UU:C_UU + P], cst[:, C_GT:C_GT + P]
            for n, (lhs, b) in enumerate(((UU, 0), (UU, 1), (GT, 0))):
                last = mm(accf[:, 1024 + n * 32:1024 + (n + 1) * 32], lhs, a_tok[:, b, :], start=True, stop=True)
            last.then_inc(S("cs_psum"), 1)
            qk_transpose(1)
            pe.wait_ge(S("qkT2_read"), 12)
            pe.wait_ge(S("qkv2_read"), 9)

            def scores2(n):
                hd, tb = JOBS2[n]
                K = P * (tb + 1)
                if n >= 2:
                    pe.wait_ge(S("s2_read"), n - 1)
                hs = slice(64 * (hd % 2), 64 * (hd % 2) + 64)
                for gi in range(3):
                    o = (n % 2) * 1024 + gi * K
                    last = mm(wkf[:, o:o + K], qT2[hs, gi * 4 + hd // 2, tb * P:(tb + 1) * P],
                              kT2[hs, gi * 4 + hd // 2, 0:K], start=True, stop=True)
                last.then_inc(S("s2_psum"), 1)

            def weighted2(n):
                hd, tb = JOBS2[n]
                nb = 3 * (tb + 1)
                pe.wait_ge(S("p2_ready"), n + 1)
                if n >= 1:
                    pe.wait_ge(S("pT2_ready"), n)
                for b in range(nb):
                    last = nc.tensor.transpose(accf[:, b * P:(b + 1) * P], p2[:, n % 2, b * P:(b + 1) * P], ident)
                last.then_inc(S("pT2_psum"), 1)
                pe.wait_ge(S("pT2_ready"), n + 1)
                if n >= 2 and n % 2 == 0:
                    pe.wait_ge(S("o2_lo"), n // 2)
                elif n == 0:
                    pe.wait_ge(S("cs_read"), 1)
                for b in range(nb):
                    gi, kb = b // (tb + 1), b % (tb + 1)
                    c = gi * 512 + hd * 64
                    last = mm(accf[64 * (hd % 2):64 * (hd % 2) + 64, 1024:1024 + P], v2[:, kb, c:c + 64],
                              pT2[:, n % 2, b * P:(b + 1) * P], start=(b == 0), stop=(b == nb - 1))
                if n % 2:
                    last.then_inc(S("o2_psum"), 1)

            def gate_piece(c):
                if c >= 1:
                    pe.wait_ge(S("gate_read"), c)
                s = arrived()
                used(tok_major(s, lambda tb: accf[:, 1536 + tb * 256:1536 + (tb + 1) * 256], 0, KD, 256, True, True))

            scores2(0)
            for n in range(16):
                if n + 1 < 16:
                    scores2(n + 1)
                if n % 2 == 0:
                    gate_piece(n // 2)
                weighted2(n)
            pe.wait_ge(S("o2_lo"), 8)
            pe.wait_ge(S("gate_read"), 8)
            clear_acc()
            for p in range(2):
                s = arrived()
                used(down(s, lambda kk: (OH[:, 2 * p + kk, :], OL[:, 2 * p + kk, :]), p == 1))
            pe.wait_ge(S("merged_attn"), 1)
            clear_acc()

            def ssd_step(g, par, proj, ssd, fin, first=False):
                gpv = gp[:, 1 - par, :]

                def decay_rows(m):
                    b = m % 2
                    if m >= 2:
                        pe.wait_ge(S("L_read"), g * 4 - 4 + m - 1)
                    elif not first:
                        if m == 0:
                            pe.wait_ge(S("bc_read"), g)
                        elif not (isinstance(g, int) and g < 2):
                            pe.wait_ge(S("y_read"), g - 1)
                    a0 = gpv[:, G_A + m:G_A + m + 1].to_broadcast([P, P])
                    a1 = gpv[:, G_A + 4 + m:G_A + 5 + m].to_broadcast([P, P])
                    mm(wk[:, b, 0:P], id_bf[:, :], neg_bf[:, :], start=True, stop=False, skip_group_check=True)
                    mm(wk[:, b, 2 * P:3 * P], id_bf[:, :], neg_bf[:, :], start=False, stop=False, skip_group_check=True)
                    mm(wk[:, b, 0:P], a0, cst[:, C_UU:C_UU + P], start=False, stop=False, skip_group_check=True)
                    mm(wk[:, b, P:3 * P], a1, cst[:, C_UU:C_UU + 2 * P], start=False, stop=True,
                       skip_group_check=True).then_inc(S("L_psum"), 1)

                if ssd:
                    pe.wait_ge(S("gp_ready"), g)
                    decay_rows(0)
                    decay_rows(1)
                if proj:
                    if not first:
                        pe.wait_ge(S("xs_read"), g)
                    s = arrived()
                    used(ch_major(s, 2))
                if fin:
                    pe.wait_ge(S("sq_ready"), g - 1)
                    pe.wait_ge(S("CB_read"), g - 1)
                    for j in range(2):
                        last = mm(wk[:, 3, 0:SEQ], ones[:, :], sq2[:, j, :], start=(j == 0), stop=(j == 1))
                    last.then_inc(S("gn_psum"), 1)
                if ssd:
                    pe.wait_ge(S("xsc_ready"), g)
                    if fin:
                        pe.wait_ge(S("gn_read"), g - 1)
                    for j in range(2):
                        for tb in range(TB):
                            o = tb * 256 + j * P
                            last = nc.tensor.transpose(wk[:, 3, o:o + P], xsc[:, 1 - par, j, tb * P:(tb + 1) * P], ident)
                    last.then_inc(S("X_psum"), 1)
                    decay_rows(2)
                    decay_rows(3)
                if proj:
                    pe.wait_ge(S("z_read"), g + 1)
                    s = arrived()
                    used(ch_major(s, 2))
                if fin:
                    pe.wait_ge(S("Y_lo"), g - 1)
                    s = arrived()
                    end = isinstance(g, int) and g == 9
                    used(down(s, lambda kk: (HH[:, par, kk, :], HL[:, par, kk, :]), end))
                if ssd:
                    pe.wait_ge(S("X_read"), g)
                    pe.wait_ge(S("bcc_ready"), g)
                    bc = bcc[:, 1 - par, :, :]
                    mm(wk[:, 3, 0:SEQ], bc[:, 0, 0:P], bc[:, 1, :], start=True, stop=True)
                    mm(wk[:, 3, SEQ:SEQ + P], bc[:, 0, P:SEQ], bc[:, 1, P:SEQ], start=True, stop=True)\
                        .then_inc(S("CB_psum"), 1)
                if proj:
                    if ssd:
                        pe.wait_ge(S("L_read"), g * 4 - 1)
                    s = arrived()
                    used(ch_major(s, 0, True))
                if ssd:
                    for m in range(4):
                        pe.wait_ge(S("M_ready"), g * 4 - 4 + m + 1)
                        if m == 0:
                            pe.wait_ge(S("L_read"), g * 4)
                        ps = slice(64 * (m % 2), 64 * (m % 2) + 64)
                        o = (m // 2) * SEQ
                        mm(wk[ps, 1, o:o + SEQ], Xt[:, 0, m * 64:(m + 1) * 64], Lm[:, m, 0:SEQ],
                           start=True, stop=False, skip_group_check=True)
                        last = mm(wk[ps, 1, o + P:o + SEQ], Xt[:, 1, m * 64:(m + 1) * 64], Lm[:, m, SEQ:SEQ + P],
                                  start=False, stop=True, skip_group_check=True)
                    last.then_inc(S("y_psum"), 1)

            ssd_step(0, 0, True, False, False, first=True)
            ssd_step(1, 1, True, True, False)
            with pe.Fori(0, 3) as i:
                ring.enter(i, 2)
                ssd_step(i * 2 + 2, 0, True, True, True)
                ssd_step(i * 2 + 3, 1, True, True, True)
            ring.leave(3)
            ssd_step(8, 0, False, True, True)
            ssd_step(9, 1, False, False, True)
            pe.wait_ge(S("merged"), 1)
            for b in range(4):
                for kk in range(2):
                    for tb in range(TB):
                        k = 2 * b + kk
                        last = nc.tensor.transpose(wk[:, b, kk * SEQ + tb * P:kk * SEQ + (tb + 1) * P],
                                                   y[:, tb, k * P:(k + 1) * P], ident)
                last.then_inc(S("mT_psum"), 1)
            clear_acc()
            pe.wait_ge(S("mT_lo"), 4)
            for p in range(4):
                s = arrived()
                used(down(s, lambda kk: (XH[:, 2 * p + kk, :], XL[:, 2 * p + kk, :]), p == 3))

            norm_transpose(5)
            xT_wait(5)

            def ffn_up(c, par):
                if not (isinstance(c, int) and c < 2):
                    pe.wait_ge(S("gv_read"), c - 1)
                s = arrived()
                used(ch_major(s, par, True))

            def ffn_down(c, par, end=False):
                pe.wait_ge(S("f_lo"), c + 1)
                s = arrived()
                used(down(s, lambda kk: (HH[:, par, kk, :], HL[:, par, kk, :]), end, kt=1))

            ffn_up(0, 0)
            clear_acc()
            with pe.Fori(0, (FC - 2) // 2) as i:
                ring.enter(i, 1)
                ffn_up(i * 2 + 1, 1)
                ffn_down(i * 2, 0)
                ffn_up(i * 2 + 2, 0)
                ffn_down(i * 2 + 1, 1)
            ring.leave((FC - 2) // 2)
            ffn_up(FC - 1, 1)
            ffn_down(FC - 2, 0)
            ffn_down(FC - 1, 1, True)

        @block.scalar
        def _(act):
            ring = Ring()
            steps = Steps(act, S("act_step"))
            A = nc.scalar.activation

            nc.scalar.dma_start(h[:, :, :], ins["x"][0].rearrange("(b p) n -> p b n", p=P)).then_inc(S("x_in"), 16)
            nc.scalar.dma_start(cst[:, :], ins["consts"]).then_inc(S("consts_in"), 16)
            with nc.allow_non_contiguous_dma(reason="two vectors of 32"):
                for dst, src in param_loads(ins, rows, pair, braw, craw, alog, dtb):
                    nc.scalar.dma_start(dst, src).then_inc(S("params_in"), 16)
            for j in range(2):
                nc.scalar.dma_start(gbc[:, j, :], ins["norm_g"][0, 2 * j + 1].partition_broadcast(P))\
                    .then_inc(S(f"gbc_in{j}"), 16)

            def hi_next():
                small_n = size(ring.n)
                s, k, n = ring.next()
                act.wait_ge(S(f"loaded{s}"), k * 32 + 32)
                if not isinstance(n, int) or n >= 4:
                    act.wait_ge(S("piece_done"), n - 3)
                A(HI[:, s, 0:small_n], raw[:, s % 2, 0:small_n], ACT.Copy).then_inc(S(f"hi_ready{s}"), 1)

            def hi_to(n):
                while ring.n <= n:
                    hi_next()

            def done(n):
                act.wait_ge(S("piece_done"), n + 1)

            def squares(src, count):
                for tb in range(TB):
                    last = A(y[:, tb, :], src[:, tb, :], ACT.Square, accum_out=ssq[:, tb:tb + 1])
                last.then_inc(S("ssq_ready"), 1)

            def xT_high(n, gains):
                for b in range(4):
                    act.wait_ge(S("xT_psum"), 4 * n + b + 1)
                    for kk in range(2):
                        last = A(XH[:, 2 * b + kk, :], wk[:, b, kk * SEQ:(kk + 1) * SEQ], ACT.Copy,
                                 scale=gains(2 * b + kk))
                    last.then_inc(S("xT_hi"), 1)

            act.wait_ge(S("x_in"), 16)
            squares(h, 0)
            act.wait_ge(S("cols_psum"), 1)
            for r, n in enumerate(ROWS[:4]):
                A(cols[:, r, 0:n], wk[:, 0, r * P:r * P + n], ACT.Copy)
            A(cols[:, 4, 0:ROWS[4]], wk[:, 1, 0:ROWS[4]], ACT.Copy)
            A(pairb[:, :], wk[:, 1, P:P + 32], ACT.Copy).then_inc(S("cols_ready"), 1)
            act.wait_ge(S("cols_ready"), 1)
            act.wait_ge(S("params_in"), 16 * N_PARAM)
            A(sm5[:, 0, :], pairb[:, 0:16], ACT.Exp).then_inc(S("dt5_ready"), 1)
            A(alog[:, :], alog[:, :], ACT.Exp).then_inc(S("alog_ready"), 1)
            act.wait_ge(S("ldt5_ready"), 1)
            A(sm5[:, 1, :], sm5[:, 1, :], ACT.Exp).then_inc(S("mag5_ready"), 1)
            act.wait_ge(S("ang5_ready"), 1)
            A(sm5[:, 4, :], sm5[:, 9, :], ACT.Sin)
            A(sm5[:, 5, :], sm5[:, 6, :], ACT.Sin).then_inc(S("sin5_ready"), 1)
            act.wait_ge(S("ct_psum"), 1)
            for r in range(2):
                last = A(ct5[:, r, :, :], wk[:, 2 + r, :].rearrange("p (q n) -> p q n", q=4), ACT.Copy)
            last.then_inc(S("ct_ready"), 1)
            xT_high(0, lambda k: gain(0, 0, k))
            hi_to(3)
            for b in range(2):
                done(b)
                A(uT[:, 2 * b:2 * b + 2, :], wk[:, b, :].rearrange("p (j t) -> p j t", j=2), ACT.Copy)\
                    .then_inc(S("u_ready"), 1)
            act.wait_ge(S("bt_psum"), 1)
            for r in range(2):
                last = A(bt5[:, r, :, :], wk[:, 2 + r, :].rearrange("p (q n) -> p q n", q=4), ACT.Copy)
            last.then_inc(S("bt_ready"), 1)
            hi_to(5)
            for q in range(4):
                act.wait_ge(S("yv_ready"), q + 1)
                steps.link(A(zf[:, q, :], yv[:, q, :], ACT.Gelu_apprx_tanh))
                A(XH[:, q, :], zf[:, q, :], ACT.Copy).then_inc(S("z_hi"), 1)
            act.wait_ge(S("glu_psum"), 1)
            for b in range(2):
                if b == 1:
                    done(2)
                A(gt5[:, 2 * b:2 * b + 2, :], wk[:, b, :].rearrange("p (j t) -> p j t", j=2), ACT.Tanh, scale=0.5)\
                    .then_inc(S("gt5_ready"), 1)
            for b in range(2):
                act.wait_ge(S("z2_ready"), b + 1)
                A(XH[:, 4 + 2 * b:6 + 2 * b, :], z2f[:, 2 * b:2 * b + 2, :], ACT.Copy, scale=0.5)\
                    .then_inc(S("z2_hi"), 1)
            hi_to(6)

            def post(last_piece):
                done(last_piece)
                squares(acc, 0)

            post(4)
            hi_to(8)

            def mlp(layer, first):
                act.wait_ge(S("h_ready"), 1 + 2 * layer)
                nxt = 2 * layer
                squares(h, 0)
                xT_high(1 + 2 * layer, lambda k: gain(layer, 2, k))
                base = layer * MC

                def hidden(c, par, piece):
                    done(piece)
                    if not (isinstance(c, int) and c + base < 2):
                        act.wait_ge(S("hid_lo"), c + base - 1)
                    A(relu_b[:, par, :], wk[:, par, :], ACT.Relu).then_inc(S("hid_read"), 1)
                    act.wait_ge(S("hid_read"), c + base + 1)
                    A(HH[:, par, :, :], relu_b[:, par, :].rearrange("p (j t) -> p j t", j=2), ACT.Square)\
                        .then_inc(S("hid_hi"), 1)

                hi_to(first + 3)
                hidden(0, 0, first)
                with act.Fori(0, (MC - 2) // 2) as i:
                    ring.enter(i, 1)
                    hi_next()
                    hidden(i * 2 + 1, 1, i * 4 + (first + 1))
                    hi_next()
                    hi_next()
                    hidden(i * 2 + 2, 0, i * 4 + (first + 3))
                    hi_next()
                ring.leave((MC - 2) // 2)
                hi_to(first + 2 * MC)
                hidden(MC - 1, 1, first + 2 * MC - 3)
                hi_to(first + 2 * MC + 2)
                post(first + 2 * MC - 1)
                hi_to(first + 2 * MC + 3)

            mlp(0, 5)

            act.wait_ge(S("h_ready"), 2)
            for j in range(2):
                nc.scalar.dma_start(gbc[:, j, :], ins["norm_g"][1, 2 * j + 1].partition_broadcast(P))\
                    .then_inc(S(f"gbc_in{2 + j}"), 16)
            squares(h, 0)
            xT_high(2, lambda k: gain(1, 0, k))
            for c in range(5):
                n = min(P_ATT + 2 * c + 1, P_ATT + 8)
                hi_to(n + 3)
                done(n)
                w = 512 if c < 4 else ATT_TAIL
                for tb in range(TB):
                    b = 2 * (c % 2) + tb
                    last = A(pj[:, tb, c * 512:c * 512 + w], wk[:, b, 0:w], ACT.Copy)
                last.then_inc(S("pj_read"), 1)
            hi_to(P_ATT + 12)
            for n in range(10):
                tb, job = n // 5, n % 5
                act.wait_ge(S("qkT_psum"), n + 1)
                dst = [qT1[:, 0:4], qT1[:, 4:8], kT1, qiT, None][job]
                ts = slice(tb * P, (tb + 1) * P)
                if job == 4:
                    last = A(kiT[:, ts], wk[:, n % 4, 0:P], ACT.Copy)
                else:
                    last = A(dst[:, :, ts], wk[:, n % 4, :].rearrange("p (b t) -> p b t", b=4), ACT.Copy)
                last.then_inc(S("qkT_read"), 1)
            for job in range(6):
                act.wait_ge(S("rel_psum"), job + 1)
                if job >= 2:
                    act.wait_ge(S("rel_used"), job - 1)
                A(rel[:, job % 2, :], wk[:, job % 4, :], ACT.Relu).then_inc(S("rel_read"), 1)

            def exps1(n):
                tb, h0, nh = JOBS1[n]
                K = P * (tb + 1)
                act.wait_ge(S("m1_ready"), n + 1)
                for b in range(nh):
                    s = p1[:, n % 3, b * K:(b + 1) * K]
                    last = A(s, s, ACT.Exp, bias=small[:, n % 2, 1, b:b + 1], scale=HD ** -0.5,
                             accum_out=small[:, n % 2, 2, b:b + 1])
                last.then_inc(S("e1_ready"), 1)

            def copies1(n):
                tb, h0, nh = JOBS1[n]
                act.wait_ge(S("pT1_psum"), n + 1)
                if n >= 2:
                    act.wait_ge(S("o1_psum"), n - 1)
                A(pT1[:, n % 2, :], accf[:, (n % 2) * 512:(n % 2 + 1) * 512], ACT.Copy).then_inc(S("pT1_ready"), 1)
                act.wait_ge(S("o1_psum"), n + 1)
                o = 1024 + (n % 2) * 512
                hs = slice(64 * (h0 % 2), 64 * (h0 % 2) + 64)
                A(XH[hs, h0 // 2:h0 // 2 + nh, tb * P:(tb + 1) * P],
                  accf[hs, o:o + nh * P].rearrange("p (a t) -> p a t", t=P), ACT.Copy).then_inc(S("o1_hi"), 1)

            exps1(0)
            for n in range(len(JOBS1)):
                if n + 1 < len(JOBS1):
                    exps1(n + 1)
                copies1(n)
            hi_to(P_ATT + 15)
            post(P_ATT + 12)
            hi_to(P_ATT + 16)
            mlp(1, P_ATT + 13)

            act.wait_ge(S("h_ready"), 4)
            squares(h, 0)
            xT_high(4, lambda k: pcol(0, R_N1 + k))

            def qk_evac(which):
                gcol = pcol(2, R_QG if which == 0 else R_KG)
                dst = qT2 if which == 0 else kT2
                for n in range(6 * which, 6 * which + 6):
                    tb, t = (n % 6) // 3, n % 3
                    act.wait_ge(S("qkT2_psum"), n + 1)
                    A(dst[:, 4 * t:4 * t + 4, tb * P:(tb + 1) * P],
                      accf[:, (n % 2) * 512:(n % 2 + 1) * 512].rearrange("p (b t) -> p b t", b=4), ACT.Copy,
                      scale=gcol).then_inc(S("qkT2_read"), 1)

            hi_to(P_B2 + 3)
            act.wait_ge(S("sp_arg"), 1)
            A(sp2[:, :, :], sp2[:, :, :], ACT.Exp).then_inc(S("sp_exp"), 1)
            for c in range(9):
                n = P_B2 + 1 + 2 * c + 1
                hi_to(n + 3)
                done(n)
                dst = v2 if 3 <= c < 6 else qk2
                if c == 6:
                    act.wait_ge(S("qkT2_psum"), 6)
                for tb in range(TB):
                    last = A(dst[:, tb, (c % 3) * 512:(c % 3 + 1) * 512], wk[:, 2 * (c % 2) + tb, :], ACT.Copy)
                last.then_inc(S("qkv2_read"), 1)
                if c == 5:
                    qk_evac(0)
            act.wait_ge(S("cs_psum"), 1)
            for n in range(3):
                last = A(gpall[:, :, G_NB + 4 * n:G_NB + 4 * n + 4],
                         accf[:, 1024 + n * 32:1024 + (n + 1) * 32].rearrange("p (g m) -> p g m", g=SG),
                         ACT.Copy, scale=(-1.0 if n < 2 else 1.0))
            last.then_inc(S("cs_read"), 1)
            hi_to(P_B2 + 22)
            qk_evac(1)

            def exps2(n):
                hd, tb = JOBS2[n]
                act.wait_ge(S("m2_ready"), n + 1)
                s = p2[:, n % 2, 0:3 * P * (tb + 1)]
                A(s, s, ACT.Exp, bias=small[:, n % 2, 1, 0:1], scale=HD ** -0.5,
                  accum_out=small[:, n % 2, 2, 0:1]).then_inc(S("e2_ready"), 1)

            def copies2(n):
                hd, tb = JOBS2[n]
                w = 3 * P * (tb + 1)
                act.wait_ge(S("pT2_psum"), n + 1)
                A(pT2[:, n % 2, 0:w], accf[:, 0:w], ACT.Copy).then_inc(S("pT2_ready"), 1)
                if n % 2:
                    act.wait_ge(S("o2_psum"), n // 2 + 1)
                    A(OH[:, hd // 2, tb * P:(tb + 1) * P], accf[:, 1024:1024 + P], ACT.Copy).then_inc(S("o2_hi"), 1)

            def gate_evac(c):
                done(P_B2 + 19 + c)
                dst = g_ssd if c < 4 else y
                A(dst[:, :, (c % 4) * 256:(c % 4 + 1) * 256],
                  accf[:, 1536:2048].rearrange("p (b n) -> p b n", b=TB), ACT.Tanh, scale=0.5)\
                    .then_inc(S("gate_read"), 1)

            exps2(0)
            for n in range(16):
                if n + 1 < 16:
                    exps2(n + 1)
                if n % 2 == 0:
                    hi_to(P_B2 + 19 + n // 2 + 3)
                    gate_evac(n // 2)
                copies2(n)
            hi_to(P_SSD + 1)
            act.wait_ge(S("merged_attn"), 1)
            hi_to(P_SSD + 2)

            def ssd_step(g, par, piece, proj, ssd, fin, splits, first=False):
                gpv = gp[:, 1 - par, :]

                def decays(m):
                    act.wait_ge(S("L_psum"), g * 4 - 4 + m + 1)
                    if not (isinstance(g, int) and g < 2):
                        act.wait_ge(S("y_psum"), g - 1)
                    for blk, c in ((0, 0), (1, 8), (2, 4)):
                        last = A(Lm[:, m, blk * P:(blk + 1) * P], wk[:, m % 2, blk * P:(blk + 1) * P], ACT.Exp,
                                 bias=gpv[:, G_NB + c + m:G_NB + c + m + 1])
                    last.then_inc(S("L_read"), 1)

                if splits != 3:
                    hi_next()
                if ssd:
                    act.wait_ge(S("gp_ready"), g)
                    decays(0)
                    decays(1)
                if proj:
                    done(piece)
                    if not (isinstance(g, int) and g < 2):
                        act.wait_ge(S("yz_ready"), g - 1)
                    A(zc[:, par, :, :], wk[:, 2, :].rearrange("p (j t) -> p j t", j=2), ACT.Copy, scale=0.5)\
                        .then_inc(S("z_read"), 1)
                    act.wait_ge(S("z_read"), g + 1)
                    A(zt[:, par, :, :], zc[:, par, :, :], ACT.Tanh).then_inc(S("zt_ready"), 1)
                if ssd:
                    decays(2)
                    decays(3)
                if splits >= 3:
                    hi_next()
                if fin:
                    act.wait_ge(S("yn_ready"), g - 1)
                    A(HH[:, par, :, :], yn[:, :, :], ACT.Copy).then_inc(S("Y_hi"), 1)
                if proj:
                    done(piece + 1)
                    if not first:
                        act.wait_ge(S("xconv_ready"), g)
                    A(xpad[:, :, 3:3 + SEQ], wk[:, 2, :].rearrange("p (j t) -> p j t", j=2), ACT.Copy)\
                        .then_inc(S("xs_read"), 1)
                if splits >= 3:
                    hi_next()
                if proj:
                    act.wait_ge(S("xconv_ready"), g + 1)
                    if not first:
                        act.wait_ge(S("xsc_ready"), g)
                    A(xtanh[:, :, :], xconv[:, :, :], ACT.Tanh).then_inc(S("xtanh_ready"), 1)
                    done(piece + (3 if fin else 2))
                    if not first:
                        act.wait_ge(S("bconv_ready"), g)
                    A(bcpad[:, :, 3:3 + SEQ], wk[:, 0, :].rearrange("p (j t) -> p j t", j=2), ACT.Copy)\
                        .then_inc(S("bc_read"), 1)
                if splits >= 3:
                    hi_next()
                if proj:
                    act.wait_ge(S("bconv_ready"), g + 1)
                    if not first:
                        act.wait_ge(S("bcc_ready"), g)
                    A(btanh[:, :, :], bconv[:, :, :], ACT.Tanh).then_inc(S("btanh_ready"), 1)
                if ssd:
                    act.wait_ge(S("yz_ready"), g)
                    if fin:
                        act.wait_ge(S("gn_psum"), g - 1)
                    A(sq2[:, :, :], yz[:, 1 - par, :, :], ACT.Square).then_inc(S("sq_ready"), 1)

            ssd_step(0, 0, P_SSD, True, False, False, 3, first=True)
            ssd_step(1, 1, P_SSD + 3, True, True, False, 3)
            with act.Fori(0, 3) as i:
                ring.enter(i, 2)
                ssd_step(i * 2 + 2, 0, i * 8 + (P_SSD + 6), True, True, True, 4)
                ssd_step(i * 2 + 3, 1, i * 8 + (P_SSD + 10), True, True, True, 4)
            ring.leave(3)
            ssd_step(8, 0, P_SSD + 30, False, True, True, 1)
            ssd_step(9, 1, P_SSD + 31, False, False, True, 1)
            hi_to(P_WOUT2 + 2)
            for b in range(4):
                act.wait_ge(S("mT_psum"), b + 1)
                A(XH[:, 2 * b:2 * b + 2, :], wk[:, b, :].rearrange("p (k t) -> p k t", k=2), ACT.Copy)\
                    .then_inc(S("mT_hi"), 1)
            first = P_WOUT2 + 4
            hi_to(first + 2)
            act.wait_ge(S("h_ready"), 5)
            hi_to(first + 3)
            squares(h, 0)
            xT_high(5, lambda k: pcol(0, R_N2 + k))

            def ffn(c, par, piece):
                done(piece)
                if not (isinstance(c, int) and c < 2):
                    act.wait_ge(S("fconv_ready"), c - 1)
                A(fpad[:, par, :, 2:2 + SEQ], wk[:, par, :].rearrange("p (j t) -> p j t", j=2), ACT.Copy)\
                    .then_inc(S("gv_read"), 1)
                act.wait_ge(S("fconv_ready"), c + 1)
                if not (isinstance(c, int) and c < 2):
                    act.wait_ge(S("fh_ready"), c - 1)
                A(ftanh[:, par, :], fconv[:, par, 0, :], ACT.Tanh).then_inc(S("ftanh_ready"), 1)

            def ffn_hi(c, par):
                act.wait_ge(S("fh_ready"), c + 1)
                A(HH[:, par, 0, :], fhid[:, par, :], ACT.Copy).then_inc(S("f_hi"), 1)

            ffn(0, 0, first)
            ffn_hi(0, 0)
            with act.Fori(0, (FC - 2) // 2) as i:
                ring.enter(i, 1)
                hi_next()
                ffn(i * 2 + 1, 1, i * 4 + (first + 1))
                ffn_hi(i * 2 + 1, 1)
                hi_next()
                hi_next()
                ffn(i * 2 + 2, 0, i * 4 + (first + 3))
                ffn_hi(i * 2 + 2, 0)
                hi_next()
            ring.leave((FC - 2) // 2)
            hi_to(first + 2 * FC - 1)
            ffn(FC - 1, 1, first + 2 * FC - 3)
            ffn_hi(FC - 1, 1)

        @block.vector
        def _(dve):
            ring = Ring()
            steps = Steps(dve, S("dve_step"))
            link = steps.link
            V = nc.vector
            TT, TS, STT = V.tensor_tensor, V.tensor_scalar, V.scalar_tensor_tensor

            def lo_next():
                low_part(V, ring, 1, size(ring.n))

            def lo_to(n):
                while ring.n <= n:
                    lo_next()

            def done(n):
                dve.wait_ge(S("piece_done"), n + 1)

            def rsqrt(v, t, r):
                link(TS(r.bitcast(I32), v.bitcast(I32), -0.5, 1597463007.0, ALU.mult, ALU.add))
                for _ in range(3):
                    link(STT(t, r, -0.5, r, ALU.mult, ALU.mult))
                    link(TT(t, t, v, ALU.mult))
                    link(STT(r, t, 1.5, r, ALU.add, ALU.mult))

            def row_rstd(count):
                dve.wait_ge(S("ssq_ready"), count)
                link(TS(nv[:, :], ssq[:, :], 1.0 / D, EPS, ALU.mult, ALU.add))
                rsqrt(nv[:, :], nt[:, :], rstd[:, :])

            def pre(count):
                row_rstd(count)
                for tb in range(TB):
                    last = TS(y[:, tb, :], h[:, tb, :], rstd[:, tb:tb + 1], None, ALU.mult)
                last.then_inc(S("y_ready"), 1)

            def xT_low(n, gains):
                for b in range(4):
                    dve.wait_ge(S("xT_hi"), 4 * n + b + 1)
                    for kk in range(2):
                        k = 2 * b + kk
                        last = STT(XL[:, k, :], wk[:, b, kk * SEQ:(kk + 1) * SEQ], gains(k), XH[:, k, :].bitcast(F32),
                                   ALU.mult, ALU.subtract)
                    last.then_inc(S("xT_lo"), 1)

            def post(j, count):
                row_rstd(count)
                dve.wait_ge(S(f"gbc_in{j}"), 16)
                for tb in range(TB):
                    link(STT(y[:, tb, :], acc[:, tb, :], rstd[:, tb:tb + 1], gbc[:, j % 2, :], ALU.mult, ALU.mult))
                    last = TT(h[:, tb, :], h[:, tb, :], y[:, tb, :], ALU.add)
                last.then_inc(S("h_ready"), 1)

            V.memset(zero_bf[:, :], 0.0)
            V.memset(bpad[:, :, :, :], 0.0)
            V.memset(e_tab[:, :, 0, 0:1], 1.0)
            V.memset(e_tab[:, :, 1, 0:1], 0.0)
            dve.wait_ge(S("consts_in"), 16)
            V.tensor_copy(id_bf[:, :], ident)
            link(V.tensor_copy(neg_bf[:, :], cst[:, C_NEGT:C_NEGT + P]))
            dve.wait_ge(S("params_in"), 16 * N_PARAM)
            for r in range(2):
                for par in range(2):
                    last = TS(cpad[:, r, :, 64 * par:64 * par + 64], craw[:, r, :, :],
                              cst[:, C_PAR + 2 * r + par:C_PAR + 2 * r + par + 1], None, ALU.mult)
            last.then_inc(S("cpad_ready"), 1)
            dve.wait_ge(S("x_in"), 16)
            pre(1)
            lr, li = cols[:, 0, R_LR:R_LR + 16], cols[:, 2, R_LI:R_LI + 16]
            v5 = [sm5[:, n, :] for n in range(10)]
            dve.wait_ge(S("dt5_ready"), 1)
            TT(v5[1], lr, v5[0], ALU.mult).then_inc(S("ldt5_ready"), 1)
            link(TT(v5[2], li, v5[0], ALU.mult))
            MAGIC = 12582912.0
            link(TS(v5[3], v5[2], 1.0 / (2 * np.pi), MAGIC, ALU.mult, ALU.add))
            link(TS(v5[3], v5[3], MAGIC, None, ALU.subtract))
            link(STT(v5[9], v5[3], -6.28125, v5[2], ALU.mult, ALU.add))
            link(STT(v5[9], v5[3], -0.0019350051879882812, v5[9], ALU.mult, ALU.add))
            link(STT(v5[9], v5[3], -3.0199160501e-07, v5[9], ALU.mult, ALU.add))
            link(TS(v5[9], v5[9], 3.1415925, -3.1415925, ALU.min, ALU.max))
            link(STT(v5[6], v5[9], -1.0, v5[9], ALU.mult, ALU.max))
            TS(v5[6], v5[6], -1.0, float(np.pi / 2), ALU.mult, ALU.add).then_inc(S("ang5_ready"), 1)
            xT_low(0, lambda k: gain(0, 0, k))
            dve.wait_ge(S("sin5_ready"), 1)
            dve.wait_ge(S("mag5_ready"), 1)
            TT(v5[3], v5[1], v5[5], ALU.mult)
            TT(v5[6], v5[1], v5[4], ALU.mult)
            TT(v5[9], lr, lr, ALU.mult)
            link(TT(v5[0], li, li, ALU.mult))
            TS(v5[3], v5[3], 1.0, None, ALU.subtract)
            link(TT(v5[9], v5[9], v5[0], ALU.add))
            link(V.reciprocal(v5[9], v5[9]))
            TT(v5[7], v5[3], lr, ALU.mult)
            link(TT(v5[0], v5[6], li, ALU.mult))
            link(TT(v5[7], v5[7], v5[0], ALU.add))
            TT(v5[7], v5[7], v5[9], ALU.mult)
            TT(v5[8], v5[6], lr, ALU.mult)
            link(TT(v5[0], v5[3], li, ALU.mult))
            link(TT(v5[8], v5[8], v5[0], ALU.subtract))
            link(TT(v5[8], v5[8], v5[9], ALU.mult))
            lo_to(3)
            fr = v5[7].unsqueeze(2).to_broadcast([P, 16, 16])
            fi = v5[8].unsqueeze(2).to_broadcast([P, 16, 16])
            bt2 = carve(s5 + 1024, 16, 16)
            for r in range(2):
                TT(bq[:, :, :], fr, braw[:, r, :, :], ALU.mult)
                link(TT(bt2[:, :, :], fi, braw[:, 1 - r, :, :], ALU.mult))
                for par in range(2):
                    ps = slice(64 * par, 64 * par + 64)
                    last = TT(bpad[ps, r, :, 16 * par:16 * par + 16], bq[ps, :, :], bt2[ps, :, :],
                              ALU.subtract if r == 0 else ALU.add)
                if r == 0:
                    link(last)
            last.then_inc(S("bpad_ready"), 1)
            dve.wait_ge(S("bpad_ready"), 1)
            V.tensor_copy(e_tab[:, :, 0, 1:2], v5[5].unsqueeze(2))
            link(V.tensor_copy(e_tab[:, :, 1, 1:2], v5[4].unsqueeze(2)))
            L = 1
            while L < SEQ:
                n = min(L, SEQ - 1 - L)
                er, ei = e_tab[:, :, 0, 1:1 + n], e_tab[:, :, 1, 1:1 + n]
                ur = e_tab[:, :, 0, L:L + 1].to_broadcast([P, ST, n])
                ui = e_tab[:, :, 1, L:L + 1].to_broadcast([P, ST, n])
                nr, ni = e_tab[:, :, 0, L + 1:L + 1 + n], e_tab[:, :, 1, L + 1:L + 1 + n]
                tmp = etmp[:, 0:ST * n].rearrange("p (i t) -> p i t", i=ST)
                TT(nr, er, ur, ALU.mult)
                TT(ni, er, ui, ALU.mult)
                link(TT(tmp, ei, ui, ALU.mult))
                link(TT(nr, nr, tmp, ALU.subtract))
                link(TT(tmp, ei, ur, ALU.mult))
                link(TT(ni, ni, tmp, ALU.add))
                L *= 2
            cw = cols[:, 1, :].rearrange("p (k t) -> p k t", k=4)
            for j in range(2):
                TS(gpall[:, :, G_WX + j:G_WX + 8:2], cw[:, :, j:16:2].rearrange("p k g -> p g k"), 0.5, None, ALU.mult)
                TS(gpall[:, :, G_BX + j], cols[:, 2, R_CB + j:R_CB + 16:2], 0.5, None, ALU.mult)
                V.tensor_copy(gpall[:, :, G_NG + j], cols[:, 0, R_SN + j:R_SN + 16:2])
                V.tensor_copy(gpall[:, :, G_D + j], pairb[:, 16 + j:32:2])
            TS(gpall[:, :, G_WB:G_WB + 4], cw[:, :, 16:24].rearrange("p k g -> p g k"), 0.5, None, ALU.mult)
            TS(gpall[:, :, G_WC:G_WC + 4], cw[:, :, 24:32].rearrange("p k g -> p g k"), 0.5, None, ALU.mult)
            TS(gpall[:, :, G_BB], cols[:, 2, R_CB + 16:R_CB + 24], 0.5, None, ALU.mult)
            TS(gpall[:, :, G_BC], cols[:, 2, R_CB + 24:R_CB + 32], 0.5, None, ALU.mult)
            for j, f in enumerate((0.5, 1.0)):
                for k in range(3):
                    blk, at = (3, k * 44) if k < 2 else (4, 0)
                    TS(fpall[:, :, 4 * j + k], cols[:, blk, at + FC * j:at + FC * (j + 1)], f, None, ALU.mult)
                last = TS(fpall[:, :, 4 * j + 3], cols[:, 2, R_FB + FC * j:R_FB + FC * (j + 1)], f, None, ALU.mult)
            link(last)

            def scan_in(i):
                dve.wait_ge(S("bu_psum"), i + 1)
                bu = wk[:, i % 4, :].rearrange("p (r t) -> p r t", r=2)
                TT(rotA[:, :, :], bu, e_tab[:, i, :, :], ALU.mult)
                TT(rotB[:, 0, :], bu[:, 0, :], e_tab[:, i, 1, :], ALU.mult)
                TT(rotB[:, 1, :], bu[:, 1, :], e_tab[:, i, 0, :], ALU.mult).then_inc(S("bu_read"), 1)
                dve.wait_ge(S("bu_read"), i + 1)
                TT(rotA[:, 0, :], rotA[:, 0, :], rotA[:, 1, :], ALU.add)
                link(TT(rotB[:, 0, :], rotB[:, 1, :], rotB[:, 0, :], ALU.subtract))
                if i >= 2:
                    dve.wait_ge(S("xi5_ready"), i - 1)
                mag = v5[1][:, i:i + 1].to_broadcast([P, SEQ])
                V.tensor_tensor_scan(zz[:, i % 2, 0, :], mag, rotA[:, 0, :], 0.0, ALU.mult, ALU.add)
                V.tensor_tensor_scan(zz[:, i % 2, 1, :], mag, rotB[:, 0, :], 0.0, ALU.mult, ALU.add)\
                    .then_inc(S("z5_ready"), 1)
                dve.wait_ge(S("z5_ready"), i + 1)
                link(TT(rotC[:, :, :], zz[:, i % 2, :, :], e_tab[:, i, :, :], ALU.mult))
                if i >= 2:
                    dve.wait_ge(S("x5_used"), i - 1)
                TT(xs5[:, i % 2, 0, :], rotC[:, 0, :], rotC[:, 1, :], ALU.subtract).then_inc(S("xr5_ready"), 1)

            def skip(q):
                dve.wait_ge(S("x5_used"), 4 * q + 4)
                STT(yv[:, q, :], uT[:, q, :], pcol(0, R_D + q), accf[:, q * 512:q * 512 + SEQ],
                    ALU.mult, ALU.add).then_inc(S("yv_ready"), 1)

            def z_low(q):
                dve.wait_ge(S("z_hi"), q + 1)
                TT(XL[:, q, :], zf[:, q, :], XH[:, q, :].bitcast(F32), ALU.subtract).then_inc(S("z_lo"), 1)

            for i in range(ST):
                scan_in(i)
                if i % 4 == 1 and i > 4:
                    skip(i // 4 - 1)
            skip(3)
            lo_to(5)
            for q in range(4):
                z_low(q)
            for b in range(2):
                bs = slice(2 * b, 2 * b + 2)
                dve.wait_ge(S("gt5_ready"), b + 1)
                STT(z2f[:, bs, :], gt5[:, bs, :], 1.0, zf[:, bs, :], ALU.add, ALU.mult).then_inc(S("z2_ready"), 1)
            for b in range(2):
                bs, bo = slice(2 * b, 2 * b + 2), slice(4 + 2 * b, 6 + 2 * b)
                dve.wait_ge(S("z2_hi"), b + 1)
                STT(XL[:, bo, :], z2f[:, bs, :], 0.5, XH[:, bo, :].bitcast(F32), ALU.mult, ALU.subtract)\
                    .then_inc(S("z2_lo"), 1)
            lo_to(6)
            post(0, 2)
            lo_to(8)

            def mlp(layer, first, count):
                pre(count)
                xT_low(1 + 2 * layer, lambda k: gain(layer, 2, k))
                base = layer * MC

                def hidden(c, par):
                    dve.wait_ge(S("hid_read"), c + base + 1)
                    link(TT(sq_b[:, par, :], relu_b[:, par, :], relu_b[:, par, :], ALU.mult))
                    dve.wait_ge(S("hid_hi"), c + base + 1)
                    TT(HL[:, par, :, :], sq_b[:, par, :].rearrange("p (j t) -> p j t", j=2),
                       HH[:, par, :, :].bitcast(F32), ALU.subtract).then_inc(S("hid_lo"), 1)

                lo_to(first + 3)
                hidden(0, 0)
                with dve.Fori(0, (MC - 2) // 2) as i:
                    ring.enter(i, 1)
                    steps.enter(i, 2)
                    lo_next()
                    hidden(i * 2 + 1, 1)
                    lo_next()
                    lo_next()
                    hidden(i * 2 + 2, 0)
                    lo_next()
                ring.leave((MC - 2) // 2)
                steps.leave((MC - 2) // 2)
                lo_to(first + 2 * MC)
                hidden(MC - 1, 1)
                lo_to(first + 2 * MC + 2)
                post(2 * layer + 1, count + 1)
                lo_to(first + 2 * MC + 3)

            mlp(0, 5, 3)

            pre(5)
            xT_low(2, lambda k: gain(1, 0, k))
            lo_to(P_ATT + 12)
            dve.wait_ge(S("pj_read"), 5)
            link(TS(wi_s[:, :, :], pj[:, :, WIOFF:WIOFF + IH], (IH ** -0.5) * (HD ** -0.5), None, ALU.mult))
            for tb in range(TB):
                for c0, nh in ((0, 20), (QIOFF, 9)):
                    x = pj[:, tb, c0:c0 + nh * HD].rearrange("p (a d) -> p a d", d=HD)
                    r1 = rope1[:, 0:nh * HD].rearrange("p (a d) -> p a d", d=HD)
                    r2 = rope2[:, 0:nh * HD].rearrange("p (a d) -> p a d", d=HD)
                    TT(r1, x, cosT[:, tb, :].unsqueeze(1).to_broadcast([P, nh, HD]), ALU.mult)
                    TT(r2[:, :, 0:32], x[:, :, 32:64], sinT[:, tb, 0:32].unsqueeze(1).to_broadcast([P, nh, 32]), ALU.mult)
                    link(TT(r2[:, :, 32:64], x[:, :, 0:32], sinT[:, tb, 32:64].unsqueeze(1).to_broadcast([P, nh, 32]),
                            ALU.mult))
                    nq = nh - (4 if nh == 20 else 1)
                    at = 0 if nh == 20 else 1536
                    TT(roped[:, tb, at:at + nq * HD], rope1[:, 0:nq * HD], rope2[:, 0:nq * HD], ALU.add)
                    for dup in range(2):
                        o = roped[:, tb, at + nq * HD:at + nq * HD + (nh - nq) * 2 * HD]\
                            .rearrange("p (a u d) -> p a u d", u=2, d=HD)[:, :, dup, :]
                        last = TT(o, r1[:, nq:nh, :], r2[:, nq:nh, :], ALU.add)
                    if nh == 20:
                        link(last)
                last.then_inc(S("rope_ready"), 1)
                dve.wait_ge(S("rope_ready"), tb + 1)
            caus = cst[:, C_CAUS:C_CAUS + P]
            for tb in range(TB):
                K = P * (tb + 1)
                sc, lf, kp = score[:, tb, 0:K], left[:, tb, 0:K], keep[:, tb, 0:K]
                for job, (jtb, h0, nh) in enumerate(IJOBS):
                    if jtb != tb:
                        continue
                    dve.wait_ge(S("rel_read"), job + 1)
                    for b in range(nh):
                        hd = h0 + 2 * b
                        r = rel[:, job % 2, b * K:(b + 1) * K]
                        w = wi_s[:, tb, hd:hd + 1]
                        ins_ = TS(sc, r, w, None, ALU.mult) if hd == 0 else STT(sc, r, w, sc, ALU.mult, ALU.add)
                        if b < nh - 1:
                            link(ins_)
                    ins_.then_inc(S("rel_used"), 1)
                    dve.wait_ge(S("rel_used"), job + 1)
                link(TT(sc[:, K - P:K], sc[:, K - P:K], caus, ALU.add))
                src = sc
                for _ in range(TOPK // 8):
                    link(V.max(top8[:, :], src))
                    link(V.match_replace(lf, top8[:, :], src, TAKEN))
                    src = lf
                link(TS(kp, lf, -2e38, NEG, ALU.is_gt, ALU.mult))
                link(TT(kp[:, K - P:K], kp[:, K - P:K], caus, ALU.add))

            def masked1(n):
                tb, h0, nh = JOBS1[n]
                K = P * (tb + 1)
                dve.wait_ge(S("s1_psum"), n + 1)
                if n >= 3:
                    dve.wait_ge(S("pT1_psum"), n - 2)
                s = p1[:, n % 3, :].rearrange("p (a k) -> p a k", a=nh)
                TT(s, wk[:, n % 4, :].rearrange("p (a k) -> p a k", a=nh),
                   keep[:, tb, 0:K].unsqueeze(1).to_broadcast([P, nh, K]), ALU.add).then_inc(S("s1_read"), 1)
                dve.wait_ge(S("s1_read"), n + 1)
                link(V.tensor_reduce(small[:, n % 2, 0, 0:nh], s, AXIS.X, ALU.max))
                TS(small[:, n % 2, 1, 0:nh], small[:, n % 2, 0, 0:nh], -HD ** -0.5, None, ALU.mult)\
                    .then_inc(S("m1_ready"), 1)

            def normed1(n):
                tb, h0, nh = JOBS1[n]
                K = P * (tb + 1)
                dve.wait_ge(S("e1_ready"), n + 1)
                link(V.reciprocal(small[:, n % 2, 3, 0:nh], small[:, n % 2, 2, 0:nh]))
                s = p1[:, n % 3, :].rearrange("p (a k) -> p a k", a=nh)
                TT(s, s, small[:, n % 2, 3, 0:nh].unsqueeze(2).to_broadcast([P, nh, K]), ALU.mult)\
                    .then_inc(S("p1_ready"), 1)

            def o1_low(n):
                tb, h0, nh = JOBS1[n]
                dve.wait_ge(S("o1_hi"), n + 1)
                o = 1024 + (n % 2) * 512
                ts = slice(tb * P, (tb + 1) * P)
                hs = slice(64 * (h0 % 2), 64 * (h0 % 2) + 64)
                TT(XL[hs, h0 // 2:h0 // 2 + nh, ts], accf[hs, o:o + nh * P].rearrange("p (a t) -> p a t", t=P),
                   XH[hs, h0 // 2:h0 // 2 + nh, ts].bitcast(F32), ALU.subtract).then_inc(S("o1_lo"), 1)

            N1 = len(JOBS1)
            masked1(0)
            for n in range(N1):
                if n + 1 < N1:
                    masked1(n + 1)
                normed1(n)
                if n >= 1:
                    o1_low(n - 1)
            o1_low(N1 - 1)
            lo_to(P_ATT + 15)
            post(2, 6)
            lo_to(P_ATT + 16)
            mlp(1, P_ATT + 13, 7)

            pre(9)
            xT_low(4, lambda k: pcol(0, R_N1 + k))
            lo_to(P_B2 + 3)
            dve.wait_ge(S("params_in"), 16 * N_PARAM)
            done(P_B2)
            for tb in range(TB):
                last = TT(sp1[:, tb, :], wk[:, tb, 0:SH], dtb[:, :], ALU.add)
            last.then_inc(S("dt_read"), 1)
            dve.wait_ge(S("dt_read"), 1)
            link(STT(sp2[:, :, :], sp1[:, :, :], -1.0, sp1[:, :, :], ALU.mult, ALU.min))
            TS(sp1[:, :, :], sp1[:, :, :], 0.0, None, ALU.max).then_inc(S("sp_arg"), 1)
            dve.wait_ge(S("sp_exp"), 1)
            link(TS(sp3[:, :, :], sp2[:, :, :], 2.0, None, ALU.add))
            link(V.reciprocal(sp3[:, :, :], sp3[:, :, :]))
            link(TT(sp2[:, :, :], sp2[:, :, :], sp3[:, :, :], ALU.mult))
            link(TT(sp3[:, :, :], sp2[:, :, :], sp2[:, :, :], ALU.mult))
            link(TS(dt_tok[:, :, :], sp3[:, :, :], 2.0 / 17, 2.0 / 15, ALU.mult, ALU.add))
            for n in (13, 11, 9, 7, 5, 3, 1):
                link(TT(dt_tok[:, :, :], dt_tok[:, :, :], sp3[:, :, :], ALU.mult))
                link(TS(dt_tok[:, :, :], dt_tok[:, :, :], 2.0 / n, None, ALU.add))
            link(TT(dt_tok[:, :, :], dt_tok[:, :, :], sp2[:, :, :], ALU.mult))
            link(TT(dt_tok[:, :, :], dt_tok[:, :, :], sp1[:, :, :], ALU.add))
            dve.wait_ge(S("alog_ready"), 1)
            for tb in range(TB):
                last = STT(a_tok[:, tb, :], dt_tok[:, tb, :], -1.0, alog[:, :], ALU.mult, ALU.mult)
            last.then_inc(S("a_ready"), 1)
            dve.wait_ge(S("a_ready"), 1)
            for tb in range(TB):
                for at, t in ((G_DT, dt_tok), (G_A, a_tok)):
                    last = V.tensor_copy(gpall[:, :, at + 4 * tb:at + 4 * tb + 4],
                                         t[:, tb, :].rearrange("p (g m) -> p g m", g=SG))
            link(last)

            def head_norm(which):
                dve.wait_ge(S("qkv2_read"), 3 if which == 0 else 9)
                for tb in range(TB):
                    x = qk2[:, tb, :].rearrange("p (a d) -> p a d", d=HD)
                    link(TT(yf[:, 0:AW], qk2[:, tb, :], qk2[:, tb, :], ALU.mult))
                    link(V.tensor_reduce(hv2[:, :], yf[:, 0:AW].rearrange("p (a d) -> p a d", d=HD), AXIS.X, ALU.add))
                    link(TS(hv2[:, :], hv2[:, :], 1.0 / HD, EPS, ALU.mult, ALU.add))
                    rsqrt(hv2[:, :], ht2[:, :], hr2[:, :])
                    last = TT(x, x, hr2[:, :].unsqueeze(2).to_broadcast([P, 24, HD]), ALU.mult)
                    if tb == 0:
                        link(last)
                last.then_inc(S("qk2_ready"), 1)

            lo_to(P_B2 + 9)
            head_norm(0)
            lo_to(P_B2 + 22)
            head_norm(1)

            def masked2(n):
                hd, tb = JOBS2[n]
                K = P * (tb + 1)
                dve.wait_ge(S("s2_psum"), n + 1)
                if n >= 2:
                    dve.wait_ge(S("pT2_psum"), n - 1)
                s = p2[:, n % 2, 0:3 * K]
                o = (n % 2) * 1024
                TT(s.rearrange("p (g k) -> p g k", g=3), wkf[:, o:o + 3 * K].rearrange("p (g k) -> p g k", g=3),
                   dilm[:, :, SEQ - K:SEQ], ALU.add).then_inc(S("s2_read"), 1)
                dve.wait_ge(S("s2_read"), n + 1)
                link(V.tensor_reduce(small[:, n % 2, 0, 0:1], s, AXIS.X, ALU.max))
                TS(small[:, n % 2, 1, 0:1], small[:, n % 2, 0, 0:1], -HD ** -0.5, None, ALU.mult)\
                    .then_inc(S("m2_ready"), 1)

            def normed2(n):
                hd, tb = JOBS2[n]
                dve.wait_ge(S("e2_ready"), n + 1)
                link(V.reciprocal(small[:, n % 2, 3, 0:1], small[:, n % 2, 2, 0:1]))
                s = p2[:, n % 2, 0:3 * P * (tb + 1)]
                TS(s, s, small[:, n % 2, 3, 0:1], None, ALU.mult).then_inc(S("p2_ready"), 1)

            def o2_low(j):
                hd, tb = JOBS2[2 * j + 1]
                ts = slice(tb * P, (tb + 1) * P)
                dve.wait_ge(S("o2_hi"), j + 1)
                TT(OL[:, hd // 2, ts], accf[:, 1024:1024 + P], OH[:, hd // 2, ts].bitcast(F32), ALU.subtract)\
                    .then_inc(S("o2_lo"), 1)

            masked2(0)
            for n in range(16):
                if n + 1 < 16:
                    masked2(n + 1)
                if n % 2 == 0:
                    lo_to(P_B2 + 19 + n // 2 + 3)
                normed2(n)
                if n % 2 == 0 and n >= 2:
                    o2_low(n // 2 - 1)
            o2_low(7)
            lo_to(P_SSD + 1)
            dve.wait_ge(S("gate_read"), 8)
            TS(yf, yf, 0.5, 0.5, ALU.mult, ALU.add)
            link(TS(g_ssd[:, :, :], g_ssd[:, :, :], 0.5, 0.5, ALU.mult, ALU.add))
            done(P_SSD - 1)
            for tb in range(TB):
                last = TT(y[:, tb, :], y[:, tb, :], acc[:, tb, :], ALU.mult)
            V.memset(xpad[:, :, 0:3], 0.0)
            V.memset(bcpad[:, :, 0:3], 0.0).then_inc(S("merged_attn"), 1)
            dve.wait_ge(S("merged_attn"), 1)
            lo_to(P_SSD + 2)

            def conv4(dst, src, w, b):
                link(TS(dst, src[:, 0:SEQ], w[0], b, ALU.mult, ALU.add))
                for k in (1, 2):
                    link(STT(dst, src[:, k:k + SEQ], w[k], dst, ALU.mult, ALU.add))
                return STT(dst, src[:, 3:3 + SEQ], w[3], dst, ALU.mult, ALU.add)

            def ssd_step(g, par, proj, ssd, fin, splits, first=False):
                gpn, gpv = gp[:, par, :], gp[:, 1 - par, :]

                def one(v, at):
                    return v[:, at:at + 1]

                if splits != 3:
                    lo_next()
                if fin:
                    dve.wait_ge(S("gn_psum"), g - 1)
                    TS(gv_[:, :], wk[:, 3, 0:SEQ], 1.0 / 256, EPS, ALU.mult, ALU.add).then_inc(S("gn_read"), 1)
                    dve.wait_ge(S("gn_read"), g - 1)
                    rsqrt(gv_[:, :], gt_[:, :], gr_[:, :])
                    for j in range(2):
                        last = STT(yn[:, j, :], yz[:, par, j, :], one(gpn, G_NG + j), gr_[:, :], ALU.mult, ALU.mult)
                    last.then_inc(S("yn_ready"), 1)
                    dve.wait_ge(S("yn_ready"), g - 1)
                if proj:
                    gi = g if isinstance(g, int) else g
                    V.tensor_copy(gpn, gpall[:, bass.ds(gi, 1), :].rearrange("p a n -> p (a n)"))\
                        .then_inc(S("gp_ready"), 1)
                    dve.wait_ge(S("gp_ready"), g + 1)
                if ssd:
                    dve.wait_ge(S("X_psum"), g)
                    if not (isinstance(g, int) and g < 2):
                        dve.wait_ge(S("y_psum"), g - 1)
                    for tb in range(TB):
                        last = TT(Xt[:, tb, :].rearrange("p (m d) -> p m d", m=4),
                                  wk[:, 3, tb * SEQ:(tb + 1) * SEQ].rearrange("p (m d) -> p m d", m=4),
                                  gpv[:, G_DT + 4 * tb:G_DT + 4 * tb + 4].unsqueeze(2).to_broadcast([P, 4, HD]), ALU.mult)
                    last.then_inc(S("X_read"), 1)
                if fin:
                    dve.wait_ge(S("Y_hi"), g - 1)
                    TT(HL[:, par, :, :], yn[:, :, :], HH[:, par, :, :].bitcast(F32), ALU.subtract)\
                        .then_inc(S("Y_lo"), 1)
                if splits >= 3:
                    lo_next()
                if proj:
                    dve.wait_ge(S("xs_read"), g + 1)
                    if not first:
                        dve.wait_ge(S("xtanh_ready"), g)
                    for j in range(2):
                        last = conv4(xconv[:, j, :], xpad[:, j, :], [one(gpn, G_WX + 2 * k + j) for k in range(4)],
                                     one(gpn, G_BX + j))
                        if j == 0:
                            link(last)
                    last.then_inc(S("xconv_ready"), 1)
                if ssd:
                    dve.wait_ge(S("CB_psum"), g)
                    V.tensor_copy(cbs[:, :], wk[:, 3, 0:384]).then_inc(S("CB_read"), 1)
                    dve.wait_ge(S("CB_read"), g)
                    for m in range(4):
                        dve.wait_ge(S("L_read"), g * 4 - 4 + m + 1)
                        TT(Lm[:, m, :], Lm[:, m, :], cbs[:, :], ALU.mult).then_inc(S("M_ready"), 1)
                if splits >= 3:
                    lo_next()
                if proj:
                    dve.wait_ge(S("xtanh_ready"), g + 1)
                    STT(xsc[:, par, :, :], xtanh[:, :, :], 1.0, xconv[:, :, :], ALU.add, ALU.mult)\
                        .then_inc(S("xsc_ready"), 1)
                    dve.wait_ge(S("bc_read"), g + 1)
                    dve.wait_ge(S("xsc_ready"), g + 1)
                    for j, (w, b) in enumerate(((G_WB, G_BB), (G_WC, G_BC))):
                        last = conv4(bconv[:, j, :], bcpad[:, j, :], [one(gpn, w + k) for k in range(4)], one(gpn, b))
                        if j == 0:
                            link(last)
                    last.then_inc(S("bconv_ready"), 1)
                if splits >= 3:
                    lo_next()
                if proj:
                    dve.wait_ge(S("btanh_ready"), g + 1)
                    STT(bcc[:, par, :, :], btanh[:, :, :], 1.0, bconv[:, :, :], ALU.add, ALU.mult)\
                        .then_inc(S("bcc_ready"), 1)
                if ssd:
                    link(STT(zt[:, 1 - par, :, :], zt[:, 1 - par, :, :], 1.0, zc[:, 1 - par, :, :], ALU.add, ALU.mult))
                    dve.wait_ge(S("y_psum"), g)
                    for j in range(2):
                        last = STT(yz[:, 1 - par, j, :], xsc[:, 1 - par, j, :], one(gpv, G_D + j),
                                   wk[:, 1, j * SEQ:(j + 1) * SEQ], ALU.mult, ALU.add)
                    last.then_inc(S("y_read"), 1)
                    dve.wait_ge(S("y_read"), g)
                    TT(yz[:, 1 - par, :, :], yz[:, 1 - par, :, :], zt[:, 1 - par, :, :], ALU.mult)\
                        .then_inc(S("yz_ready"), 1)

            ssd_step(0, 0, True, False, False, 3, first=True)
            ssd_step(1, 1, True, True, False, 3)
            with dve.Fori(0, 3) as i:
                ring.enter(i, 2)
                steps.enter(i, 2 * (10 + 2 * 7 + 1))
                ssd_step(i * 2 + 2, 0, True, True, True, 4)
                ssd_step(i * 2 + 3, 1, True, True, True, 4)
            ring.leave(3)
            steps.leave(3)
            ssd_step(8, 0, False, True, True, 1)
            ssd_step(9, 1, False, False, True, 1)
            done(P_WOUT2 - 1)
            for tb in range(TB):
                link(TT(g_ssd[:, tb, :], g_ssd[:, tb, :], acc[:, tb, :], ALU.mult))
                last = TT(y[:, tb, :], y[:, tb, :], g_ssd[:, tb, :], ALU.add)
            last.then_inc(S("merged"), 1)
            lo_to(P_WOUT2 + 2)
            for b in range(4):
                dve.wait_ge(S("mT_hi"), b + 1)
                TT(XL[:, 2 * b:2 * b + 2, :], wk[:, b, :].rearrange("p (k t) -> p k t", k=2),
                   XH[:, 2 * b:2 * b + 2, :].bitcast(F32), ALU.subtract).then_inc(S("mT_lo"), 1)
            first = P_WOUT2 + 4
            lo_to(first + 2)
            done(first - 1)
            for tb in range(TB):
                last = TT(h[:, tb, :], h[:, tb, :], acc[:, tb, :], ALU.add)
            last.then_inc(S("h_ready"), 1)
            lo_to(first + 3)
            link(V.memset(fpad[:, :, :, 0:2], 0.0))
            pre(10)
            xT_low(5, lambda k: pcol(0, R_N2 + k))

            def ffn(c, par):
                V.tensor_copy(fp[:, par, :], fpall[:, bass.ds(c, 1), :].rearrange("p a n -> p (a n)"))\
                    .then_inc(S("fp_ready"), 1)
                dve.wait_ge(S("fp_ready"), c + 1)
                dve.wait_ge(S("gv_read"), c + 1)
                for j in range(2):
                    o, s, w = fconv[:, par, j, :], fpad[:, par, j, :], [fp[:, par, 4 * j + k:4 * j + k + 1] for k in range(4)]
                    link(TS(o, s[:, 0:SEQ], w[0], w[3], ALU.mult, ALU.add))
                    link(STT(o, s[:, 1:1 + SEQ], w[1], o, ALU.mult, ALU.add))
                    last = STT(o, s[:, 2:2 + SEQ], w[2], o, ALU.mult, ALU.add)
                    if j == 0:
                        link(last)
                last.then_inc(S("fconv_ready"), 1)
                dve.wait_ge(S("ftanh_ready"), c + 1)
                link(STT(fhid[:, par, :], ftanh[:, par, :], 1.0, fconv[:, par, 0, :], ALU.add, ALU.mult))
                TT(fhid[:, par, :], fhid[:, par, :], fconv[:, par, 1, :], ALU.mult).then_inc(S("fh_ready"), 1)
                dve.wait_ge(S("f_hi"), c + 1)
                TT(HL[:, par, 0, :], fhid[:, par, :], HH[:, par, 0, :].bitcast(F32), ALU.subtract)\
                    .then_inc(S("f_lo"), 1)

            ffn(0, 0)
            with dve.Fori(0, (FC - 2) // 2) as i:
                ring.enter(i, 1)
                steps.enter(i, 12)
                lo_next()
                ffn(i * 2 + 1, 1)
                lo_next()
                lo_next()
                ffn(i * 2 + 2, 0)
                lo_next()
            ring.leave((FC - 2) // 2)
            steps.leave((FC - 2) // 2)
            lo_to(first + 2 * FC - 1)
            ffn(FC - 1, 1)
            done(first + 2 * FC - 1)
            for tb in range(TB):
                last = TT(y[:, tb, :], h[:, tb, :], acc[:, tb, :], ALU.add)
            last.then_inc(S("out_ready"), 1)


def param_loads(ins, rows, pair, braw, craw, alog, dtb):
    def r128(ap):
        return ap.rearrange("(r c) -> r c", c=P)

    loads = [
        (rows[R_NG:R_NG + 64, 0, :], ins["norm_g"].rearrange("a b (k c) -> (a b k) c", c=P)),
        (rows[R_N1:R_N1 + 8, 0, :], r128(ins["norm1_g_2"][0])),
        (rows[R_N2:R_N2 + 8, 0, :], r128(ins["norm2_g_2"][0])),
        (rows[R_SN:R_SN + 16, 0, :], r128(ins["ssd_norm_g_2"][0])),
        (rows[R_D:R_D + 4, 0, :], ins["ssm_d"][0].rearrange("(q a) c -> q (a c)", q=4)),
        (rows[R_LR:R_LR + 16, 0, :], ins["ssm_lam_re"][0].rearrange("(i q) s -> i (q s)", q=2)),
        (rows[0:128, 1, :], ins["ssd_conv_w_2"][0].rearrange("k (t c) -> (k t) c", c=P)),
        (rows[R_CB:R_CB + 32, 2, :], r128(ins["ssd_conv_b_2"][0])),
        (rows[R_FB:R_FB + 44, 2, :], r128(ins["ffn_conv_b_2"][0])),
        (rows[R_LI:R_LI + 16, 2, :], ins["ssm_lam_im"][0].rearrange("(i q) s -> i (q s)", q=2)),
        (rows[0:88, 3, :], ins["ffn_conv_w_2"][0, 0:2].rearrange("k (t c) -> (k t) c", c=P)),
        (rows[0:44, 4, :], r128(ins["ffn_conv_w_2"][0, 2])),
        (pair[:, 0:16], ins["ssm_log_dt"][0].rearrange("(i q) -> q i", q=2)),
        (pair[:, 16:32], ins["d_skip_2"][0].rearrange("(i q) -> q i", q=2)),
        (alog[:, :], ins["a_log_2"][0].partition_broadcast(P)),
        (dtb[:, :], ins["dt_bias_2"][0].partition_broadcast(P)),
    ]
    for at, name in ((R_QG, "q_norm_g_2"), (R_KG, "k_norm_g_2")):
        for half in range(2):
            loads.append((rows[at:at + 1, 2, 64 * half:64 * half + 64], ins[name]))
    for r, (b, c) in enumerate((("ssm_b_re", "ssm_c_re"), ("ssm_b_im", "ssm_c_im"))):
        loads.append((braw[:, r, :, :], ins[b][0].rearrange("(i q) s c -> (q s) i c", q=2)))
        loads.append((craw[:, r, :, :], ins[c][0].rearrange("(t a) c s -> (a c) t s", t=4)))
    return loads





def constants():
    c = np.zeros((P, C_END), np.float32)
    i, j = np.arange(P)[:, None], np.arange(P)[None, :]
    c[:, C_ID:C_ID + P] = i == j
    c[:, C_UU:C_UU + 2 * P] = np.tile(i <= j, 2)
    c[:, C_GT:C_GT + P] = i > j
    c[:, C_NEGT:C_NEGT + P] = np.where(j < i, NEG, 0)
    c[:, C_CAUS:C_CAUS + P] = np.where(j > i, NEG, 0)
    for g, (window, dil) in enumerate(((128, 1), (512, 4), (2048, 16))):
        dist = np.concatenate([P + i - j, i - j], axis=1)
        ok = (dist >= 0) & (dist <= window) & (dist % dil == 0)
        c[:, C_DIL + g * SEQ:C_DIL + (g + 1) * SEQ] = np.where(ok, 0, NEG)
    half = HD // 2
    freq = np.float32(10000.0) ** (-np.arange(half, dtype=np.float32) * np.float32(2.0) / np.float32(HD))
    ang = (np.arange(SEQ, dtype=np.float32)[:, None] * freq[None, :].astype(np.float32)).astype(np.float32)
    cos, sin = np.cos(ang), np.sin(ang)
    for b in range(TB):
        ts = slice(b * P, (b + 1) * P)
        c[:, C_COS + b * HD:C_COS + (b + 1) * HD] = np.concatenate([cos[ts], cos[ts]], axis=1)
        c[:, C_SIN + b * HD:C_SIN + (b + 1) * HD] = np.concatenate([-sin[ts], sin[ts]], axis=1)
    c[0, C_SEL:C_SEL + 64] = 1
    c[1, C_SEL + 64:C_SEL + 128] = 1
    odd = (np.arange(P) // CH) % 2
    c[:, C_PAR], c[:, C_PAR + 1], c[:, C_PAR + 2], c[:, C_PAR + 3] = 1 - odd, odd, odd - 1, -odd
    return c


_INS = ["x", "norm_g", "mlp_w1", "mlp_w2", "ssm_w_in", "ssm_lam_re", "ssm_lam_im", "ssm_log_dt", "ssm_b_re",
        "ssm_b_im", "ssm_c_re", "ssm_c_im", "ssm_d", "ssm_w_glu", "ssm_w_out", "att_w_in", "att_w_out", "norm1_g_2",
        "w_in_2", "ssd_conv_w_2", "ssd_conv_b_2", "dt_bias_2", "a_log_2", "d_skip_2", "ssd_norm_g_2",
        "w_ssd_proj_2", "q_norm_g_2", "k_norm_g_2", "w_attn_proj_2", "w_out_2", "norm2_g_2", "w_up_2",
        "ffn_conv_w_2", "ffn_conv_b_2", "w_down_2"]


def kernel(**inputs):
    import concourse.bacc as bacc
    from concourse.bass_utils import run_bass_kernel_spmd

    nc = bacc.Bacc("TRN2", target_bir_lowering=False, num_devices=1)
    arrays, aps = {}, {}
    for name in _INS:
        a = np.ascontiguousarray(inputs[name])
        arrays[f"in_{name}"] = a
        aps[name] = nc.dram_tensor(f"in_{name}", a.shape, mybir.dt.from_np(a.dtype), kind="ExternalInput").ap()
    arrays["consts"] = constants()
    aps["consts"] = nc.dram_tensor("consts", (P, C_END), F32, kind="ExternalInput").ap()
    out = nc.dram_tensor("out", (1, SEQ, D), F32, kind="ExternalOutput").ap()
    build(nc, aps, out)
    r = run_bass_kernel_spmd(nc, [arrays], core_ids=[0])
    return r.results[0]["out"]
```

```python
import concourse.bass as bass
from concourse import mybir
from contextlib import ExitStack

import numpy as np

F32 = mybir.dt.float32
F32R = mybir.dt.float32r
BF16 = mybir.dt.bfloat16
I32 = mybir.dt.int32
ALU = mybir.AluOpType
ACT = mybir.ActivationFunctionType
AXIS = mybir.AxisListType

P = 128
SEQ = 256
TB = SEQ // P
D = 1024
KD = D // P
EPS = 1e-6
NEG = -1e30
TAKEN = -3e38

GROUPS, CH, STATE, E5 = 32, 16, 64, 512
ST = GROUPS * STATE // P
E_SPLIT = 10
DFF = 4 * D
MC = DFF // 256
NH, NKV, HD, IH, TOPK = 16, 4, 64, 8, 64
QW, KW, IW = NH * HD, NKV * HD, IH * HD
VOFF, QIOFF = QW + KW, QW + 2 * KW
KIOFF = QIOFF + IW
WIOFF = KIOFF + HD
ATT_COLS = WIOFF + IH
ATT_TAIL = ATT_COLS - 4 * 512
DIN, SG, SH, DSTATE = 2048, 8, 32, 128
ZOFF, XSOFF = 0, DIN
BOFF = XSOFF + DIN
COFF = BOFF + SG * DSTATE
DTOFF = COFF + SG * DSTATE
AW = 3 * 8 * 64
Q2OFF = DTOFF + SH
K2OFF, V2OFF = Q2OFF + AW, Q2OFF + 2 * AW
GATEOFF = Q2OFF + 3 * AW
DFF2 = 2816
FC = DFF2 // P

C_ID, C_SEL, C_PAR, C_UU, C_GT, C_NEGT, C_CAUS, C_DIL, C_COS, C_SIN = (
    0, 128, 384, 388, 644, 772, 900, 1028, 1796, 1924)
C_END = 2052
C_FIRST = C_UU
R_LR, R_LI, R_D = 0, 16, 32
R_CB, R_FB, R_SN, R_QG, R_KG = 0, 32, 76, 92, 93
ROWS = [36, 128, 94, 88, 44]
JOBS1 = [(0, h0, 4) for h0 in (0, 1, 8, 9)] + [(1, h0, 2) for h0 in (0, 1, 4, 5, 8, 9, 12, 13)]
IJOBS = [(0, h0, 4) for h0 in (0, 1)] + [(1, h0, 2) for h0 in (0, 1, 4, 5)]
JOBS2 = [(2 * pr + hh, tb) for pr in range(4) for tb in range(TB) for hh in range(2)]
G_WX, G_WB, G_WC, G_BX, G_BB, G_BC, G_NG, G_D, G_DT, G_A, G_NB, G_END = 0, 8, 12, 16, 18, 19, 20, 22, 24, 32, 40, 52
N_S5, N_BC5, N_LATE = 4, 4, 13
P_ATT, P_B2, P_SSD, P_WOUT2 = 37, 82, 111, 143


class Ring:

    def __init__(self):
        self.n, self.uses, self.off = 0, [0] * 4, 0

    def next(self):
        s, k, n = self.n % 4, self.uses[self.n % 4] + self.off, self.n + self.off * 4
        self.n += 1
        self.uses[s] += 1
        return s, k, n

    def enter(self, i, per_slot):
        self.off, self.per = i * per_slot, per_slot

    def leave(self, turns):
        self.off = 0
        self.n += 4 * self.per * (turns - 1)
        self.uses = [u + self.per * (turns - 1) for u in self.uses]


class Steps:

    def __init__(self, eng, sem):
        self.eng, self.sem, self.n, self.off = eng, sem, 0, 0

    def link(self, ins):
        ins.then_inc(self.sem, 1)
        self.n += 1
        self.eng.wait_ge(self.sem, self.off + self.n)

    def enter(self, i, per):
        self.off, self.start, self.per = i * per, self.n, per

    def leave(self, turns):
        assert self.n - self.start == self.per, (self.n - self.start, self.per)
        self.n += self.per * (turns - 1)
        self.off = 0


def build(nc, ins, out):
    ctx = ExitStack()
    with ctx:
        def sb(name, shape, dt=F32):
            return ctx.enter_context(nc.sbuf_tensor(name, shape, dt))

        sems = {}

        def S(name):
            if name not in sems:
                sems[name] = ctx.enter_context(nc.semaphore(name))
            return sems[name]

        raw = sb("raw", [P, 2, 2, 1024])
        HI = sb("HI", [P, 4, 2048], F32R)
        LO = sb("LO", [P, 4, 2048], F32R)
        XH = sb("XH", [P, KD, SEQ], F32R)
        XL = sb("XL", [P, KD, SEQ], F32R)
        HH = sb("HH", [P, 2, 2, SEQ], F32R)
        HL = sb("HL", [P, 2, 2, SEQ], F32R)
        OH = HH[:, :, :, :].rearrange("p a b t -> p (a b) t")
        OL = HL[:, :, :, :].rearrange("p a b t -> p (a b) t")
        cst = sb("cst", [P, C_END])
        cols = sb("cols", [P, 5, P])
        gpall = sb("gpall", [P, SG, G_END])
        gp = sb("gp", [P, 2, G_END])
        fpall = sb("fpall", [P, FC, 8])
        fp = sb("fp", [P, 2, 8])
        h = sb("h", [P, TB, D])
        y = sb("y", [P, TB, D])
        gpost = sb("gpost", [P, D])
        gpre = sb("gpre", [P, D])
        half = sb("half", [P, 2])
        ct5n = sb("ct5n", [P, 4, P])
        zero_bf = sb("zero_bf", [P, 512], BF16)
        id_bf = sb("id_bf", [P, P], BF16)
        neg_bf = sb("neg_bf", [P, P], BF16)
        ones = sb("ones", [P, P])
        ssq = sb("ssq", [P, TB, 2])
        nv = sb("nv", [P, 2])
        rstd = sb("rstd", [P, 2])
        arena = sb("arena", [P, 15520])
        acc = ctx.enter_context(nc.psum_tensor("acc", [P, TB, D], F32))
        wk = ctx.enter_context(nc.psum_tensor("wk", [P, 4, 512], F32))
        accf = acc[:, :, :].rearrange("p a n -> p (a n)")

        def carve(at, *shape):
            n = int(np.prod(shape))
            v = arena[:, at:at + n]
            if len(shape) == 2:
                return v.rearrange("p (a b) -> p a b", a=shape[0])
            if len(shape) == 3:
                return v.rearrange("p (a b c) -> p a b c", a=shape[0], b=shape[1])
            return v

        ident = cst[:, C_ID:C_ID + P]
        cosT = cst[:, C_COS:C_COS + 128].rearrange("p (b d) -> p b d", b=TB)
        sinT = cst[:, C_SIN:C_SIN + 128].rearrange("p (b d) -> p b d", b=TB)
        dilm = cst[:, C_DIL:C_DIL + 768].rearrange("p (g n) -> p g n", g=3)

        def pcol(block, r):
            return cols[:, block, r:r + 1]

        def halves(t, tb, n):
            return t[:, tb, n * 512:(n + 1) * 512]

        etmp = y[:, :, :].rearrange("p b n -> p (b n)")
        e_tab = carve(0, ST, 2, SEQ)
        s5 = 8192
        uT = carve(s5, 4, SEQ)
        rows = carve(s5 + 1024, 5, P)
        rotA = carve(s5 + 1024, 2, 2, SEQ)
        zz = carve(s5 + 2048, 2, 2, SEQ)
        rotB = carve(s5 + 3072, 2, 2, SEQ)
        prod_re = carve(s5 + 4096, 2, 2, SEQ)
        prod_im = y[:, 1, :].rearrange("p (a b t) -> p a b t", a=2, b=2)
        bt5 = carve(s5 + 5120, 2, 4, P)
        ct5 = carve(s5 + 6144, 2, 4, P)
        sm5 = carve(s5 + 7168, 10, 16)
        bpad = carve(s5 + 2048, 2, 16, 32)
        cpad = carve(s5 + 3072, 2, 4, P)
        braw = carve(s5 + 4096, 2, 16, 16)
        craw = carve(s5 + 4608, 2, 4, 64)
        bq = etmp[:, 256:512].rearrange("p (a b) -> p a b", a=16)
        yv = carve(0, 4, SEQ)
        gt5 = carve(2048, 4, SEQ)
        zf = y[:, 0, :].rearrange("p (q t) -> p q t", q=4)
        z2f = y[:, 1, :].rearrange("p (q t) -> p q t", q=4)
        pair = sb("pair", [1, 64])
        pairb = sb("pairb", [P, 32])
        alog = sb("alog", [P, SH])
        dtb = sb("dtb", [P, SH])

        squared = carve(13312, 2, 512)
        relu_b = carve(0, 2, 512)
        sq_b = carve(1024, 2, 512)
        pj = carve(0, TB, ATT_COLS)
        qT1 = carve(4240, 8, SEQ)
        kT1 = carve(6288, 4, SEQ)
        qiT = carve(7312, 4, SEQ)
        kiT = carve(8336, SEQ)
        roped = carve(11152, TB, 2176)
        rope_i = carve(9616, 2, 576)
        rope_q, rope_k = y[:, 0, :].rearrange("p (u n) -> p u n", u=2), y[:, 1, 0:512].rearrange("p (u n) -> p u n", u=2)
        rel = carve(8592, 2, 512)
        score = carve(9616, TB, SEQ)
        left = carve(10128, TB, SEQ)
        keep = carve(10640, TB, SEQ)
        p1 = carve(11152, 3, 512)
        pT1 = carve(12688, 2, 512)
        qk2 = carve(0, TB, AW)
        v2 = carve(3072, TB, AW)
        qT2 = carve(6144, 12, SEQ)
        kT2 = carve(9216, 12, SEQ)
        p2 = carve(0, 3, 768)
        pT2 = [carve(2304, 768), gpost[:, 0:768]]
        sqh = y[:, :, :].rearrange("p b n -> p (b n)").rearrange("p (u m) -> p u m", u=2)
        g_ssd = carve(12288, TB, D)
        dt_tok = carve(14336, TB, SH)
        a_tok = carve(14400, TB, SH)
        sp1 = carve(14464, TB, SH)
        sp2 = carve(14528, TB, SH)
        sp3 = carve(14592, TB, SH)
        hv2 = carve(14656, 16)
        ht2 = carve(14680, 16)
        hr2 = carve(14704, 16)
        zc = carve(0, 2, 2, SEQ)
        zt = carve(1024, 2, 2, SEQ)
        xpad = carve(2048, 2, 260)
        xconv = carve(2568, 2, SEQ)
        xtanh = carve(3080, 2, SEQ)
        xsc = carve(3592, 2, 2, SEQ)
        bcpad = carve(4616, 2, 260)
        bconv = carve(5136, 2, SEQ)
        btanh = carve(5648, 2, SEQ)
        bcc = carve(6160, 2, 2, SEQ)
        Lm = carve(7184, 4, 384)
        Xt = carve(8720, TB, SEQ)
        cbs = carve(9232, 384)
        yz = carve(9616, 2, 2, SEQ)
        sq2 = carve(10640, 2, SEQ)
        gv_ = carve(11152, SEQ)
        gt_ = carve(11408, SEQ)
        gr_ = carve(11664, SEQ)
        yn = carve(14900, 2, SEQ)
        fpad = carve(0, 2, 2, 260)
        fconv = carve(1040, 2, 2, SEQ)
        ftanh = carve(2064, 2, SEQ)
        fhid = carve(2576, 2, SEQ)
        wkf = wk[:, :, :].rearrange("p b n -> p (b n)")
        yf = y[:, :, :].rearrange("p b n -> p (b n)")
        small = sb("small", [P, 2, 4, 4])
        top8 = sb("top8", [P, 8])
        wi_s = sb("wi_s", [P, TB, IH])

        block = ctx.enter_context(nc.Block())

        def kview(w):
            return w.rearrange("(k p) n -> p k n", p=P)

        w1 = [kview(ins["mlp_w1"][l]) for l in range(2)]
        w2 = [kview(ins["mlp_w2"][l]) for l in range(2)]
        sw_in, sw_glu, sw_out = (kview(ins[n][0]) for n in ("ssm_w_in", "ssm_w_glu", "ssm_w_out"))
        aw_in, aw_out = kview(ins["att_w_in"][0]), kview(ins["att_w_out"][0])
        w_in2, w_ssd, w_atp, w_out2, w_up, w_dn = (
            kview(ins[n][0]) for n in ("w_in_2", "w_ssd_proj_2", "w_attn_proj_2", "w_out_2", "w_up_2", "w_down_2"))

        @block.sync
        def _(sp):
            ring = Ring()

            def load(a, b, shape):
                first = ring.n < 2
                s, _, piece = ring.next()
                rows_k, n = shape
                for part, src in zip("ab", (a, b)):
                    if not first:
                        sp.wait_ge(S(f"lo_{part}"), piece - 1)
                    dst = raw[:, s % 2, "ab".index(part), 0:rows_k * n]
                    sp.dma_start(dst.rearrange("p (k n) -> p k n", n=n), src).then_inc(S(f"loaded_{part}{s % 2}"), 16)

            def up(w, c0):
                cs = bass.ds(c0, 256)
                load(w[:, 0:4, cs], w[:, 4:8, cs], (4, 256))

            def chunk4(w, c0):
                for kk in (0, 4):
                    cs = bass.ds(c0, 512)
                    load(w[:, kk:kk + 2, cs], w[:, kk + 2:kk + 4, cs], (2, 512))

            def down(w, k0):
                load(w[:, bass.ds(k0, 1), :], w[:, bass.ds(k0 + 1, 1), :], (1, 1024))

            def narrow(w, c0, n):
                load(w[:, 0:4, c0:c0 + n], w[:, 4:8, c0:c0 + n], (4, n))

            xv = ins["x"][0].rearrange("(b p) n -> b p n", p=P)
            sp.dma_start(h[:, 0, :], xv[0]).then_inc(S("x_in0"), 16)
            sp.dma_start(cst[:, 0:C_FIRST], ins["consts"][:, 0:C_FIRST]).then_inc(S("first_in"), 16)
            sp.dma_start(h[:, 1, :], xv[1]).then_inc(S("x_in1"), 16)
            sp.dma_start(gpre[:, :], ins["norm_g"][0, 0].partition_broadcast(P)).then_inc(S("gpre_in"), 16)
            up(sw_in, 0)
            up(sw_in, 256)
            for dst, src in bc5_loads(ins, braw, craw):
                sp.dma_start(dst, src).then_inc(S("bc5_in"), 16)
            sp.dma_start(cst[:, C_FIRST:], ins["consts"][:, C_FIRST:]).then_inc(S("consts_in"), 16)
            for dst, src in late_loads(ins, rows, pair, alog, dtb):
                sp.dma_start(dst, src).then_inc(S("late_in"), 16)
            sp.dma_start(gpost[:, :], ins["norm_g"][0, 1].partition_broadcast(P)).then_inc(S("gpost_in"), 16)
            load(sw_glu[:, 0:2, :], sw_glu[:, 2:4, :], (2, 512))
            down(sw_out, 0)
            down(sw_out, 2)

            def mlp(layer):
                up(w1[layer], 0)
                with sp.Fori(0, (MC - 2) // 2) as i:
                    ring.enter(i, 1)
                    up(w1[layer], i * 512 + 256)
                    down(w2[layer], i * 4)
                    up(w1[layer], i * 512 + 512)
                    down(w2[layer], i * 4 + 2)
                ring.leave((MC - 2) // 2)
                up(w1[layer], (MC - 1) * 256)
                down(w2[layer], 2 * MC - 4)
                down(w2[layer], 2 * MC - 2)

            mlp(0)
            chunk4(aw_in, QIOFF)
            narrow(aw_in, KIOFF, ATT_TAIL)
            for c in range(3):
                chunk4(aw_in, 512 * c)
            for k in range(0, KD, 2):
                down(aw_out, k)
            mlp(1)
            narrow(w_in2, DTOFF, SH)
            for off in (Q2OFF, V2OFF, K2OFF):
                for c in range(3):
                    chunk4(w_in2, off + 512 * c)
            for c in range(8):
                up(w_in2, GATEOFF + 256 * c)
            down(w_atp, 0)
            down(w_atp, 2)

            def ssd_step(g, with_out):
                up(w_in2, g * 256 + ZOFF)
                up(w_in2, g * 256 + XSOFF)
                load(w_in2[:, :, bass.ds(g * P + BOFF, P)], w_in2[:, :, bass.ds(g * P + COFF, P)], (8, P))
                if with_out:
                    down(w_ssd, g * 2 - 4)

            ssd_step(0, False)
            ssd_step(1, False)
            with sp.Fori(0, 3) as i:
                ring.enter(i, 2)
                ssd_step(i * 2 + 2, True)
                ssd_step(i * 2 + 3, True)
            ring.leave(3)
            down(w_ssd, 12)
            down(w_ssd, 14)
            for k in range(0, KD, 2):
                down(w_out2, k)

            def gate_val(c):
                load(w_up[:, :, bass.ds(c * P, P)], w_up[:, :, bass.ds(c * P + DFF2, P)], (8, P))

            def down1(c):
                load(w_dn[:, bass.ds(c, 1), 0:512], w_dn[:, bass.ds(c, 1), 512:1024], (1, 512))

            gate_val(0)
            with sp.Fori(0, (FC - 2) // 2) as i:
                ring.enter(i, 1)
                gate_val(i * 2 + 1)
                down1(i * 2)
                gate_val(i * 2 + 2)
                down1(i * 2 + 1)
            ring.leave((FC - 2) // 2)
            gate_val(FC - 1)
            down1(FC - 2)
            down1(FC - 1)
            sp.wait_ge(S("out_ready"), 1)
            sp.dma_start(out[0].rearrange("(b p) n -> p b n", p=P), y[:, :, :]).then_inc(S("out_stored"), 16)
            sp.wait_ge(S("out_stored"), 16)

        SMALL = {P_ATT + 2: 8 * ATT_TAIL, P_B2: 8 * SH}

        def size(n):
            if n >= P_WOUT2 + 4:
                m = n - P_WOUT2 - 4
                return 1024 if (m in (42, 43) or (m % 2 == 0 and 2 <= m < 42)) else 2048
            return SMALL.get(n, 2048)

        def low_part(eng, tensor_tensor, ring, part, n):
            s, _, piece = ring.next()
            m = n // 2
            cs = slice(0, m) if part == "a" else slice(m, n)
            eng.wait_ge(S(f"hi_{part}"), piece + 1)
            tensor_tensor(LO[:, s, cs], raw[:, s % 2, "ab".index(part), 0:m], HI[:, s, cs].bitcast(F32),
                          ALU.subtract).then_inc(S(f"lo_{part}"), 1)

        def rotate(eng, link, work, x, heads, tb, outs):
            r1, r2 = (work[:, u, 0:heads * HD].rearrange("p (a d) -> p a d", d=HD) for u in range(2))
            eng.tensor_tensor(r1, x, cosT[:, tb, :].unsqueeze(1).to_broadcast([P, heads, HD]), ALU.mult)
            eng.tensor_tensor(r2[:, :, 0:32], x[:, :, 32:64], sinT[:, tb, 0:32].unsqueeze(1).to_broadcast([P, heads, 32]),
                              ALU.mult)
            link(eng.tensor_tensor(r2[:, :, 32:64], x[:, :, 0:32],
                                   sinT[:, tb, 32:64].unsqueeze(1).to_broadcast([P, heads, 32]), ALU.mult))
            for o in outs:
                last = eng.tensor_tensor(o, r1, r2, ALU.add)
            return last

        def heads_of(t, tb, c0, heads):
            return t[:, tb, c0:c0 + heads * HD].rearrange("p (a d) -> p a d", d=HD)

        def doubled(tb, c0, heads):
            v = roped[:, tb, c0:c0 + heads * 2 * HD].rearrange("p (a u d) -> p a u d", u=2, d=HD)
            return [v[:, :, u, :] for u in range(2)]

        def turn_table(eng, link, i0, i1, room, L, end):
            e = e_tab[:, i0:i1]
            if L == 1:
                eng.tensor_copy(e[:, :, 0, 1:2], sm5[:, 5, i0:i1].unsqueeze(2))
                link(eng.tensor_copy(e[:, :, 1, 1:2], sm5[:, 4, i0:i1].unsqueeze(2)))
            while L < end:
                n = min(L, end - L)
                er, ei = e[:, :, 0, 1:1 + n], e[:, :, 1, 1:1 + n]
                ur = e[:, :, 0, L:L + 1].to_broadcast([P, i1 - i0, n])
                ui = e[:, :, 1, L:L + 1].to_broadcast([P, i1 - i0, n])
                nr, ni = e[:, :, 0, L + 1:L + 1 + n], e[:, :, 1, L + 1:L + 1 + n]
                tmp = room[:, 0:(i1 - i0) * n].rearrange("p (i t) -> p i t", i=i1 - i0)
                eng.tensor_tensor(nr, er, ur, ALU.mult)
                eng.tensor_tensor(ni, er, ui, ALU.mult)
                link(eng.tensor_tensor(tmp, ei, ui, ALU.mult))
                link(eng.tensor_tensor(nr, nr, tmp, ALU.subtract))
                link(eng.tensor_tensor(tmp, ei, ur, ALU.mult))
                link(eng.tensor_tensor(ni, ni, tmp, ALU.add))
                L *= 2

        @block.gpsimd
        def _(pool):
            ring = Ring()
            steps = Steps(pool, S("pool_step"))
            G = nc.gpsimd
            nc.gpsimd.memset(ones[:, :], 1.0).then_inc(S("ones_set"), 1)
            steps.link(G.memset(half[:, :], -0.5))

            def row_rstd(e):
                for tb in range(TB):
                    cs = slice(tb, tb + 1)
                    pool.wait_ge(S("ssq_ready"), 2 * (TB * e + tb) + 2)
                    steps.link(G.tensor_tensor(nv[:, cs], ssq[:, tb, 0:1], ssq[:, tb, 1:2], ALU.add))
                    steps.link(G.tensor_scalar(nv[:, cs], nv[:, cs], 1.0 / D, EPS, ALU.mult, ALU.add))
                    G.tensor_tensor(rstd[:, cs], nv[:, cs], half[:, cs], ALU.pow).then_inc(S("rstd_ready"), 1)

            def upto(n):
                while ring.n <= n:
                    low_part(pool, nc.gpsimd.tensor_tensor, ring, "b", size(ring.n))

            def loop(turns, per, first):
                with pool.Fori(0, turns) as i:
                    ring.enter(i, per)
                    for j in range(4 * per):
                        low_part(pool, nc.gpsimd.tensor_tensor, ring, "b", size(first + j))
                ring.leave(turns)

            row_rstd(0)
            pool.wait_ge(S("sin5_ready"), 1)
            turn_table(G, steps.link, E_SPLIT, ST, carve(s5 + 1024 + 5 * P, 3 * P), 1, 64)
            upto(1)
            turn_table(G, steps.link, E_SPLIT, ST, etmp[:, E_SPLIT * P:], 64, SEQ - 1)
            upto(3)
            def turned_sums(i):
                b = i % 2
                pool.wait_ge(S("bu_read"), i + 1)
                G.tensor_tensor(rotA[:, b, 0, :], rotA[:, b, 0, :], rotA[:, b, 1, :], ALU.add).then_inc(S("vr5_ready"), 1)
                G.tensor_tensor(rotB[:, b, 0, :], rotB[:, b, 1, :], rotB[:, b, 0, :], ALU.subtract)\
                    .then_inc(S("vi5_ready"), 1)

            turned_sums(0)
            for i in range(ST):
                b = i % 2
                if i + 1 < ST:
                    turned_sums(i + 1)
                pool.wait_ge(S("z5_ready"), i + 1)
                if i >= 2:
                    pool.wait_ge(S("x5_used"), i - 1)
                G.tensor_tensor(prod_im[:, b, 0, :], zz[:, b, 0, :], e_tab[:, i, 1, :], ALU.mult)
                G.tensor_tensor(prod_im[:, b, 1, :], zz[:, b, 1, :], e_tab[:, i, 0, :], ALU.mult)\
                    .then_inc(S("xi5_ready"), 1)
            upto(6)
            row_rstd(1)
            row_rstd(2)
            upto(8)
            upto(5)
            loop(7, 1, 9)
            upto(P_ATT + 1)
            row_rstd(3)
            row_rstd(4)
            upto(P_ATT + 7)
            for c in range(2):
                pool.wait_ge(S("pj_read"), 3 + c)
                for tb in range(TB):
                    rotate(G, steps.link, rope_q, heads_of(pj, tb, c * 512, 8), 8, tb, [heads_of(roped, tb, c * 512, 8)])\
                        .then_inc(S("q_roped"), 1)
                    pool.wait_ge(S("q_roped"), TB * c + tb + 1)
                upto(P_ATT + 8)
            upto(P_ATT + 14)
            row_rstd(5)
            row_rstd(6)
            upto(P_ATT + 16)
            loop(7, 1, P_ATT + 17)
            upto(P_B2 + 1)
            row_rstd(7)
            row_rstd(8)
            upto(P_SSD + 5)
            with pool.Fori(0, 3) as i:
                ring.enter(i, 2)
                steps.enter(i, 0)
                for j in range(8):
                    low_part(pool, G.tensor_tensor, ring, "b", 2048)
            ring.leave(3)
            upto(P_WOUT2 + 5)
            row_rstd(9)
            upto(P_WOUT2 + 8)
            loop(9, 1, P_WOUT2 + 9)
            upto(P_WOUT2 + 4 + 43)

        @block.tensor
        def _(pe):
            ring = Ring()
            mm = nc.tensor.matmul

            def arrived():
                s, _, piece = ring.next()
                pe.wait_ge(S("lo_a"), piece + 1)
                pe.wait_ge(S("lo_b"), piece + 1)
                return s

            def used(ins):
                ins.then_inc(S("piece_done"), 1)

            def three(o, lh, ll, rh, rl, start, stop, skip=False):
                mm(o, lh, rh, start=start, stop=False, skip_group_check=skip)
                mm(o, lh, rl, start=False, stop=False, skip_group_check=skip)
                return mm(o, ll, rh, start=False, stop=stop, skip_group_check=skip)

            def ch_major(s, bank, paired=False, norm=None):
                for j in range(2):
                    for k in range(KD):
                        w = (j * KD + k) * P if paired else k * 256 + j * P
                        if norm is not None and j == 0:
                            xT_wait(norm, k)
                        last = three(wk[:, bank, j * SEQ:(j + 1) * SEQ], HI[:, s, w:w + P], LO[:, s, w:w + P],
                                     XH[:, k, :], XL[:, k, :], k == 0, k == KD - 1)
                return last

            def tok_major(s, outs, k0, kt, n, start, stop, xh=XH, xl=XL, skip=False):
                for tb in range(TB):
                    for k in range(kt):
                        ts = slice(tb * P, (tb + 1) * P)
                        last = three(outs(tb), xh[:, k0 + k, ts], xl[:, k0 + k, ts], HI[:, s, k * n:(k + 1) * n],
                                     LO[:, s, k * n:(k + 1) * n], start and k == 0, stop and k == kt - 1, skip)
                return last

            def clear_acc():
                for q in range(4):
                    mm(accf[:, q * 512:(q + 1) * 512], zero_bf[:, 0:P], zero_bf[:, :], start=True, stop=False,
                       skip_group_check=True)

            def down(s, tiles, last_group, kt=2):
                for tb in range(TB):
                    ts = slice(tb * P, (tb + 1) * P)
                    for kk in range(kt):
                        xh, xl = tiles(kk)
                        stop = last_group and kk == kt - 1
                        for lhs, w, end in ((xh, HI, False), (xh, LO, False), (xl, HI, stop)):
                            for n in range(2):
                                c = kk * 1024 + n * 512
                                last = mm(acc[:, tb, n * 512:(n + 1) * 512], lhs[:, ts], w[:, s, c:c + 512],
                                          start=False, stop=end, skip_group_check=True)
                    if last_group and tb == 0:
                        last.then_inc(S("acc_first"), 1)
                return last

            def norm_transpose(n):
                for q in range(4):
                    tb, b = q // 2, q % 2
                    pe.wait_ge(S("y_ready"), 4 * n + q + 1)
                    for kk in range(4):
                        k = 4 * b + kk
                        last = nc.tensor.transpose(wk[:, q, kk * P:(kk + 1) * P], y[:, tb, k * P:(k + 1) * P], ident)
                    last.then_inc(S("xT_psum"), 1)

            def xT_wait(n, k):
                if k % 4 == 0:
                    pe.wait_ge(S("xT_lo"), 4 * n + 3 + k // 4)

            def by_halves(o, row):
                for q in range(2):
                    last = mm(o, cst[0:1, C_SEL + q * P:C_SEL + (q + 1) * P], row[:, q::2], start=(q == 0), stop=(q == 1))
                return last

            pe.wait_ge(S("first_in"), 16)
            pe.wait_ge(S("s5_in"), 16 * N_S5)
            nc.tensor.transpose(accf[:, 0:ROWS[0]], rows[0:ROWS[0], 0, :], ident[0:ROWS[0], 0:ROWS[0]])
            by_halves(accf[:, P:P + 16], pair[0:1, 0:32]).then_inc(S("cols_psum"), 1)
            norm_transpose(0)
            for b in range(2):
                s = arrived()
                last = ch_major(s, b, norm=0 if b == 0 else None)
                used(last)
            pe.wait_ge(S("cpad_ready"), 1)
            for r in range(2):
                for q in range(4):
                    last = nc.tensor.transpose(accf[:, 512 + r * 512 + q * P:512 + r * 512 + (q + 1) * P],
                                               cpad[:, r, q, :], ident)
            last.then_inc(S("ct_psum"), 1)
            pe.wait_ge(S("late_in"), 16 * N_LATE)
            by_halves(accf[:, P + 16:P + 32], pair[0:1, 32:64])
            for r, n in enumerate(ROWS[1:]):
                last = nc.tensor.transpose(accf[:, 1536 + r * P:1536 + r * P + n], rows[0:n, 1 + r, :], ident[0:n, 0:n])
            last.then_inc(S("cols_psum"), 1)
            pe.wait_ge(S("bpad_ready"), 1)
            pe.wait_ge(S("u_ready"), 2)
            for r in range(2):
                for q in range(4):
                    last = nc.tensor.transpose(wk[:, 2 + r, q * P:(q + 1) * P],
                                               bpad[:, r, 4 * q:4 * q + 4, :].rearrange("p a b -> p (a b)"), ident)
            last.then_inc(S("bt_psum"), 1)
            pe.wait_ge(S("bt_ready"), 1)
            pe.wait_ge(S("ct_ready"), 1)
            pe.wait_ge(S("cols_ready"), 2)

            def drive(i):
                q, j = i // 4, i % 4
                js = slice(32 * j, 32 * j + 32)
                if i >= 4:
                    pe.wait_ge(S("bu_read"), i - 3)
                for r in range(2):
                    last = mm(wk[:, i % 4, r * SEQ:(r + 1) * SEQ], bt5[js, r, q, :], uT[js, q, :],
                              start=True, stop=True)
                last.then_inc(S("bu_psum"), 1)

            def glu(s, k):
                pe.wait_ge(S("z_lo"), k + 1)
                for b in range(2):
                    for j in range(2):
                        w = k * 512 + (2 * b + j) * P
                        last = three(wk[:, b, j * SEQ:(j + 1) * SEQ], HI[:, s, w:w + P], LO[:, s, w:w + P],
                                     XH[:, k, :], XL[:, k, :], False, k == 3, True)
                    if k == 3 and b == 0:
                        last.then_inc(S("glu_psum"), 1)
                return last

            for i in range(4):
                drive(i)
            for i in range(ST):
                q, j = i // 4, i % 4
                js = slice(32 * j, 32 * j + 32)
                pe.wait_ge(S("xr5_ready"), i + 1)
                pe.wait_ge(S("xi5_ready"), i + 1)
                b = i % 2
                for n, (c, x) in enumerate(((ct5[:, 0, q, js], prod_re[:, b, 0, :]), (ct5n[:, q, js], prod_re[:, b, 1, :]),
                                            (ct5[:, 1, q, js], prod_im[:, b, 0, :]), (ct5[:, 1, q, js], prod_im[:, b, 1, :]))):
                    last = mm(accf[js, q * 512:q * 512 + SEQ], c, x, start=(n == 0), stop=(n == 3))
                last.then_inc(S("x5_used"), 1)
                if i + 4 < ST:
                    drive(i + 4)
                if i == 13:
                    glu_slot = arrived()
                    pe.wait_ge(S("bu_read"), 14)
                    for b in range(2):
                        mm(wk[:, b, :], zero_bf[:, 0:P], zero_bf[:, :], start=True, stop=False, skip_group_check=True)
                if i >= 13:
                    last = glu(glu_slot, i - 13)
            last = glu(glu_slot, 3)
            used(last)
            pe.wait_ge(S("z2_lo"), 2)
            clear_acc()
            for p in range(2):
                s = arrived()
                used(down(s, lambda kk: (XH[:, 4 + 2 * p + kk, :], XL[:, 4 + 2 * p + kk, :]), p == 1))

            def mlp(layer):
                norm_transpose(1 + 2 * layer)
                base = layer * MC

                def mlp_up(c, par):
                    if not (isinstance(c, int) and c + base < 2):
                        pe.wait_ge(S("hid_read"), c + base - 1)
                    s = arrived()
                    used(ch_major(s, par, norm=1 + 2 * layer if isinstance(c, int) and c == 0 else None))

                def mlp_down(c, par, end=False):
                    pe.wait_ge(S("hid_lo"), c + base + 1)
                    s = arrived()
                    used(down(s, lambda kk: (HH[:, par, kk, :], HL[:, par, kk, :]), end))

                def turn(c):
                    mlp_up(c + 1, 1)
                    mlp_down(c, 0)
                    mlp_up(c + 2, 0)
                    mlp_down(c + 1, 1)

                mlp_up(0, 0)
                clear_acc()
                turn(0)
                with pe.Fori(0, MC // 2 - 2) as i:
                    ring.enter(i, 1)
                    turn(i * 2 + 2)
                ring.leave(MC // 2 - 2)
                mlp_up(MC - 1, 1)
                mlp_down(MC - 2, 0)
                mlp_down(MC - 1, 1, True)

            mlp(0)

            norm_transpose(2)
            for k in (0, 4):
                xT_wait(2, k)
            def proj1(e, part):
                if e >= 2 and part == 0:
                    pe.wait_ge(S("pj_read"), e - 1)
                s = arrived()
                used(tok_major(s, lambda tb: wk[:, 2 * (e % 2) + tb, :], 4 * part, 4, 512, part == 0, part == 1))

            def tile_transpose(n, blocks):
                if n >= 2:
                    pe.wait_ge(S("qkT_read"), n - 1)
                for b, (tb, c) in enumerate(blocks):
                    last = nc.tensor.transpose(accf[:, (n % 2) * 512 + b * P:(n % 2) * 512 + (b + 1) * P],
                                               roped[:, tb, c:c + P], ident)
                last.then_inc(S("qkT_psum"), 1)

            def row4(tb, c):
                return [(tb, c + b * P) for b in range(4)]

            def index(job):
                tb, h0, nh = IJOBS[job]
                if job >= 2:
                    pe.wait_ge(S("rel_read"), job - 1)
                K = P * (tb + 1)
                for b in range(nh):
                    hd = h0 + 2 * b
                    hs = slice(64 * (hd % 2), 64 * (hd % 2) + 64)
                    o = 1024 + (job % 2) * 512 + b * K
                    last = mm(accf[:, o:o + K], qiT[hs, hd // 2, tb * P:(tb + 1) * P], kiT[hs, 0:K], start=True, stop=True)
                last.then_inc(S("rel_psum"), 1)

            proj1(0, 0)
            proj1(0, 1)
            s = arrived()
            used(tok_major(s, lambda tb: wk[:, 2 + tb, 0:ATT_TAIL], 0, KD, ATT_TAIL, True, True))
            proj1(2, 0)
            pe.wait_ge(S("i_roped"), 2)
            tile_transpose(0, row4(0, 1536))
            tile_transpose(1, row4(1, 1536))
            tile_transpose(2, [(0, 2048), (1, 2048)])
            proj1(2, 1)
            pe.wait_ge(S("qkT_read"), 3)
            index(0)
            index(1)
            proj1(3, 0)
            index(2)
            index(3)
            proj1(3, 1)
            index(4)
            index(5)
            pe.wait_ge(S("q_roped"), 2)
            tile_transpose(3, row4(0, 0))
            tile_transpose(4, row4(1, 0))
            proj1(4, 0)
            proj1(4, 1)
            pe.wait_ge(S("q_roped"), 4)
            tile_transpose(5, row4(0, 512))
            tile_transpose(6, row4(1, 512))
            pe.wait_ge(S("k_roped"), 2)
            tile_transpose(7, row4(0, 1024))
            tile_transpose(8, row4(1, 1024))
            pe.wait_ge(S("qkT_read"), 9)

            def scores1(n):
                tb, h0, nh = JOBS1[n]
                K = P * (tb + 1)
                if n >= 4:
                    pe.wait_ge(S("s1_read"), n - 3)
                for b in range(nh):
                    hd = h0 + 2 * b
                    hs = slice(64 * (hd % 2), 64 * (hd % 2) + 64)
                    last = mm(wk[:, n % 4, b * K:(b + 1) * K], qT1[hs, hd // 2, tb * P:(tb + 1) * P],
                              kT1[hs, hd // 4, 0:K], start=True, stop=True)
                last.then_inc(S("s1_psum"), 1)

            def transposed1(n):
                pe.wait_ge(S("p1_ready"), n + 1)
                if n >= 2:
                    pe.wait_ge(S("pT1_ready"), n - 1)
                for b in range(4):
                    last = nc.tensor.transpose(accf[:, (n % 2) * 512 + b * P:(n % 2) * 512 + (b + 1) * P],
                                               p1[:, n % 3, b * P:(b + 1) * P], ident)
                last.then_inc(S("pT1_psum"), 1)

            def weighted1(n):
                tb, h0, nh = JOBS1[n]
                pe.wait_ge(S("pT1_ready"), n + 1)
                if n >= 2:
                    pe.wait_ge(S("o1_lo"), n - 1)
                for b in range(nh):
                    hd = h0 + 2 * b
                    o = 1024 + (n % 2) * 512 + b * P
                    for kb in range(tb + 1):
                        last = mm(accf[64 * (hd % 2):64 * (hd % 2) + 64, o:o + P],
                                  pj[:, kb, VOFF + (hd // 4) * 64:VOFF + (hd // 4) * 64 + 64],
                                  pT1[:, n % 2, (b * (tb + 1) + kb) * P:(b * (tb + 1) + kb + 1) * P],
                                  start=(kb == 0), stop=(kb == tb))
                last.then_inc(S("o1_psum"), 1)

            N1 = len(JOBS1)
            scores1(0)
            scores1(1)
            for n in range(N1 + 1):
                if n + 2 < N1:
                    scores1(n + 2)
                if n < N1:
                    transposed1(n)
                if n >= 1:
                    weighted1(n - 1)
            pe.wait_ge(S("o1_lo"), len(JOBS1))
            clear_acc()
            for p in range(4):
                s = arrived()
                used(down(s, lambda kk: (XH[:, 2 * p + kk, :], XL[:, 2 * p + kk, :]), p == 3))

            mlp(1)

            norm_transpose(4)
            for k in (0, 4):
                xT_wait(4, k)
            s = arrived()
            used(tok_major(s, lambda tb: wk[:, tb, 0:SH], 0, KD, SH, True, True))

            def qk_transpose(c):
                j = c % 6 if c < 3 else c - 3
                pe.wait_ge(S("qk2_normed"), j + 1)
                for tb in range(TB):
                    n = TB * j + tb
                    if n >= 2:
                        pe.wait_ge(S("qkT2_read"), n - 1)
                    for b in range(4):
                        col = (c % 3) * 512 + b * P
                        last = nc.tensor.transpose(accf[:, (n % 2) * 512 + b * P:(n % 2) * 512 + (b + 1) * P],
                                                   qk2[:, tb, col:col + P], ident)
                    last.then_inc(S("qkT2_psum"), 1)

            for c in range(9):
                if c == 0:
                    pe.wait_ge(S("dt_read"), 1)
                elif 5 <= c < 8:
                    pe.wait_ge(S("v2_read"), c - 4)
                elif c >= 2:
                    pe.wait_ge(S("qk2_normed"), c - 1 if c < 5 else c - 4)
                for part in range(2):
                    s = arrived()
                    last = tok_major(s, lambda tb: wk[:, 2 * (c % 2) + tb, :], 4 * part, 4, 512, part == 0, part == 1)
                    used(last)
                if c >= 1 and not 3 <= c - 1 < 6:
                    qk_transpose(c - 1)
            pe.wait_ge(S("a_ready"), 1)
            UU, GT = cst[:, C_UU:C_UU + P], cst[:, C_GT:C_GT + P]
            for n, (lhs, b) in enumerate(((UU, 0), (UU, 1), (GT, 0))):
                last = mm(accf[:, 1024 + n * 32:1024 + (n + 1) * 32], lhs, a_tok[:, b, :], start=True, stop=True)
            last.then_inc(S("cs_psum"), 1)

            gate_slot = [0]

            def gate_half(c, tb):
                if tb == 0:
                    if c >= 1:
                        pe.wait_ge(S("gate_read"), c)
                    gate_slot[0] = arrived()
                s = gate_slot[0]
                for k in range(KD):
                    ts = slice(tb * P, (tb + 1) * P)
                    last = three(accf[:, 1536 + tb * 256:1536 + (tb + 1) * 256], XH[:, k, ts], XL[:, k, ts],
                                 HI[:, s, k * 256:(k + 1) * 256], LO[:, s, k * 256:(k + 1) * 256], k == 0, k == KD - 1)
                if tb == 1:
                    used(last)

            gate_half(0, 0)
            gate_half(0, 1)
            qk_transpose(8)
            pe.wait_ge(S("qkT2_read"), 12)

            def scores2(n):
                hd, tb = JOBS2[n]
                K = P * (tb + 1)
                if n >= 2:
                    pe.wait_ge(S("s2_read"), n - 1)
                hs = slice(64 * (hd % 2), 64 * (hd % 2) + 64)
                for gi in range(3):
                    o = (n % 2) * 1024 + gi * K
                    last = mm(wkf[:, o:o + K], qT2[hs, gi * 4 + hd // 2, tb * P:(tb + 1) * P],
                              kT2[hs, gi * 4 + hd // 2, 0:K], start=True, stop=True)
                last.then_inc(S("s2_psum"), 1)

            def transposed2(n):
                hd, tb = JOBS2[n]
                pe.wait_ge(S("p2_ready"), n + 1)
                if n >= 1:
                    pe.wait_ge(S("pT2_ready"), n)
                for b in range(3 * (tb + 1)):
                    last = nc.tensor.transpose(accf[:, b * P:(b + 1) * P], p2[:, n % 3, b * P:(b + 1) * P], ident)
                last.then_inc(S("pT2_psum"), 1)

            def weighted2(n):
                hd, tb = JOBS2[n]
                nb = 3 * (tb + 1)
                pe.wait_ge(S("pT2_ready"), n + 1)
                if n >= 2 and n % 2 == 0:
                    pe.wait_ge(S("o2_lo"), n // 2)
                elif n == 0:
                    pe.wait_ge(S("cs_read"), 1)
                for b in range(nb):
                    gi, kb = b // (tb + 1), b % (tb + 1)
                    c = gi * 512 + hd * 64
                    last = mm(accf[64 * (hd % 2):64 * (hd % 2) + 64, 1024:1024 + P], v2[:, kb, c:c + 64],
                              pT2[n % 2][:, b * P:(b + 1) * P], start=(b == 0), stop=(b == nb - 1))
                if n % 2:
                    last.then_inc(S("o2_psum"), 1)

            N2 = len(JOBS2)
            scores2(0)
            scores2(1)
            for n in range(N2 + 1):
                if n + 2 < N2:
                    scores2(n + 2)
                if n < N2:
                    transposed2(n)
                if n >= 1:
                    weighted2(n - 1)
                if n < 14:
                    gate_half(1 + n // 2, n % 2)
            pe.wait_ge(S("o2_lo"), 8)
            pe.wait_ge(S("gate_read"), 8)
            clear_acc()
            for p in range(2):
                s = arrived()
                used(down(s, lambda kk: (OH[:, 2 * p + kk, :], OL[:, 2 * p + kk, :]), p == 1))
            pe.wait_ge(S("merged_attn"), 1)
            clear_acc()

            def ssd_step(g, par, proj, ssd, fin, first=False):
                gpv = gp[:, 1 - par, :]

                def decay_rows(m):
                    b = m % 2
                    if m >= 2:
                        pe.wait_ge(S("L_read"), g * 4 - 4 + m - 1)
                    elif not first:
                        if m == 0:
                            pe.wait_ge(S("bc_read"), g)
                        elif not (isinstance(g, int) and g < 2):
                            pe.wait_ge(S("y_read"), g - 1)
                    a0 = gpv[:, G_A + m:G_A + m + 1].to_broadcast([P, P])
                    a1 = gpv[:, G_A + 4 + m:G_A + 5 + m].to_broadcast([P, P])
                    mm(wk[:, b, 0:P], id_bf[:, :], neg_bf[:, :], start=True, stop=False, skip_group_check=True)
                    mm(wk[:, b, 2 * P:3 * P], id_bf[:, :], neg_bf[:, :], start=False, stop=False, skip_group_check=True)
                    mm(wk[:, b, 0:P], a0, cst[:, C_UU:C_UU + P], start=False, stop=False, skip_group_check=True)
                    mm(wk[:, b, P:3 * P], a1, cst[:, C_UU:C_UU + 2 * P], start=False, stop=True,
                       skip_group_check=True).then_inc(S("L_psum"), 1)

                if proj:
                    if not first:
                        pe.wait_ge(S("xs_read"), g)
                    s = arrived()
                    used(ch_major(s, 2))
                if ssd:
                    pe.wait_ge(S("gp_ready"), g)
                    decay_rows(0)
                    pe.wait_ge(S("xsc_ready"), g)
                    if not first and not (isinstance(g, int) and g < 2):
                        pe.wait_ge(S("CB_read"), g - 1)
                    for j in range(2):
                        for tb in range(TB):
                            o = tb * 256 + j * P
                            last = nc.tensor.transpose(wk[:, 3, o:o + P], xsc[:, 1 - par, j, tb * P:(tb + 1) * P], ident)
                    last.then_inc(S("X_psum"), 1)
                if proj:
                    pe.wait_ge(S("z_read"), g + 1)
                    s = arrived()
                    used(ch_major(s, 2))
                if ssd:
                    decay_rows(1)
                if fin:
                    pe.wait_ge(S("sq_ready"), g - 1)
                    if ssd:
                        pe.wait_ge(S("X_read"), g)
                    else:
                        pe.wait_ge(S("CB_read"), g - 1)
                    for j in range(2):
                        last = mm(wk[:, 3, 0:SEQ], ones[:, :], sq2[:, j, :], start=(j == 0), stop=(j == 1))
                    last.then_inc(S("gn_psum"), 1)
                if ssd:
                    decay_rows(2)
                    decay_rows(3)
                    pe.wait_ge(S("X_read"), g)
                    if fin:
                        pe.wait_ge(S("gn_read"), g - 1)
                    pe.wait_ge(S("bcc_ready"), g)
                    bc = bcc[:, 1 - par, :, :]
                    mm(wk[:, 3, 0:SEQ], bc[:, 0, 0:P], bc[:, 1, :], start=True, stop=True)
                    mm(wk[:, 3, SEQ:SEQ + P], bc[:, 0, P:SEQ], bc[:, 1, P:SEQ], start=True, stop=True)\
                        .then_inc(S("CB_psum"), 1)
                if proj:
                    if ssd:
                        pe.wait_ge(S("L_read"), g * 4 - 1)
                    s = arrived()
                    used(ch_major(s, 0, True))
                if fin:
                    pe.wait_ge(S("Y_lo"), g - 1)
                    s = arrived()
                    end = isinstance(g, int) and g == 9
                    used(down(s, lambda kk: (HH[:, par, kk, :], HL[:, par, kk, :]), end))
                if ssd:
                    for m in range(4):
                        pe.wait_ge(S("M_ready"), g * 4 - 4 + m + 1)
                        if m == 0:
                            pe.wait_ge(S("L_read"), g * 4)
                        ps = slice(64 * (m % 2), 64 * (m % 2) + 64)
                        o = (m // 2) * SEQ
                        mm(wk[ps, 1, o:o + SEQ], Xt[:, 0, m * 64:(m + 1) * 64], Lm[:, m, 0:SEQ],
                           start=True, stop=False, skip_group_check=True)
                        last = mm(wk[ps, 1, o + P:o + SEQ], Xt[:, 1, m * 64:(m + 1) * 64], Lm[:, m, SEQ:SEQ + P],
                                  start=False, stop=True, skip_group_check=True)
                    last.then_inc(S("y_psum"), 1)

            ssd_step(0, 0, True, False, False, first=True)
            ssd_step(1, 1, True, True, False)
            with pe.Fori(0, 3) as i:
                ring.enter(i, 2)
                ssd_step(i * 2 + 2, 0, True, True, True)
                ssd_step(i * 2 + 3, 1, True, True, True)
            ring.leave(3)
            ssd_step(8, 0, False, True, True)
            ssd_step(9, 1, False, False, True)
            pe.wait_ge(S("merged"), 1)
            for b in range(4):
                for kk in range(2):
                    for tb in range(TB):
                        k = 2 * b + kk
                        last = nc.tensor.transpose(wk[:, b, kk * SEQ + tb * P:kk * SEQ + (tb + 1) * P],
                                                   y[:, tb, k * P:(k + 1) * P], ident)
                last.then_inc(S("mT_psum"), 1)
            clear_acc()
            pe.wait_ge(S("mT_lo"), 4)
            for p in range(4):
                s = arrived()
                used(down(s, lambda kk: (XH[:, 2 * p + kk, :], XL[:, 2 * p + kk, :]), p == 3))

            norm_transpose(5)

            def ffn_up(c, par):
                if not (isinstance(c, int) and c < 2):
                    pe.wait_ge(S("gv_read"), c - 1)
                s = arrived()
                used(ch_major(s, par, True, norm=5 if isinstance(c, int) and c == 0 else None))

            def ffn_down(c, par, end=False):
                pe.wait_ge(S("f_lo"), c + 1)
                s = arrived()
                used(down(s, lambda kk: (HH[:, par, kk, :], HL[:, par, kk, :]), end, kt=1))

            def ffn_turn(c):
                ffn_up(c + 1, 1)
                ffn_down(c, 0)
                ffn_up(c + 2, 0)
                ffn_down(c + 1, 1)

            ffn_up(0, 0)
            clear_acc()
            ffn_turn(0)
            with pe.Fori(0, FC // 2 - 2) as i:
                ring.enter(i, 1)
                ffn_turn(i * 2 + 2)
            ring.leave(FC // 2 - 2)
            ffn_up(FC - 1, 1)
            ffn_down(FC - 2, 0)
            ffn_down(FC - 1, 1, True)

        @block.scalar
        def _(act):
            ring = Ring()
            steps = Steps(act, S("act_step"))
            A = nc.scalar.activation

            for dst, src in s5_loads(ins, rows, pair):
                nc.scalar.dma_start(dst, src).then_inc(S("s5_in"), 16)

            def load_gpre(n):
                src = (ins["norm_g"][0, 0], ins["norm_g"][0, 2], ins["norm_g"][1, 0], ins["norm_g"][1, 2],
                       ins["norm1_g_2"][0], ins["norm2_g_2"][0])[n]
                nc.scalar.dma_start(gpre[:, :], src.partition_broadcast(P)).then_inc(S("gpre_in"), 16)

            def load_gpost(j):
                nc.scalar.dma_start(gpost[:, :], ins["norm_g"][j // 2, 2 * (j % 2) + 1].partition_broadcast(P))\
                    .then_inc(S("gpost_in"), 16)

            def hi_next():
                m = size(ring.n) // 2
                s, k, n = ring.next()
                if not isinstance(n, int) or n >= 4:
                    act.wait_ge(S("piece_done"), n - 3)
                for j, part in enumerate("ab"):
                    act.wait_ge(S(f"loaded_{part}{s % 2}"), k * 32 + (16 * (s // 2) + 16))
                    A(HI[:, s, j * m:(j + 1) * m], raw[:, s % 2, j, 0:m], ACT.Copy).then_inc(S(f"hi_{part}"), 1)

            def hi_to(n):
                while ring.n <= n:
                    hi_next()

            def done(n):
                act.wait_ge(S("piece_done"), n + 1)

            squares_done = [0]

            def squares(src, tb, n, sem, count):
                act.wait_ge(S(sem), count)
                if squares_done[0] >= 2:
                    act.wait_ge(S("ssq_ready"), squares_done[0] - 1)
                A(squared[:, n, :], halves(src, tb, n), ACT.Square, accum_out=ssq[:, tb, n:n + 1])\
                    .then_inc(S("ssq_ready"), 1)
                squares_done[0] += 1

            def post(n, last_piece):
                for tb, (sem, count) in enumerate((("acc_first", n), ("piece_done", last_piece + 1))):
                    for n in range(2):
                        squares(acc, tb, n, sem, count)

            def pre(j):
                for tb in range(TB):
                    for n in range(2):
                        squares(h, tb, n, "h_ready", 2 * (TB * j + tb) + n + 1)

            def xT_high(n):
                for q in range(4):
                    tb, b = q // 2, q % 2
                    act.wait_ge(S("xT_psum"), 4 * n + q + 1)
                    A(XH[:, 4 * b:4 * b + 4, tb * P:(tb + 1) * P], wk[:, q, :].rearrange("p (k t) -> p k t", k=4),
                      ACT.Copy).then_inc(S("xT_hi"), 1)
                if n + 1 < 6:
                    load_gpre(n + 1)
                if 1 <= n < 4:
                    load_gpost(n)

            for n in range(2):
                squares(h, 0, n, "x_in0", 16)
            act.wait_ge(S("cols_psum"), 1)
            A(cols[:, 0, 0:ROWS[0]], accf[:, 0:ROWS[0]], ACT.Copy)
            A(pairb[:, 0:16], accf[:, P:P + 16], ACT.Copy).then_inc(S("cols_ready"), 1)
            act.wait_ge(S("cols_ready"), 1)
            A(sm5[:, 0, :], pairb[:, 0:16], ACT.Exp).then_inc(S("dt5_ready"), 1)
            for n in range(2):
                squares(h, 1, n, "x_in1", 16)
            act.wait_ge(S("ldt5_ready"), 1)
            A(sm5[:, 1, :], sm5[:, 1, :], ACT.Exp).then_inc(S("mag5_ready"), 1)
            act.wait_ge(S("ang5_ready"), 1)
            A(sm5[:, 4, :], sm5[:, 9, :], ACT.Sin)
            A(sm5[:, 5, :], sm5[:, 6, :], ACT.Sin).then_inc(S("sin5_ready"), 1)
            xT_high(0)
            hi_to(1)
            hi_to(3)
            for b in range(2):
                done(b)
                A(uT[:, 2 * b:2 * b + 2, :], wk[:, b, :].rearrange("p (j t) -> p j t", j=2), ACT.Copy)\
                    .then_inc(S("u_ready"), 1)
            act.wait_ge(S("ct_psum"), 1)
            for r in range(2):
                A(ct5[:, r, :, :], accf[:, 512 + r * 512:1024 + r * 512].rearrange("p (q n) -> p q n", q=4), ACT.Copy)
            A(ct5n[:, :, :], accf[:, 512:1024].rearrange("p (q n) -> p q n", q=4), ACT.Copy, scale=-1.0)\
                .then_inc(S("ct_ready"), 1)
            act.wait_ge(S("cols_psum"), 2)
            A(pairb[:, 16:32], accf[:, P + 16:P + 32], ACT.Copy)
            for r, n in enumerate(ROWS[1:]):
                last = A(cols[:, 1 + r, 0:n], accf[:, 1536 + r * P:1536 + r * P + n], ACT.Copy)
            last.then_inc(S("cols_ready"), 1)
            act.wait_ge(S("bt_psum"), 1)
            for r in range(2):
                last = A(bt5[:, r, :, :], wk[:, 2 + r, :].rearrange("p (q n) -> p q n", q=4), ACT.Copy)
            last.then_inc(S("bt_ready"), 1)
            L = 128
            act.wait_ge(S("turn_low"), 1)
            for i in range(E_SPLIT):
                for r in range(2):
                    last = A(e_tab[:, i, r, L + 1:SEQ], e_tab[:, i, 0, 1:SEQ - L], ACT.Copy, scale=e_tab[:, i, r, L:L + 1])
                last.then_inc(S("turn_prod"), 1)
            act.wait_ge(S("late_in"), 16 * N_LATE)
            A(alog[:, :], alog[:, :], ACT.Exp).then_inc(S("alog_ready"), 1)
            for q in range(4):
                act.wait_ge(S("yv_ready"), q + 1)
                steps.link(A(zf[:, q, :], yv[:, q, :], ACT.Gelu_apprx_tanh))
                A(XH[:, q, :], zf[:, q, :], ACT.Copy).then_inc(S("z_hi"), 1)
                if q in (1, 2):
                    hi_to(3 + q)
            act.wait_ge(S("glu_psum"), 1)
            for b in range(2):
                if b == 1:
                    done(2)
                A(gt5[:, 2 * b:2 * b + 2, :], wk[:, b, :].rearrange("p (j t) -> p j t", j=2), ACT.Tanh, scale=0.5)\
                    .then_inc(S("gt5_ready"), 1)
            for b in range(2):
                act.wait_ge(S("z2_ready"), b + 1)
                A(XH[:, 4 + 2 * b:6 + 2 * b, :], z2f[:, 2 * b:2 * b + 2, :], ACT.Copy, scale=0.5)\
                    .then_inc(S("z2_hi"), 1)
            hi_to(6)

            post(1, 4)

            def mlp(layer, first):
                pre(2 * layer)
                xT_high(1 + 2 * layer)
                base = layer * MC

                def hidden(c, par, piece):
                    done(piece)
                    if not (isinstance(c, int) and c + base < 2):
                        act.wait_ge(S("hid_lo"), c + base - 1)
                    A(relu_b[:, par, :], wk[:, par, :], ACT.Relu).then_inc(S("hid_read"), 1)
                    act.wait_ge(S("hid_read"), c + base + 1)
                    A(HH[:, par, :, :], relu_b[:, par, :].rearrange("p (j t) -> p j t", j=2), ACT.Square)\
                        .then_inc(S("hid_hi"), 1)

                hi_to(first + 3)
                hidden(0, 0, first)
                def turn(c, piece):
                    hi_next()
                    hidden(c + 1, 1, piece)
                    hi_next()
                    hi_next()
                    hidden(c + 2, 0, piece + 2)
                    hi_next()

                turn(0, first + 1)
                with act.Fori(0, MC // 2 - 2) as i:
                    ring.enter(i, 1)
                    turn(i * 2 + 2, i * 4 + (first + 5))
                ring.leave(MC // 2 - 2)
                hi_to(first + 2 * MC)
                hidden(MC - 1, 1, first + 2 * MC - 3)
                hi_to(first + 2 * MC + 1)
                post(2 + 2 * layer, first + 2 * MC - 1)

            mlp(0, 5)

            pre(1)
            xT_high(2)
            def evac1(e, last_piece):
                done(last_piece)
                c0, w = ((QIOFF, 512), (KIOFF, ATT_TAIL), (0, 512), (512, 512), (1024, 512))[e]
                for tb in range(TB):
                    last = A(pj[:, tb, c0:c0 + w], wk[:, 2 * (e % 2) + tb, 0:w], ACT.Copy)
                last.then_inc(S("pj_read"), 1)

            def tile_evac(n, dst):
                act.wait_ge(S("qkT_psum"), n + 1)
                b, t = dst.shape[1], dst.shape[2]
                A(dst, accf[:, (n % 2) * 512:(n % 2) * 512 + b * t].rearrange("p (b t) -> p b t", b=b), ACT.Copy)\
                    .then_inc(S("qkT_read"), 1)

            def index_relu(job):
                act.wait_ge(S("rel_psum"), job + 1)
                if job >= 2:
                    act.wait_ge(S("rel_used"), job - 1)
                A(rel[:, job % 2, :], accf[:, 1024 + (job % 2) * 512:1536 + (job % 2) * 512], ACT.Relu)\
                    .then_inc(S("rel_read"), 1)

            hi_to(P_ATT + 4)
            evac1(0, P_ATT + 1)
            hi_to(P_ATT + 5)
            evac1(1, P_ATT + 2)
            hi_to(P_ATT + 6)
            tile_evac(0, qiT[:, :, 0:P])
            tile_evac(1, qiT[:, :, P:SEQ])
            tile_evac(2, kiT[:, :].rearrange("p (b t) -> p b t", b=TB))
            hi_to(P_ATT + 7)
            evac1(2, P_ATT + 4)
            index_relu(0)
            index_relu(1)
            hi_to(P_ATT + 8)
            index_relu(2)
            index_relu(3)
            hi_to(P_ATT + 9)
            evac1(3, P_ATT + 6)
            index_relu(4)
            index_relu(5)
            tile_evac(3, qT1[:, 0:4, 0:P])
            tile_evac(4, qT1[:, 0:4, P:SEQ])
            hi_to(P_ATT + 10)
            evac1(4, P_ATT + 8)
            tile_evac(5, qT1[:, 4:8, 0:P])
            tile_evac(6, qT1[:, 4:8, P:SEQ])
            tile_evac(7, kT1[:, :, 0:P])
            tile_evac(8, kT1[:, :, P:SEQ])
            hi_to(P_ATT + 12)

            def exps1(n):
                tb, h0, nh = JOBS1[n]
                K = P * (tb + 1)
                act.wait_ge(S("m1_ready"), n + 1)
                for b in range(nh):
                    s = p1[:, n % 3, b * K:(b + 1) * K]
                    last = A(s, s, ACT.Exp, bias=small[:, n % 2, 1, b:b + 1], scale=HD ** -0.5,
                             accum_out=small[:, n % 2, 2, b:b + 1])
                last.then_inc(S("e1_ready"), 1)

            def copies1(n):
                act.wait_ge(S("pT1_psum"), n + 1)
                A(pT1[:, n % 2, :], accf[:, (n % 2) * 512:(n % 2 + 1) * 512], ACT.Copy).then_inc(S("pT1_ready"), 1)

            def o1_high(n):
                tb, h0, nh = JOBS1[n]
                act.wait_ge(S("o1_psum"), n + 1)
                o = 1024 + (n % 2) * 512
                hs = slice(64 * (h0 % 2), 64 * (h0 % 2) + 64)
                A(XH[hs, h0 // 2:h0 // 2 + nh, tb * P:(tb + 1) * P],
                  accf[hs, o:o + nh * P].rearrange("p (a t) -> p a t", t=P), ACT.Copy).then_inc(S("o1_hi"), 1)

            N1 = len(JOBS1)
            exps1(0)
            exps1(1)
            for n in range(N1 + 1):
                if n < N1:
                    copies1(n)
                if n >= 2:
                    o1_high(n - 2)
                if n + 2 < N1:
                    exps1(n + 2)
            o1_high(N1 - 1)
            hi_to(P_ATT + 14)
            post(3, P_ATT + 12)
            mlp(1, P_ATT + 13)

            pre(3)
            xT_high(4)

            def qk_evac(c):
                gcol = pcol(2, R_QG if c < 3 else R_KG)
                dst, t = (qT2 if c < 3 else kT2), c % 3
                for tb in range(TB):
                    n = TB * (c if c < 3 else c - 3) + tb
                    act.wait_ge(S("qkT2_psum"), n + 1)
                    A(dst[:, 4 * t:4 * t + 4, tb * P:(tb + 1) * P],
                      accf[:, (n % 2) * 512:(n % 2 + 1) * 512].rearrange("p (b t) -> p b t", b=4), ACT.Copy,
                      scale=gcol).then_inc(S("qkT2_read"), 1)

            hi_to(P_B2 + 3)
            act.wait_ge(S("sp_arg"), 1)
            A(sp2[:, :, :], sp2[:, :, :], ACT.Exp).then_inc(S("sp_exp"), 1)
            for c in range(9):
                n = P_B2 + 1 + 2 * c + 1
                hi_to(n + 3)
                done(n)
                if 3 <= c < 6:
                    for tb in range(TB):
                        last = A(v2[:, tb, (c - 3) * 512:(c - 2) * 512], wk[:, 2 * (c % 2) + tb, :], ACT.Copy)
                    last.then_inc(S("v2_read"), 1)
                else:
                    j = c if c < 3 else c - 3
                    if j >= 2:
                        act.wait_ge(S("qk2_normed"), j - 1)
                    A(sqh[:, j % 2, :], wk[:, 2 * (c % 2):2 * (c % 2) + 2, :].rearrange("p b n -> p (b n)"), ACT.Square)\
                        .then_inc(S("qk2_sq"), 1)
                if c >= 1 and not 3 <= c - 1 < 6:
                    qk_evac(c - 1)
            act.wait_ge(S("cs_psum"), 1)
            for n in range(3):
                last = A(gpall[:, :, G_NB + 4 * n:G_NB + 4 * n + 4],
                         accf[:, 1024 + n * 32:1024 + (n + 1) * 32].rearrange("p (g m) -> p g m", g=SG),
                         ACT.Copy, scale=(-1.0 if n < 2 else 1.0))
            last.then_inc(S("cs_read"), 1)
            hi_to(P_B2 + 22)

            def exps2(n):
                hd, tb = JOBS2[n]
                act.wait_ge(S("m2_ready"), n + 1)
                s = p2[:, n % 3, 0:3 * P * (tb + 1)]
                A(s, s, ACT.Exp, bias=small[:, n % 2, 1, 0:1], scale=HD ** -0.5,
                  accum_out=small[:, n % 2, 2, 0:1]).then_inc(S("e2_ready"), 1)

            def copies2(n):
                hd, tb = JOBS2[n]
                w = 3 * P * (tb + 1)
                act.wait_ge(S("pT2_psum"), n + 1)
                A(pT2[n % 2][:, 0:w], accf[:, 0:w], ACT.Copy).then_inc(S("pT2_ready"), 1)

            def o2_high(j):
                hd, tb = JOBS2[2 * j + 1]
                act.wait_ge(S("o2_psum"), j + 1)
                A(OH[:, hd // 2, tb * P:(tb + 1) * P], accf[:, 1024:1024 + P], ACT.Copy).then_inc(S("o2_hi"), 1)

            def gate_evac(c):
                done(P_B2 + 19 + c)
                dst = g_ssd if c < 4 else y
                A(dst[:, :, (c % 4) * 256:(c % 4 + 1) * 256],
                  accf[:, 1536:2048].rearrange("p (b n) -> p b n", b=TB), ACT.Tanh, scale=0.5)\
                    .then_inc(S("gate_read"), 1)

            gate_evac(0)
            qk_evac(8)
            N2 = len(JOBS2)
            exps2(0)
            exps2(1)
            for n in range(N2 + 1):
                if n < N2:
                    copies2(n)
                if n + 2 < N2:
                    exps2(n + 2)
                if n >= 1 and n % 2 == 0:
                    o2_high(n // 2 - 1)
                if n < 14 and n % 2 == 0:
                    hi_to(P_B2 + 19 + n // 2 + 4)
                elif n < 14:
                    gate_evac(1 + n // 2)
            hi_to(P_SSD + 1)
            act.wait_ge(S("merged_attn"), 1)
            hi_to(P_SSD + 2)

            def ssd_step(g, par, piece, proj, ssd, fin, splits, first=False):
                gpv = gp[:, 1 - par, :]

                def decays(m):
                    act.wait_ge(S("L_psum"), g * 4 - 4 + m + 1)
                    if not (isinstance(g, int) and g < 2):
                        act.wait_ge(S("y_psum"), g - 1)
                    for blk, c in ((0, 0), (1, 8), (2, 4)):
                        last = A(Lm[:, m, blk * P:(blk + 1) * P], wk[:, m % 2, blk * P:(blk + 1) * P], ACT.Exp,
                                 bias=gpv[:, G_NB + c + m:G_NB + c + m + 1])
                    last.then_inc(S("L_read"), 1)

                if splits != 3:
                    hi_next()
                if proj:
                    done(piece)
                    if not (isinstance(g, int) and g < 2):
                        act.wait_ge(S("yz_ready"), g - 1)
                    A(zc[:, par, :, :], wk[:, 2, :].rearrange("p (j t) -> p j t", j=2), ACT.Copy, scale=0.5)\
                        .then_inc(S("z_read"), 1)
                    act.wait_ge(S("z_read"), g + 1)
                    A(zt[:, par, :, :], zc[:, par, :, :], ACT.Tanh).then_inc(S("zt_ready"), 1)
                if ssd:
                    act.wait_ge(S("bconv_ready"), g)
                    if not (isinstance(g, int) and g < 2):
                        act.wait_ge(S("bcc_ready"), g - 1)
                    A(btanh[:, :, :], bconv[:, :, :], ACT.Tanh).then_inc(S("btanh_ready"), 1)
                if fin:
                    act.wait_ge(S("yz_ready"), g - 1)
                    if not proj:
                        act.wait_ge(S("gn_psum"), g - 2)
                    A(sq2[:, :, :], yz[:, par, :, :], ACT.Square).then_inc(S("sq_ready"), 1)
                if splits >= 3:
                    hi_next()
                if ssd:
                    act.wait_ge(S("gp_ready"), g)
                    decays(0)
                if proj:
                    done(piece + 1)
                    if not first:
                        act.wait_ge(S("xconv_ready"), g)
                    A(xpad[:, :, 3:3 + SEQ], wk[:, 2, :].rearrange("p (j t) -> p j t", j=2), ACT.Copy)\
                        .then_inc(S("xs_read"), 1)
                if ssd:
                    decays(1)
                    decays(2)
                    decays(3)
                if splits >= 3:
                    hi_next()
                if fin:
                    act.wait_ge(S("yn_ready"), g - 1)
                    A(HH[:, par, :, :], yn[:, :, :], ACT.Copy).then_inc(S("Y_hi"), 1)
                if proj:
                    done(piece + 2)
                    if not first:
                        act.wait_ge(S("bconv_ready"), g)
                    A(bcpad[:, :, 3:3 + SEQ], wk[:, 0, :].rearrange("p (j t) -> p j t", j=2), ACT.Copy)\
                        .then_inc(S("bc_read"), 1)
                if splits >= 3:
                    hi_next()
                if proj:
                    act.wait_ge(S("xconv_ready"), g + 1)
                    if not first:
                        act.wait_ge(S("xsc_ready"), g)
                    A(xtanh[:, :, :], xconv[:, :, :], ACT.Tanh).then_inc(S("xtanh_ready"), 1)

            ssd_step(0, 0, P_SSD, True, False, False, 3, first=True)
            ssd_step(1, 1, P_SSD + 3, True, True, False, 3)
            with act.Fori(0, 3) as i:
                ring.enter(i, 2)
                ssd_step(i * 2 + 2, 0, i * 8 + (P_SSD + 6), True, True, True, 4)
                ssd_step(i * 2 + 3, 1, i * 8 + (P_SSD + 10), True, True, True, 4)
            ring.leave(3)
            ssd_step(8, 0, P_SSD + 30, False, True, True, 1)
            ssd_step(9, 1, P_SSD + 31, False, False, True, 1)
            hi_to(P_WOUT2 + 2)
            for b in range(4):
                act.wait_ge(S("mT_psum"), b + 1)
                A(XH[:, 2 * b:2 * b + 2, :], wk[:, b, :].rearrange("p (k t) -> p k t", k=2), ACT.Copy)\
                    .then_inc(S("mT_hi"), 1)
            first = P_WOUT2 + 4
            hi_to(first + 1)
            pre(4)
            xT_high(5)
            hi_to(first + 2)

            def ffn(c, par, piece):
                done(piece)
                if not (isinstance(c, int) and c < 2):
                    act.wait_ge(S("fconv_ready"), c - 1)
                A(fpad[:, par, :, 2:2 + SEQ], wk[:, par, :].rearrange("p (j t) -> p j t", j=2), ACT.Copy)\
                    .then_inc(S("gv_read"), 1)
                act.wait_ge(S("fconv_ready"), c + 1)
                if not (isinstance(c, int) and c < 2):
                    act.wait_ge(S("fh_ready"), c - 1)
                A(ftanh[:, par, :], fconv[:, par, 0, :], ACT.Tanh).then_inc(S("ftanh_ready"), 1)

            def ffn_hi(c, par):
                act.wait_ge(S("fh_ready"), c + 1)
                A(HH[:, par, 0, :], fhid[:, par, :], ACT.Copy).then_inc(S("f_hi"), 1)

            ffn(0, 0, first)
            ffn_hi(0, 0)

            def ffn_turn(c, piece):
                hi_next()
                ffn(c + 1, 1, piece)
                ffn_hi(c + 1, 1)
                hi_next()
                hi_next()
                ffn(c + 2, 0, piece + 2)
                ffn_hi(c + 2, 0)
                hi_next()

            ffn_turn(0, first + 1)
            with act.Fori(0, FC // 2 - 2) as i:
                ring.enter(i, 1)
                ffn_turn(i * 2 + 2, i * 4 + (first + 5))
            ring.leave(FC // 2 - 2)
            hi_to(first + 2 * FC - 1)
            ffn(FC - 1, 1, first + 2 * FC - 3)
            ffn_hi(FC - 1, 1)

        @block.vector
        def _(dve):
            ring = Ring()
            steps = Steps(dve, S("dve_step"))
            link = steps.link
            V = nc.vector
            TT, TS, STT = V.tensor_tensor, V.tensor_scalar, V.scalar_tensor_tensor

            def lo_next():
                low_part(dve, TT, ring, "a", size(ring.n))

            def lo_to(n):
                while ring.n <= n:
                    lo_next()

            def done(n):
                dve.wait_ge(S("piece_done"), n + 1)

            def rsqrt(v, t, r):
                link(TS(r.bitcast(I32), v.bitcast(I32), -0.5, 1597463007.0, ALU.mult, ALU.add))
                for _ in range(3):
                    link(STT(t, r, -0.5, r, ALU.mult, ALU.mult))
                    link(TT(t, t, v, ALU.mult))
                    link(STT(r, t, 1.5, r, ALU.add, ALU.mult))

            def pre(n, e):
                dve.wait_ge(S("gpre_in"), 16 * (n + 1))
                for tb in range(TB):
                    dve.wait_ge(S("rstd_ready"), TB * e + tb + 1)
                    for b in range(2):
                        STT(halves(y, tb, b), halves(h, tb, b), rstd[:, tb:tb + 1], gpre[:, b * 512:(b + 1) * 512],
                            ALU.mult, ALU.mult).then_inc(S("y_ready"), 1)

            def xT_low(n):
                for q in range(4):
                    tb, b = q // 2, q % 2
                    dve.wait_ge(S("xT_hi"), 4 * n + q + 1)
                    ks, ts = slice(4 * b, 4 * b + 4), slice(tb * P, (tb + 1) * P)
                    TT(XL[:, ks, ts], wk[:, q, :].rearrange("p (k t) -> p k t", k=4), XH[:, ks, ts].bitcast(F32),
                       ALU.subtract).then_inc(S("xT_lo"), 1)

            def post(j, e):
                dve.wait_ge(S("gpost_in"), 16 * (j + 1))
                for tb in range(TB):
                    for n in range(2):
                        dve.wait_ge(S("ssq_ready"), 2 * (TB * e + tb) + n + 1)
                        last = TT(halves(y, tb, n), halves(acc, tb, n), gpost[:, n * 512:(n + 1) * 512], ALU.mult)
                    link(last)
                    dve.wait_ge(S("rstd_ready"), TB * e + tb + 1)
                    for n in range(2):
                        STT(halves(h, tb, n), halves(y, tb, n), rstd[:, tb:tb + 1], halves(h, tb, n), ALU.mult, ALU.add)\
                            .then_inc(S("h_ready"), 1)

            V.memset(zero_bf[:, :], 0.0)
            V.memset(bpad[:, :, :, :], 0.0)
            V.memset(e_tab[:, :, 0, 0:1], 1.0)
            V.memset(e_tab[:, :, 1, 0:1], 0.0)
            dve.wait_ge(S("first_in"), 16)
            V.tensor_copy(id_bf[:, :], ident)
            lr, li = cols[:, 0, R_LR:R_LR + 16], cols[:, 0, R_LI:R_LI + 16]
            v5 = [sm5[:, n, :] for n in range(10)]
            dve.wait_ge(S("dt5_ready"), 1)
            TT(v5[1], lr, v5[0], ALU.mult).then_inc(S("ldt5_ready"), 1)
            link(TT(v5[2], li, v5[0], ALU.mult))
            MAGIC = 12582912.0
            link(TS(v5[3], v5[2], 1.0 / (2 * np.pi), MAGIC, ALU.mult, ALU.add))
            link(TS(v5[3], v5[3], MAGIC, None, ALU.subtract))
            link(STT(v5[9], v5[3], -6.28125, v5[2], ALU.mult, ALU.add))
            link(STT(v5[9], v5[3], -0.0019350051879882812, v5[9], ALU.mult, ALU.add))
            link(STT(v5[9], v5[3], -3.0199160501e-07, v5[9], ALU.mult, ALU.add))
            link(TS(v5[9], v5[9], 3.1415925, -3.1415925, ALU.min, ALU.max))
            link(STT(v5[6], v5[9], -1.0, v5[9], ALU.mult, ALU.max))
            TS(v5[6], v5[6], -1.0, float(np.pi / 2), ALU.mult, ALU.add).then_inc(S("ang5_ready"), 1)
            dve.wait_ge(S("sin5_ready"), 1)
            dve.wait_ge(S("mag5_ready"), 1)
            TT(v5[3], v5[1], v5[5], ALU.mult)
            TT(v5[6], v5[1], v5[4], ALU.mult)
            TT(v5[9], lr, lr, ALU.mult)
            link(TT(v5[0], li, li, ALU.mult))
            TS(v5[3], v5[3], 1.0, None, ALU.subtract)
            link(TT(v5[9], v5[9], v5[0], ALU.add))
            link(V.reciprocal(v5[9], v5[9]))
            TT(v5[7], v5[3], lr, ALU.mult)
            link(TT(v5[0], v5[6], li, ALU.mult))
            link(TT(v5[7], v5[7], v5[0], ALU.add))
            TT(v5[7], v5[7], v5[9], ALU.mult)
            TT(v5[8], v5[6], lr, ALU.mult)
            link(TT(v5[0], v5[3], li, ALU.mult))
            link(TT(v5[8], v5[8], v5[0], ALU.subtract))
            link(TT(v5[8], v5[8], v5[9], ALU.mult))
            pre(0, 0)
            xT_low(0)
            lo_to(1)
            dve.wait_ge(S("bc5_in"), 16 * N_BC5)
            fr = v5[7].unsqueeze(2).to_broadcast([P, 16, 16])
            fi = v5[8].unsqueeze(2).to_broadcast([P, 16, 16])
            bt2 = etmp[:, 0:256].rearrange("p (a b) -> p a b", a=16)
            for r in range(2):
                TT(bq[:, :, :], fr, braw[:, r, :, :], ALU.mult)
                link(TT(bt2[:, :, :], fi, braw[:, 1 - r, :, :], ALU.mult))
                for par in range(2):
                    ps = slice(64 * par, 64 * par + 64)
                    last = TT(bpad[ps, r, :, 16 * par:16 * par + 16], bq[ps, :, :], bt2[ps, :, :],
                              ALU.subtract if r == 0 else ALU.add)
                if r == 0:
                    link(last)
            last.then_inc(S("bpad_ready"), 1)
            dve.wait_ge(S("bpad_ready"), 1)
            for r in range(2):
                for par in range(2):
                    last = TS(cpad[:, r, :, 64 * par:64 * par + 64], craw[:, r, :, :],
                              cst[:, C_PAR + 2 * r + par:C_PAR + 2 * r + par + 1], None, ALU.mult)
            last.then_inc(S("cpad_ready"), 1)
            turn_table(V, link, 0, E_SPLIT, etmp, 1, 128)
            L = 128
            TS(v5[9][:, 0:E_SPLIT].unsqueeze(2), e_tab[:, 0:E_SPLIT, 1, L:L + 1], -1.0, None, ALU.mult)\
                .then_inc(S("turn_low"), 1)
            dve.wait_ge(S("turn_low"), 1)
            for i in range(E_SPLIT):
                dve.wait_ge(S("turn_prod"), i + 1)
                for r, f in ((0, v5[9][:, i:i + 1]), (1, e_tab[:, i, 0, L:L + 1])):
                    high = e_tab[:, i, r, L + 1:SEQ]
                    last = STT(high, e_tab[:, i, 1, 1:SEQ - L], f, high, ALU.mult, ALU.add)
            link(last)
            def turned(i):
                dve.wait_ge(S("bu_psum"), i + 1)
                b = i % 2
                bu = wk[:, i % 4, :].rearrange("p (r t) -> p r t", r=2)
                TT(rotA[:, b, :, :], bu, e_tab[:, i, :, :], ALU.mult)
                TT(rotB[:, b, 0, :], bu[:, 0, :], e_tab[:, i, 1, :], ALU.mult)
                TT(rotB[:, b, 1, :], bu[:, 1, :], e_tab[:, i, 0, :], ALU.mult).then_inc(S("bu_read"), 1)

            def scan(i):
                b = i % 2
                dve.wait_ge(S("vr5_ready"), i + 1)
                if i >= 2:
                    dve.wait_ge(S("xi5_ready"), i - 1)
                mag = v5[1][:, i:i + 1].to_broadcast([P, SEQ])
                V.tensor_tensor_scan(zz[:, b, 0, :], mag, rotA[:, b, 0, :], 0.0, ALU.mult, ALU.add)
                dve.wait_ge(S("vi5_ready"), i + 1)
                V.tensor_tensor_scan(zz[:, b, 1, :], mag, rotB[:, b, 0, :], 0.0, ALU.mult, ALU.add)\
                    .then_inc(S("z5_ready"), 1)
                dve.wait_ge(S("z5_ready"), i + 1)
                if i >= 2:
                    dve.wait_ge(S("x5_used"), i - 1)
                TT(prod_re[:, b, :, :], zz[:, b, :, :], e_tab[:, i, :, :], ALU.mult).then_inc(S("xr5_ready"), 1)

            def skip(q):
                dve.wait_ge(S("x5_used"), 4 * q + 4)
                STT(yv[:, q, :], uT[:, q, :], pcol(0, R_D + q), accf[:, q * 512:q * 512 + SEQ],
                    ALU.mult, ALU.add).then_inc(S("yv_ready"), 1)

            def z_low(q):
                dve.wait_ge(S("z_hi"), q + 1)
                TT(XL[:, q, :], zf[:, q, :], XH[:, q, :].bitcast(F32), ALU.subtract).then_inc(S("z_lo"), 1)

            dve.wait_ge(S("cols_ready"), 2)
            turned(0)
            for i in range(ST):
                if i + 1 < ST:
                    if i + 1 == E_SPLIT:
                        dve.wait_ge(S("vi5_ready"), 1)
                    turned(i + 1)
                scan(i)
                if i % 4 == 1 and i > 4:
                    skip(i // 4 - 1)
                if i % 4 == 3 and i > 4:
                    z_low(i // 4 - 1)
                if i == 6 or i == 10:
                    lo_next()
            skip(3)
            z_low(3)
            lo_to(5)
            for b in range(2):
                bs = slice(2 * b, 2 * b + 2)
                dve.wait_ge(S("gt5_ready"), b + 1)
                STT(z2f[:, bs, :], gt5[:, bs, :], 1.0, zf[:, bs, :], ALU.add, ALU.mult).then_inc(S("z2_ready"), 1)
            for b in range(2):
                bs, bo = slice(2 * b, 2 * b + 2), slice(4 + 2 * b, 6 + 2 * b)
                dve.wait_ge(S("z2_hi"), b + 1)
                STT(XL[:, bo, :], z2f[:, bs, :], 0.5, XH[:, bo, :].bitcast(F32), ALU.mult, ALU.subtract)\
                    .then_inc(S("z2_lo"), 1)
            dve.wait_ge(S("consts_in"), 16)
            V.tensor_copy(neg_bf[:, :], cst[:, C_NEGT:C_NEGT + P])
            cw = cols[:, 1, :].rearrange("p (k t) -> p k t", k=4)
            for j in range(2):
                TS(gpall[:, :, G_WX + j:G_WX + 8:2], cw[:, :, j:16:2].rearrange("p k g -> p g k"), 0.5, None, ALU.mult)
                TS(gpall[:, :, G_BX + j], cols[:, 2, R_CB + j:R_CB + 16:2], 0.5, None, ALU.mult)
                V.tensor_copy(gpall[:, :, G_NG + j], cols[:, 2, R_SN + j:R_SN + 16:2])
                V.tensor_copy(gpall[:, :, G_D + j], pairb[:, 16 + j:32:2])
            TS(gpall[:, :, G_WB:G_WB + 4], cw[:, :, 16:24].rearrange("p k g -> p g k"), 0.5, None, ALU.mult)
            TS(gpall[:, :, G_WC:G_WC + 4], cw[:, :, 24:32].rearrange("p k g -> p g k"), 0.5, None, ALU.mult)
            TS(gpall[:, :, G_BB], cols[:, 2, R_CB + 16:R_CB + 24], 0.5, None, ALU.mult)
            TS(gpall[:, :, G_BC], cols[:, 2, R_CB + 24:R_CB + 32], 0.5, None, ALU.mult)
            for j, f in enumerate((0.5, 1.0)):
                for k in range(3):
                    blk, at = (3, k * 44) if k < 2 else (4, 0)
                    TS(fpall[:, :, 4 * j + k], cols[:, blk, at + FC * j:at + FC * (j + 1)], f, None, ALU.mult)
                last = TS(fpall[:, :, 4 * j + 3], cols[:, 2, R_FB + FC * j:R_FB + FC * (j + 1)], f, None, ALU.mult)
            link(last)
            lo_to(6)
            post(0, 1)

            def mlp(layer, first):
                pre(1 + 2 * layer, 2 + 4 * layer)
                xT_low(1 + 2 * layer)
                base = layer * MC

                def hidden(c, par):
                    dve.wait_ge(S("hid_read"), c + base + 1)
                    link(TT(sq_b[:, par, :], relu_b[:, par, :], relu_b[:, par, :], ALU.mult))
                    dve.wait_ge(S("hid_hi"), c + base + 1)
                    TT(HL[:, par, :, :], sq_b[:, par, :].rearrange("p (j t) -> p j t", j=2),
                       HH[:, par, :, :].bitcast(F32), ALU.subtract).then_inc(S("hid_lo"), 1)

                lo_to(first + 3)
                hidden(0, 0)
                with dve.Fori(0, (MC - 2) // 2) as i:
                    ring.enter(i, 1)
                    steps.enter(i, 2)
                    lo_next()
                    hidden(i * 2 + 1, 1)
                    lo_next()
                    lo_next()
                    hidden(i * 2 + 2, 0)
                    lo_next()
                ring.leave((MC - 2) // 2)
                steps.leave((MC - 2) // 2)
                lo_to(first + 2 * MC)
                hidden(MC - 1, 1)
                lo_to(first + 2 * MC + 1)
                post(2 * layer + 1, 3 + 4 * layer)

            mlp(0, 5)

            pre(2, 4)
            xT_low(2)
            lo_to(P_ATT + 4)
            dve.wait_ge(S("pj_read"), 1)
            for tb in range(TB):
                link(rotate(V, link, rope_i, heads_of(pj, tb, QIOFF, IH), IH, tb, [heads_of(roped, tb, 1536, IH)]))
            lo_to(P_ATT + 5)
            dve.wait_ge(S("pj_read"), 2)
            for tb in range(TB):
                rotate(V, link, rope_i, heads_of(pj, tb, KIOFF, 1), 1, tb, doubled(tb, 2048, 1)).then_inc(S("i_roped"), 1)
                dve.wait_ge(S("i_roped"), tb + 1)
            link(TS(wi_s[:, :, :], pj[:, :, WIOFF:WIOFF + IH], (IH ** -0.5) * (HD ** -0.5), None, ALU.mult))
            lo_to(P_ATT + 7)

            def rotate_keys():
                dve.wait_ge(S("pj_read"), 5)
                for tb in range(TB):
                    rotate(V, link, rope_k, heads_of(pj, tb, QW, NKV), NKV, tb, doubled(tb, QW, NKV))\
                        .then_inc(S("k_roped"), 1)
                    dve.wait_ge(S("k_roped"), tb + 1)

            caus = cst[:, C_CAUS:C_CAUS + P]
            for tb in range(TB):
                K = P * (tb + 1)
                sc, lf, kp = score[:, tb, 0:K], left[:, tb, 0:K], keep[:, tb, 0:K]
                for job, (jtb, h0, nh) in enumerate(IJOBS):
                    if jtb != tb:
                        continue
                    dve.wait_ge(S("rel_read"), job + 1)
                    for b in range(nh):
                        hd = h0 + 2 * b
                        r = rel[:, job % 2, b * K:(b + 1) * K]
                        w = wi_s[:, tb, hd:hd + 1]
                        ins_ = TS(sc, r, w, None, ALU.mult) if hd == 0 else STT(sc, r, w, sc, ALU.mult, ALU.add)
                        if b < nh - 1:
                            link(ins_)
                    ins_.then_inc(S("rel_used"), 1)
                    dve.wait_ge(S("rel_used"), job + 1)
                    if job == 3:
                        lo_to(P_ATT + 8)
                link(TT(sc[:, K - P:K], sc[:, K - P:K], caus, ALU.add))
                src = sc
                for turn in range(TOPK // 8):
                    link(V.max(top8[:, :], src))
                    link(V.match_replace(lf, top8[:, :], src, TAKEN))
                    src = lf
                    if tb == 1 and turn == 6:
                        rotate_keys()
                link(TS(kp, lf, -2e38, NEG, ALU.is_gt, ALU.mult))
                link(TT(kp[:, K - P:K], kp[:, K - P:K], caus, ALU.add))
            lo_to(P_ATT + 12)

            def masked1(n):
                tb, h0, nh = JOBS1[n]
                K = P * (tb + 1)
                dve.wait_ge(S("s1_psum"), n + 1)
                if n >= 3:
                    dve.wait_ge(S("pT1_psum"), n - 2)
                s = p1[:, n % 3, :].rearrange("p (a k) -> p a k", a=nh)
                TT(s, wk[:, n % 4, :].rearrange("p (a k) -> p a k", a=nh),
                   keep[:, tb, 0:K].unsqueeze(1).to_broadcast([P, nh, K]), ALU.add).then_inc(S("s1_read"), 1)
                dve.wait_ge(S("s1_read"), n + 1)
                link(V.tensor_reduce(small[:, n % 2, 0, 0:nh], s, AXIS.X, ALU.max))
                TS(small[:, n % 2, 1, 0:nh], small[:, n % 2, 0, 0:nh], -HD ** -0.5, None, ALU.mult)\
                    .then_inc(S("m1_ready"), 1)

            def normed1(n):
                tb, h0, nh = JOBS1[n]
                K = P * (tb + 1)
                dve.wait_ge(S("e1_ready"), n + 1)
                link(V.reciprocal(small[:, n % 2, 3, 0:nh], small[:, n % 2, 2, 0:nh]))
                s = p1[:, n % 3, :].rearrange("p (a k) -> p a k", a=nh)
                TT(s, s, small[:, n % 2, 3, 0:nh].unsqueeze(2).to_broadcast([P, nh, K]), ALU.mult)\
                    .then_inc(S("p1_ready"), 1)

            def o1_low(n):
                tb, h0, nh = JOBS1[n]
                dve.wait_ge(S("o1_hi"), n + 1)
                o = 1024 + (n % 2) * 512
                ts = slice(tb * P, (tb + 1) * P)
                hs = slice(64 * (h0 % 2), 64 * (h0 % 2) + 64)
                TT(XL[hs, h0 // 2:h0 // 2 + nh, ts], accf[hs, o:o + nh * P].rearrange("p (a t) -> p a t", t=P),
                   XH[hs, h0 // 2:h0 // 2 + nh, ts].bitcast(F32), ALU.subtract).then_inc(S("o1_lo"), 1)

            N1 = len(JOBS1)
            masked1(0)
            masked1(1)
            normed1(0)
            for n in range(N1 + 1):
                if n + 2 < N1:
                    masked1(n + 2)
                if n + 1 < N1:
                    normed1(n + 1)
                if n >= 2:
                    o1_low(n - 2)
            o1_low(N1 - 1)
            lo_to(P_ATT + 14)
            post(2, 5)
            mlp(1, P_ATT + 13)

            pre(4, 8)
            xT_low(4)
            lo_to(P_B2 + 3)
            done(P_B2)
            for tb in range(TB):
                last = TT(sp1[:, tb, :], wk[:, tb, 0:SH], dtb[:, :], ALU.add)
            last.then_inc(S("dt_read"), 1)
            dve.wait_ge(S("dt_read"), 1)
            link(STT(sp2[:, :, :], sp1[:, :, :], -1.0, sp1[:, :, :], ALU.mult, ALU.min))
            TS(sp1[:, :, :], sp1[:, :, :], 0.0, None, ALU.max).then_inc(S("sp_arg"), 1)
            dve.wait_ge(S("sp_exp"), 1)
            link(TS(sp3[:, :, :], sp2[:, :, :], 2.0, None, ALU.add))
            link(V.reciprocal(sp3[:, :, :], sp3[:, :, :]))
            link(TT(sp2[:, :, :], sp2[:, :, :], sp3[:, :, :], ALU.mult))
            link(TT(sp3[:, :, :], sp2[:, :, :], sp2[:, :, :], ALU.mult))
            link(TS(dt_tok[:, :, :], sp3[:, :, :], 2.0 / 17, 2.0 / 15, ALU.mult, ALU.add))
            for n in (13, 11, 9, 7, 5, 3, 1):
                link(TT(dt_tok[:, :, :], dt_tok[:, :, :], sp3[:, :, :], ALU.mult))
                link(TS(dt_tok[:, :, :], dt_tok[:, :, :], 2.0 / n, None, ALU.add))
            link(TT(dt_tok[:, :, :], dt_tok[:, :, :], sp2[:, :, :], ALU.mult))
            link(TT(dt_tok[:, :, :], dt_tok[:, :, :], sp1[:, :, :], ALU.add))
            dve.wait_ge(S("alog_ready"), 1)
            for tb in range(TB):
                last = STT(a_tok[:, tb, :], dt_tok[:, tb, :], -1.0, alog[:, :], ALU.mult, ALU.mult)
            last.then_inc(S("a_ready"), 1)
            dve.wait_ge(S("a_ready"), 1)
            for tb in range(TB):
                for at, t in ((G_DT, dt_tok), (G_A, a_tok)):
                    last = V.tensor_copy(gpall[:, :, at + 4 * tb:at + 4 * tb + 4],
                                         t[:, tb, :].rearrange("p (g m) -> p g m", g=SG))
            link(last)

            def head_norm(c):
                j, t = (c if c < 3 else c - 3), c % 3
                dve.wait_ge(S("qk2_sq"), j + 1)
                link(V.tensor_reduce(hv2[:, :], sqh[:, j % 2, :].rearrange("p (a d) -> p a d", d=HD), AXIS.X, ALU.add))
                link(TS(hv2[:, :], hv2[:, :], 1.0 / HD, EPS, ALU.mult, ALU.add))
                rsqrt(hv2[:, :], ht2[:, :], hr2[:, :])
                for tb in range(TB):
                    last = TT(qk2[:, tb, t * 512:(t + 1) * 512].rearrange("p (a d) -> p a d", d=HD),
                              wk[:, 2 * (c % 2) + tb, :].rearrange("p (a d) -> p a d", d=HD),
                              hr2[:, 8 * tb:8 * tb + 8].unsqueeze(2).to_broadcast([P, 8, HD]), ALU.mult)
                last.then_inc(S("qk2_normed"), 1)

            for c in range(9):
                lo_to(P_B2 + 1 + 2 * c + 1 + 3)
                if not 3 <= c < 6:
                    head_norm(c)
            lo_to(P_B2 + 22)

            def masked2(n):
                hd, tb = JOBS2[n]
                K = P * (tb + 1)
                dve.wait_ge(S("s2_psum"), n + 1)
                if n >= 3:
                    dve.wait_ge(S("pT2_psum"), n - 2)
                s = p2[:, n % 3, 0:3 * K]
                o = (n % 2) * 1024
                TT(s.rearrange("p (g k) -> p g k", g=3), wkf[:, o:o + 3 * K].rearrange("p (g k) -> p g k", g=3),
                   dilm[:, :, SEQ - K:SEQ], ALU.add).then_inc(S("s2_read"), 1)
                dve.wait_ge(S("s2_read"), n + 1)
                link(V.tensor_reduce(small[:, n % 2, 0, 0:1], s, AXIS.X, ALU.max))
                TS(small[:, n % 2, 1, 0:1], small[:, n % 2, 0, 0:1], -HD ** -0.5, None, ALU.mult)\
                    .then_inc(S("m2_ready"), 1)

            def normed2(n):
                hd, tb = JOBS2[n]
                dve.wait_ge(S("e2_ready"), n + 1)
                link(V.reciprocal(small[:, n % 2, 3, 0:1], small[:, n % 2, 2, 0:1]))
                s = p2[:, n % 3, 0:3 * P * (tb + 1)]
                TS(s, s, small[:, n % 2, 3, 0:1], None, ALU.mult).then_inc(S("p2_ready"), 1)

            def o2_low(j):
                hd, tb = JOBS2[2 * j + 1]
                ts = slice(tb * P, (tb + 1) * P)
                dve.wait_ge(S("o2_hi"), j + 1)
                TT(OL[:, hd // 2, ts], accf[:, 1024:1024 + P], OH[:, hd // 2, ts].bitcast(F32), ALU.subtract)\
                    .then_inc(S("o2_lo"), 1)

            N2 = len(JOBS2)
            masked2(0)
            masked2(1)
            normed2(0)
            for n in range(N2 + 1):
                if n + 1 < N2:
                    normed2(n + 1)
                if n + 2 < N2:
                    masked2(n + 2)
                if n >= 1 and n % 2 == 0:
                    o2_low(n // 2 - 1)
                if n < 14 and n % 2 == 0:
                    lo_to(P_B2 + 19 + n // 2 + 4)
            lo_to(P_SSD + 1)
            dve.wait_ge(S("gate_read"), 8)
            TS(yf, yf, 0.5, 0.5, ALU.mult, ALU.add)
            link(TS(g_ssd[:, :, :], g_ssd[:, :, :], 0.5, 0.5, ALU.mult, ALU.add))
            done(P_SSD - 1)
            for tb in range(TB):
                last = TT(y[:, tb, :], y[:, tb, :], acc[:, tb, :], ALU.mult)
            V.memset(xpad[:, :, 0:3], 0.0)
            V.memset(bcpad[:, :, 0:3], 0.0).then_inc(S("merged_attn"), 1)
            dve.wait_ge(S("merged_attn"), 1)
            lo_to(P_SSD + 2)

            def conv4(dst, src, w, b):
                link(TS(dst, src[:, 0:SEQ], w[0], b, ALU.mult, ALU.add))
                for k in (1, 2):
                    link(STT(dst, src[:, k:k + SEQ], w[k], dst, ALU.mult, ALU.add))
                return STT(dst, src[:, 3:3 + SEQ], w[3], dst, ALU.mult, ALU.add)

            def ssd_step(g, par, proj, ssd, fin, splits, first=False):
                gpn, gpv = gp[:, par, :], gp[:, 1 - par, :]

                def one(v, at):
                    return v[:, at:at + 1]

                if splits != 3:
                    lo_next()
                if ssd:
                    dve.wait_ge(S("btanh_ready"), g)
                    STT(bcc[:, 1 - par, :, :], btanh[:, :, :], 1.0, bconv[:, :, :], ALU.add, ALU.mult)\
                        .then_inc(S("bcc_ready"), 1)
                    dve.wait_ge(S("X_psum"), g)
                    if not (isinstance(g, int) and g < 2):
                        dve.wait_ge(S("y_psum"), g - 1)
                    for tb in range(TB):
                        last = TT(Xt[:, tb, :].rearrange("p (m d) -> p m d", m=4),
                                  wk[:, 3, tb * SEQ:(tb + 1) * SEQ].rearrange("p (m d) -> p m d", m=4),
                                  gpv[:, G_DT + 4 * tb:G_DT + 4 * tb + 4].unsqueeze(2).to_broadcast([P, 4, HD]), ALU.mult)
                    last.then_inc(S("X_read"), 1)
                if splits >= 3:
                    lo_next()
                if fin:
                    dve.wait_ge(S("gn_psum"), g - 1)
                    TS(gv_[:, :], wk[:, 3, 0:SEQ], 1.0 / 256, EPS, ALU.mult, ALU.add).then_inc(S("gn_read"), 1)
                    dve.wait_ge(S("gn_read"), g - 1)
                    rsqrt(gv_[:, :], gt_[:, :], gr_[:, :])
                    for j in range(2):
                        last = STT(yn[:, j, :], yz[:, par, j, :], one(gpn, G_NG + j), gr_[:, :], ALU.mult, ALU.mult)
                    last.then_inc(S("yn_ready"), 1)
                    dve.wait_ge(S("yn_ready"), g - 1)
                if proj:
                    V.tensor_copy(gpn, gpall[:, bass.ds(g, 1), :].rearrange("p a n -> p (a n)"))\
                        .then_inc(S("gp_ready"), 1)
                    dve.wait_ge(S("gp_ready"), g + 1)
                if fin:
                    dve.wait_ge(S("Y_hi"), g - 1)
                    TT(HL[:, par, :, :], yn[:, :, :], HH[:, par, :, :].bitcast(F32), ALU.subtract)\
                        .then_inc(S("Y_lo"), 1)
                if ssd:
                    dve.wait_ge(S("CB_psum"), g)
                    V.tensor_copy(cbs[:, :], wk[:, 3, 0:384]).then_inc(S("CB_read"), 1)
                    dve.wait_ge(S("CB_read"), g)
                    for m in range(4):
                        dve.wait_ge(S("L_read"), g * 4 - 4 + m + 1)
                        TT(Lm[:, m, :], Lm[:, m, :], cbs[:, :], ALU.mult).then_inc(S("M_ready"), 1)
                if splits >= 3:
                    lo_next()
                if proj:
                    dve.wait_ge(S("xs_read"), g + 1)
                    if not first:
                        dve.wait_ge(S("xtanh_ready"), g)
                    for j in range(2):
                        last = conv4(xconv[:, j, :], xpad[:, j, :], [one(gpn, G_WX + 2 * k + j) for k in range(4)],
                                     one(gpn, G_BX + j))
                        if j == 0:
                            link(last)
                    last.then_inc(S("xconv_ready"), 1)
                if splits >= 3:
                    lo_next()
                if proj:
                    dve.wait_ge(S("xtanh_ready"), g + 1)
                    STT(xsc[:, par, :, :], xtanh[:, :, :], 1.0, xconv[:, :, :], ALU.add, ALU.mult)\
                        .then_inc(S("xsc_ready"), 1)
                if ssd:
                    link(STT(zt[:, 1 - par, :, :], zt[:, 1 - par, :, :], 1.0, zc[:, 1 - par, :, :], ALU.add, ALU.mult))
                    dve.wait_ge(S("y_psum"), g)
                    for j in range(2):
                        last = STT(yz[:, 1 - par, j, :], xsc[:, 1 - par, j, :], one(gpv, G_D + j),
                                   wk[:, 1, j * SEQ:(j + 1) * SEQ], ALU.mult, ALU.add)
                    last.then_inc(S("y_read"), 1)
                    dve.wait_ge(S("y_read"), g)
                    TT(yz[:, 1 - par, :, :], yz[:, 1 - par, :, :], zt[:, 1 - par, :, :], ALU.mult)\
                        .then_inc(S("yz_ready"), 1)
                if proj:
                    dve.wait_ge(S("bc_read"), g + 1)
                    dve.wait_ge(S("xsc_ready"), g + 1)
                    for j, (w, b) in enumerate(((G_WB, G_BB), (G_WC, G_BC))):
                        last = conv4(bconv[:, j, :], bcpad[:, j, :], [one(gpn, w + k) for k in range(4)], one(gpn, b))
                        if j == 0:
                            link(last)
                    last.then_inc(S("bconv_ready"), 1)

            ssd_step(0, 0, True, False, False, 3, first=True)
            ssd_step(1, 1, True, True, False, 3)
            with dve.Fori(0, 3) as i:
                ring.enter(i, 2)
                steps.enter(i, 2 * (10 + 2 * 7 + 1))
                ssd_step(i * 2 + 2, 0, True, True, True, 4)
                ssd_step(i * 2 + 3, 1, True, True, True, 4)
            ring.leave(3)
            steps.leave(3)
            ssd_step(8, 0, False, True, True, 1)
            ssd_step(9, 1, False, False, True, 1)
            done(P_WOUT2 - 1)
            for tb in range(TB):
                link(TT(g_ssd[:, tb, :], g_ssd[:, tb, :], acc[:, tb, :], ALU.mult))
                last = TT(y[:, tb, :], y[:, tb, :], g_ssd[:, tb, :], ALU.add)
            last.then_inc(S("merged"), 1)
            lo_to(P_WOUT2 + 2)
            for b in range(4):
                dve.wait_ge(S("mT_hi"), b + 1)
                TT(XL[:, 2 * b:2 * b + 2, :], wk[:, b, :].rearrange("p (k t) -> p k t", k=2),
                   XH[:, 2 * b:2 * b + 2, :].bitcast(F32), ALU.subtract).then_inc(S("mT_lo"), 1)
            first = P_WOUT2 + 4
            lo_to(first + 1)
            link(V.memset(fpad[:, :, :, 0:2], 0.0))
            for tb in range(TB):
                if tb == 0:
                    dve.wait_ge(S("acc_first"), 7)
                else:
                    done(first - 1)
                for n in range(2):
                    TT(halves(h, tb, n), halves(h, tb, n), halves(acc, tb, n), ALU.add).then_inc(S("h_ready"), 1)
            pre(5, 9)
            xT_low(5)
            lo_to(first + 2)

            def ffn(c, par):
                V.tensor_copy(fp[:, par, :], fpall[:, bass.ds(c, 1), :].rearrange("p a n -> p (a n)"))\
                    .then_inc(S("fp_ready"), 1)
                dve.wait_ge(S("fp_ready"), c + 1)
                dve.wait_ge(S("gv_read"), c + 1)
                for j in range(2):
                    o, s, w = fconv[:, par, j, :], fpad[:, par, j, :], [fp[:, par, 4 * j + k:4 * j + k + 1] for k in range(4)]
                    link(TS(o, s[:, 0:SEQ], w[0], w[3], ALU.mult, ALU.add))
                    link(STT(o, s[:, 1:1 + SEQ], w[1], o, ALU.mult, ALU.add))
                    last = STT(o, s[:, 2:2 + SEQ], w[2], o, ALU.mult, ALU.add)
                    if j == 0:
                        link(last)
                last.then_inc(S("fconv_ready"), 1)
                dve.wait_ge(S("ftanh_ready"), c + 1)
                link(STT(fhid[:, par, :], ftanh[:, par, :], 1.0, fconv[:, par, 0, :], ALU.add, ALU.mult))
                TT(fhid[:, par, :], fhid[:, par, :], fconv[:, par, 1, :], ALU.mult).then_inc(S("fh_ready"), 1)
                dve.wait_ge(S("f_hi"), c + 1)
                TT(HL[:, par, 0, :], fhid[:, par, :], HH[:, par, 0, :].bitcast(F32), ALU.subtract)\
                    .then_inc(S("f_lo"), 1)

            ffn(0, 0)
            with dve.Fori(0, (FC - 2) // 2) as i:
                ring.enter(i, 1)
                steps.enter(i, 12)
                lo_next()
                ffn(i * 2 + 1, 1)
                lo_next()
                lo_next()
                ffn(i * 2 + 2, 0)
                lo_next()
            ring.leave((FC - 2) // 2)
            steps.leave((FC - 2) // 2)
            lo_to(first + 2 * FC - 1)
            ffn(FC - 1, 1)
            done(first + 2 * FC - 1)
            for tb in range(TB):
                last = TT(y[:, tb, :], h[:, tb, :], acc[:, tb, :], ALU.add)
            last.then_inc(S("out_ready"), 1)


def r128(ap):
    return ap.rearrange("(r c) -> r c", c=P)


def s5_loads(ins, rows, pair):
    return [
        (rows[R_LR:R_LR + 16, 0, :], ins["ssm_lam_re"][0].rearrange("(i q) s -> i (q s)", q=2)),
        (rows[R_LI:R_LI + 16, 0, :], ins["ssm_lam_im"][0].rearrange("(i q) s -> i (q s)", q=2)),
        (rows[R_D:R_D + 4, 0, :], ins["ssm_d"][0].rearrange("(q a) c -> q (a c)", q=4)),
        (pair[:, 0:32], ins["ssm_log_dt"]),
    ]


def bc5_loads(ins, braw, craw):
    loads = []
    for r, (b, c) in enumerate((("ssm_b_re", "ssm_c_re"), ("ssm_b_im", "ssm_c_im"))):
        loads.append((braw[:, r, :, :], ins[b][0].rearrange("(i q) s c -> (q s) i c", q=2)))
        loads.append((craw[:, r, :, :], ins[c][0].rearrange("(t a) c s -> (a c) t s", t=4)))
    return loads


def late_loads(ins, rows, pair, alog, dtb):
    loads = [
        (rows[R_SN:R_SN + 16, 2, :], r128(ins["ssd_norm_g_2"][0])),
        (rows[0:128, 1, :], ins["ssd_conv_w_2"][0].rearrange("k (t c) -> (k t) c", c=P)),
        (rows[R_CB:R_CB + 32, 2, :], r128(ins["ssd_conv_b_2"][0])),
        (rows[R_FB:R_FB + 44, 2, :], r128(ins["ffn_conv_b_2"][0])),
        (rows[0:88, 3, :], ins["ffn_conv_w_2"][0, 0:2].rearrange("k (t c) -> (k t) c", c=P)),
        (rows[0:44, 4, :], r128(ins["ffn_conv_w_2"][0, 2])),
        (pair[:, 32:64], ins["d_skip_2"]),
        (alog[:, :], ins["a_log_2"][0].partition_broadcast(P)),
        (dtb[:, :], ins["dt_bias_2"][0].partition_broadcast(P)),
    ]
    for at, name in ((R_QG, "q_norm_g_2"), (R_KG, "k_norm_g_2")):
        for part in range(2):
            loads.append((rows[at:at + 1, 2, 64 * part:64 * part + 64], ins[name]))
    return loads


def constants():
    c = np.zeros((P, C_END), np.float32)
    i, j = np.arange(P)[:, None], np.arange(P)[None, :]
    c[:, C_ID:C_ID + P] = i == j
    c[:, C_UU:C_UU + 2 * P] = np.tile(i <= j, 2)
    c[:, C_GT:C_GT + P] = i > j
    c[:, C_NEGT:C_NEGT + P] = np.where(j < i, NEG, 0)
    c[:, C_CAUS:C_CAUS + P] = np.where(j > i, NEG, 0)
    for g, (window, dil) in enumerate(((128, 1), (512, 4), (2048, 16))):
        dist = np.concatenate([P + i - j, i - j], axis=1)
        ok = (dist >= 0) & (dist <= window) & (dist % dil == 0)
        c[:, C_DIL + g * SEQ:C_DIL + (g + 1) * SEQ] = np.where(ok, 0, NEG)
    half = HD // 2
    freq = np.float32(10000.0) ** (-np.arange(half, dtype=np.float32) * np.float32(2.0) / np.float32(HD))
    ang = (np.arange(SEQ, dtype=np.float32)[:, None] * freq[None, :].astype(np.float32)).astype(np.float32)
    cos, sin = np.cos(ang), np.sin(ang)
    for b in range(TB):
        ts = slice(b * P, (b + 1) * P)
        c[:, C_COS + b * HD:C_COS + (b + 1) * HD] = np.concatenate([cos[ts], cos[ts]], axis=1)
        c[:, C_SIN + b * HD:C_SIN + (b + 1) * HD] = np.concatenate([-sin[ts], sin[ts]], axis=1)
    c[0, C_SEL:C_SEL + 64] = 1
    c[0, C_SEL + P + 64:C_SEL + 2 * P] = 1
    odd = (np.arange(P) // CH) % 2
    c[:, C_PAR], c[:, C_PAR + 1], c[:, C_PAR + 2], c[:, C_PAR + 3] = 1 - odd, odd, odd - 1, -odd
    return c


_INS = ["x", "norm_g", "mlp_w1", "mlp_w2", "ssm_w_in", "ssm_lam_re", "ssm_lam_im", "ssm_log_dt", "ssm_b_re",
        "ssm_b_im", "ssm_c_re", "ssm_c_im", "ssm_d", "ssm_w_glu", "ssm_w_out", "att_w_in", "att_w_out", "norm1_g_2",
        "w_in_2", "ssd_conv_w_2", "ssd_conv_b_2", "dt_bias_2", "a_log_2", "d_skip_2", "ssd_norm_g_2",
        "w_ssd_proj_2", "q_norm_g_2", "k_norm_g_2", "w_attn_proj_2", "w_out_2", "norm2_g_2", "w_up_2",
        "ffn_conv_w_2", "ffn_conv_b_2", "w_down_2"]


def kernel(**inputs):
    import concourse.bacc as bacc
    from concourse.bass_utils import run_bass_kernel_spmd

    nc = bacc.Bacc("TRN2", target_bir_lowering=False, num_devices=1)
    arrays, aps = {}, {}
    for name in _INS:
        a = np.ascontiguousarray(inputs[name])
        arrays[f"in_{name}"] = a
        aps[name] = nc.dram_tensor(f"in_{name}", a.shape, mybir.dt.from_np(a.dtype), kind="ExternalInput").ap()
    arrays["consts"] = constants()
    aps["consts"] = nc.dram_tensor("consts", (P, C_END), F32, kind="ExternalInput").ap()
    out = nc.dram_tensor("out", (1, SEQ, D), F32, kind="ExternalOutput").ap()
    build(nc, aps, out)
    r = run_bass_kernel_spmd(nc, [arrays], core_ids=[0])
    return r.results[0]["out"]
```

```python
import concourse.bass as bass
from concourse import mybir
from contextlib import ExitStack

import numpy as np

F32 = mybir.dt.float32
F32R = mybir.dt.float32r
BF16 = mybir.dt.bfloat16
I32 = mybir.dt.int32
ALU = mybir.AluOpType
ACT = mybir.ActivationFunctionType
AXIS = mybir.AxisListType

P = 128
SEQ = 256
TB = SEQ // P
D = 1024
KD = D // P
EPS = 1e-6
NEG = -1e30
TAKEN = -3e38

GROUPS, CH, STATE = 32, 16, 64
ST = GROUPS * STATE // P
E_SPLIT = 10
DFF = 4 * D
MC = DFF // 256
NH, NKV, HD, IH, TOPK = 16, 4, 64, 8, 64
QW, KW, IW = NH * HD, NKV * HD, IH * HD
VOFF, QIOFF = QW + KW, QW + 2 * KW
KIOFF = QIOFF + IW
WIOFF = KIOFF + HD
ATT_COLS = WIOFF + IH
ATT_TAIL = ATT_COLS - 4 * 512
DIN, SG, SH, DSTATE = 2048, 8, 32, 128
ZOFF, XSOFF = 0, DIN
BOFF = XSOFF + DIN
COFF = BOFF + SG * DSTATE
DTOFF = COFF + SG * DSTATE
AW = 3 * 8 * 64
Q2OFF = DTOFF + SH
K2OFF, V2OFF = Q2OFF + AW, Q2OFF + 2 * AW
GATEOFF = Q2OFF + 3 * AW
DFF2 = 2816
FC = DFF2 // P

C_ID, C_SEL, C_PAR, C_UU, C_GT, C_NEGT, C_CAUS, C_DIL, C_COS, C_SIN = (
    0, 128, 384, 388, 644, 772, 900, 1028, 1796, 1924)
C_END = 2052
C_FIRST = C_UU
R_LR, R_LI, R_D = 0, 16, 32
R_CB, R_FB, R_SN, R_QG, R_KG = 0, 32, 76, 92, 93
ROWS = [36, 128, 94, 88, 44]
JOBS1 = [(0, h0, 4) for h0 in (0, 1, 8, 9)] + [(1, h0, 2) for h0 in (0, 1, 4, 5, 8, 9, 12, 13)]
IJOBS = [(0, h0, 4) for h0 in (0, 1)] + [(1, h0, 2) for h0 in (0, 1, 4, 5)]
JOBS2 = [(2 * pr + hh, tb) for pr in range(4) for tb in range(TB) for hh in range(2)]
G_WX, G_WB, G_WC, G_BX, G_BB, G_BC, G_NG, G_D, G_DT, G_A, G_NB, G_END = 0, 8, 12, 16, 18, 19, 20, 22, 24, 32, 40, 52
N_S5, N_BC5, N_LATE = 4, 4, 13
P_ATT, P_B2, P_SSD, P_WOUT2 = 37, 82, 111, 143


class Ring:

    def __init__(self):
        self.n, self.uses, self.off = 0, [0] * 4, 0

    def next(self):
        s, k, n = self.n % 4, self.uses[self.n % 4] + self.off, self.n + self.off * 4
        self.n += 1
        self.uses[s] += 1
        return s, k, n

    def enter(self, i, per_slot):
        self.off, self.per = i * per_slot, per_slot

    def leave(self, turns):
        self.off = 0
        self.n += 4 * self.per * (turns - 1)
        self.uses = [u + self.per * (turns - 1) for u in self.uses]


class Steps:

    def __init__(self, eng, sem):
        self.eng, self.sem, self.n, self.off = eng, sem, 0, 0

    def link(self, ins):
        ins.then_inc(self.sem, 1)
        self.n += 1
        self.eng.wait_ge(self.sem, self.off + self.n)

    def enter(self, i, per):
        self.off, self.start, self.per = i * per, self.n, per

    def leave(self, turns):
        assert self.n - self.start == self.per, (self.n - self.start, self.per)
        self.n += self.per * (turns - 1)
        self.off = 0


def build(nc, ins, out):
    ctx = ExitStack()
    with ctx:
        def sb(name, shape, dt=F32):
            return ctx.enter_context(nc.sbuf_tensor(name, shape, dt))

        sems = {}

        def S(name):
            if name not in sems:
                sems[name] = ctx.enter_context(nc.semaphore(name))
            return sems[name]

        raw = sb("raw", [P, 2, 2, 1024])
        HI = sb("HI", [P, 4, 2048], F32R)
        LO = sb("LO", [P, 4, 2048], F32R)
        XH = sb("XH", [P, KD, SEQ], F32R)
        XL = sb("XL", [P, KD, SEQ], F32R)
        HH = sb("HH", [P, 2, 2, SEQ], F32R)
        HL = sb("HL", [P, 2, 2, SEQ], F32R)
        OH = HH[:, :, :, :].rearrange("p a b t -> p (a b) t")
        OL = HL[:, :, :, :].rearrange("p a b t -> p (a b) t")
        cst = sb("cst", [P, C_END])
        cols = sb("cols", [P, 5, P])
        gpall = sb("gpall", [P, SG, G_END])
        gp = sb("gp", [P, 2, G_END])
        fpall = sb("fpall", [P, FC, 8])
        fp = sb("fp", [P, 2, 8])
        h = sb("h", [P, TB, D])
        y = sb("y", [P, TB, D])
        gpost = sb("gpost", [P, D])
        gpre = sb("gpre", [P, D])
        half = sb("half", [P, 2])
        ct5n = sb("ct5n", [P, 4, P])
        zero_bf = sb("zero_bf", [P, 512], BF16)
        id_bf = sb("id_bf", [P, P], BF16)
        neg_bf = sb("neg_bf", [P, P], BF16)
        ones = sb("ones", [P, P])
        ssq = sb("ssq", [P, TB, 2])
        nv = sb("nv", [P, 2])
        rstd = sb("rstd", [P, 2])
        arena = sb("arena", [P, 15520])
        acc = ctx.enter_context(nc.psum_tensor("acc", [P, TB, D], F32))
        wk = ctx.enter_context(nc.psum_tensor("wk", [P, 4, 512], F32))
        accf = acc[:, :, :].rearrange("p a n -> p (a n)")

        def carve(at, *shape):
            n = int(np.prod(shape))
            v = arena[:, at:at + n]
            if len(shape) == 2:
                return v.rearrange("p (a b) -> p a b", a=shape[0])
            if len(shape) == 3:
                return v.rearrange("p (a b c) -> p a b c", a=shape[0], b=shape[1])
            return v

        ident = cst[:, C_ID:C_ID + P]
        cosT = cst[:, C_COS:C_COS + 128].rearrange("p (b d) -> p b d", b=TB)
        sinT = cst[:, C_SIN:C_SIN + 128].rearrange("p (b d) -> p b d", b=TB)
        dilm = cst[:, C_DIL:C_DIL + 768].rearrange("p (g n) -> p g n", g=3)

        def pcol(block, r):
            return cols[:, block, r:r + 1]

        def halves(t, tb, n):
            return t[:, tb, n * 512:(n + 1) * 512]

        etmp = y[:, :, :].rearrange("p b n -> p (b n)")
        e_tab = carve(0, ST, 2, SEQ)
        s5 = 8192
        uT = carve(s5, 4, SEQ)
        rows = carve(s5 + 1024, 5, P)
        rotA = carve(s5 + 1024, 2, 2, SEQ)
        zz = carve(s5 + 2048, 2, 2, SEQ)
        rotB = carve(s5 + 3072, 2, 2, SEQ)
        prod_re = carve(s5 + 4096, 2, 2, SEQ)
        prod_im = y[:, 1, :].rearrange("p (a b t) -> p a b t", a=2, b=2)
        bt5 = carve(s5 + 5120, 2, 4, P)
        ct5 = carve(s5 + 6144, 2, 4, P)
        sm5 = carve(s5 + 7168, 10, 16)
        bpad = carve(s5 + 2048, 2, 16, 32)
        cpad = carve(s5 + 3072, 2, 4, P)
        braw = carve(s5 + 4096, 2, 16, 16)
        craw = carve(s5 + 4608, 2, 4, 64)
        bq = etmp[:, 256:512].rearrange("p (a b) -> p a b", a=16)
        yv = carve(0, 4, SEQ)
        gt5 = carve(2048, 4, SEQ)
        zf = y[:, 0, :].rearrange("p (q t) -> p q t", q=4)
        z2f = y[:, 1, :].rearrange("p (q t) -> p q t", q=4)
        pair = sb("pair", [1, 64])
        pairb = sb("pairb", [P, 32])
        alog = sb("alog", [P, SH])
        dtb = sb("dtb", [P, SH])

        squared = carve(13312, 2, 512)
        relu_b = carve(0, 2, 512)
        sq_b = carve(1024, 2, 512)
        pj = carve(0, TB, ATT_COLS)
        qT1 = carve(4240, 8, SEQ)
        kT1 = carve(6288, 4, SEQ)
        qiT = carve(7312, 4, SEQ)
        kiT = carve(8336, SEQ)
        roped = carve(11152, TB, 2176)
        rope_i = carve(9616, 2, 576)
        rope_q, rope_k = y[:, 0, :].rearrange("p (u n) -> p u n", u=2), y[:, 1, 0:512].rearrange("p (u n) -> p u n", u=2)
        rel = carve(8592, 2, 512)
        score = carve(9616, TB, SEQ)
        left = carve(10128, TB, SEQ)
        keep = carve(10640, SEQ).bitcast(BF16).rearrange("p (b t) -> p b t", b=TB)
        p1 = carve(11152, 3, 512)
        pT1 = carve(12688, 2, 512)
        qk2 = carve(0, TB, AW)
        v2 = carve(3072, TB, AW)
        qT2 = carve(6144, 12, SEQ)
        kT2 = carve(9216, 12, SEQ)
        p2 = carve(0, 3, 768)
        pT2 = [carve(2304, 768), gpost[:, 0:768]]
        sqh = y[:, :, :].rearrange("p b n -> p (b n)").rearrange("p (u m) -> p u m", u=2)
        g_ssd = carve(12288, TB, D)
        dt_tok = carve(14336, TB, SH)
        a_tok = carve(14400, TB, SH)
        sp1 = carve(14464, TB, SH)
        sp2 = carve(14528, TB, SH)
        sp3 = carve(14592, TB, SH)
        hv2 = carve(14656, 16)
        ht2 = carve(14680, 16)
        hr2 = carve(14704, 16)
        zc = carve(0, 2, 2, SEQ)
        zt = carve(1024, 2, 2, SEQ)
        xpad = carve(2048, 2, 260)
        xconv = carve(2568, 2, SEQ)
        xtanh = carve(3080, 2, SEQ)
        xsc = carve(3592, 2, 2, SEQ)
        bcpad = carve(4616, 2, 260)
        bconv = carve(5136, 2, SEQ)
        btanh = carve(5648, 2, SEQ)
        bcc = carve(6160, 2, 2, SEQ)
        Lm = carve(7184, 4, 384)
        Xt = carve(8720, TB, SEQ)
        cbs = carve(9232, 384)
        yz = carve(9616, 2, 2, SEQ)
        sq2 = carve(10640, 2, SEQ)
        gv_ = carve(11152, SEQ)
        gt_ = carve(11408, SEQ)
        gr_ = carve(11664, SEQ)
        yn = carve(14900, 2, SEQ)
        fpad = carve(0, 2, 2, 260)
        fconv = carve(1040, 2, 2, SEQ)
        ftanh = carve(2064, 2, SEQ)
        fhid = carve(2576, 2, SEQ)
        wkf = wk[:, :, :].rearrange("p b n -> p (b n)")
        yf = y[:, :, :].rearrange("p b n -> p (b n)")
        small = sb("small", [P, 2, 4, 4])
        top8 = sb("top8", [P, 8])
        wi_s = sb("wi_s", [P, TB, IH])

        block = ctx.enter_context(nc.Block())

        def kview(w):
            return w.rearrange("(k p) n -> p k n", p=P)

        w1 = [kview(ins["mlp_w1"][l]) for l in range(2)]
        w2 = [kview(ins["mlp_w2"][l]) for l in range(2)]
        sw_in, sw_glu, sw_out = (kview(ins[n][0]) for n in ("ssm_w_in", "ssm_w_glu", "ssm_w_out"))
        aw_in, aw_out = kview(ins["att_w_in"][0]), kview(ins["att_w_out"][0])
        w_in2, w_ssd, w_atp, w_out2, w_up, w_dn = (
            kview(ins[n][0]) for n in ("w_in_2", "w_ssd_proj_2", "w_attn_proj_2", "w_out_2", "w_up_2", "w_down_2"))

        @block.sync
        def _(sp):
            ring = Ring()

            def load(a, b, shape):
                first = ring.n < 2
                s, _, piece = ring.next()
                rows_k, n = shape
                for part, src in zip("ab", (a, b)):
                    if not first:
                        sp.wait_ge(S(f"lo_{part}"), piece - 1)
                    dst = raw[:, s % 2, "ab".index(part), 0:rows_k * n]
                    sp.dma_start(dst.rearrange("p (k n) -> p k n", n=n), src).then_inc(S(f"loaded_{part}{s % 2}"), 16)

            def up(w, c0):
                cs = bass.ds(c0, 256)
                load(w[:, 0:4, cs], w[:, 4:8, cs], (4, 256))

            def chunk4(w, c0):
                for kk in (0, 4):
                    cs = bass.ds(c0, 512)
                    load(w[:, kk:kk + 2, cs], w[:, kk + 2:kk + 4, cs], (2, 512))

            def down(w, k0):
                load(w[:, bass.ds(k0, 1), :], w[:, bass.ds(k0 + 1, 1), :], (1, 1024))

            def narrow(w, c0, n):
                load(w[:, 0:4, c0:c0 + n], w[:, 4:8, c0:c0 + n], (4, n))

            xv = ins["x"][0].rearrange("(b p) n -> b p n", p=P)
            sp.dma_start(h[:, 0, :], xv[0]).then_inc(S("x_in0"), 16)
            sp.dma_start(cst[:, 0:C_FIRST], ins["consts"][:, 0:C_FIRST]).then_inc(S("first_in"), 16)
            sp.dma_start(h[:, 1, :], xv[1]).then_inc(S("x_in1"), 16)
            sp.dma_start(gpre[:, :], ins["norm_g"][0, 0].partition_broadcast(P)).then_inc(S("gpre_in"), 16)
            up(sw_in, 0)
            up(sw_in, 256)
            for dst, src in bc5_loads(ins, braw, craw):
                sp.dma_start(dst, src).then_inc(S("bc5_in"), 16)
            sp.dma_start(cst[:, C_FIRST:], ins["consts"][:, C_FIRST:]).then_inc(S("consts_in"), 16)
            for dst, src in late_loads(ins, rows, pair, alog, dtb):
                sp.dma_start(dst, src).then_inc(S("late_in"), 16)
            sp.dma_start(gpost[:, :], ins["norm_g"][0, 1].partition_broadcast(P)).then_inc(S("gpost_in"), 16)
            load(sw_glu[:, 0:2, :], sw_glu[:, 2:4, :], (2, 512))
            down(sw_out, 0)
            down(sw_out, 2)

            def mlp(layer):
                up(w1[layer], 0)
                with sp.Fori(0, (MC - 2) // 2) as i:
                    ring.enter(i, 1)
                    up(w1[layer], i * 512 + 256)
                    down(w2[layer], i * 4)
                    up(w1[layer], i * 512 + 512)
                    down(w2[layer], i * 4 + 2)
                ring.leave((MC - 2) // 2)
                up(w1[layer], (MC - 1) * 256)
                down(w2[layer], 2 * MC - 4)
                down(w2[layer], 2 * MC - 2)

            mlp(0)
            chunk4(aw_in, QIOFF)
            narrow(aw_in, KIOFF, ATT_TAIL)
            for c in range(3):
                chunk4(aw_in, 512 * c)
            for k in range(0, KD, 2):
                down(aw_out, k)
            mlp(1)
            for off in (Q2OFF, V2OFF, K2OFF):
                for c in range(3):
                    chunk4(w_in2, off + 512 * c)
                    if off == Q2OFF and c == 0:
                        narrow(w_in2, DTOFF, SH)
            for c in range(8):
                up(w_in2, GATEOFF + 256 * c)
            down(w_atp, 0)
            down(w_atp, 2)

            def ssd_step(g, with_out):
                up(w_in2, g * 256 + ZOFF)
                up(w_in2, g * 256 + XSOFF)
                load(w_in2[:, :, bass.ds(g * P + BOFF, P)], w_in2[:, :, bass.ds(g * P + COFF, P)], (8, P))
                if with_out:
                    down(w_ssd, g * 2 - 4)

            ssd_step(0, False)
            ssd_step(1, False)
            with sp.Fori(0, 3) as i:
                ring.enter(i, 2)
                ssd_step(i * 2 + 2, True)
                ssd_step(i * 2 + 3, True)
            ring.leave(3)
            down(w_ssd, 12)
            down(w_ssd, 14)
            for k in range(0, KD, 2):
                down(w_out2, k)

            def gate_val(c):
                load(w_up[:, :, bass.ds(c * P, P)], w_up[:, :, bass.ds(c * P + DFF2, P)], (8, P))

            def down1(c):
                load(w_dn[:, bass.ds(c, 1), 0:512], w_dn[:, bass.ds(c, 1), 512:1024], (1, 512))

            gate_val(0)
            with sp.Fori(0, (FC - 2) // 2) as i:
                ring.enter(i, 1)
                gate_val(i * 2 + 1)
                down1(i * 2)
                gate_val(i * 2 + 2)
                down1(i * 2 + 1)
            ring.leave((FC - 2) // 2)
            gate_val(FC - 1)
            down1(FC - 2)
            down1(FC - 1)
            outv = out[0].rearrange("(b p) n -> b p n", p=P)
            for tb in range(TB):
                for n in range(2):
                    sp.wait_ge(S("out_ready"), 2 * tb + n + 1)
                    sp.dma_start(outv[tb][:, n * 512:(n + 1) * 512], halves(y, tb, n)).then_inc(S("out_stored"), 16)
            sp.wait_ge(S("out_stored"), 2 * TB * 16)

        SMALL = {P_ATT + 2: 8 * ATT_TAIL, P_B2 + 2: 8 * SH}

        def size(n):
            if n >= P_WOUT2 + 4:
                m = n - P_WOUT2 - 4
                return 1024 if (m in (42, 43) or (m % 2 == 0 and 2 <= m < 42)) else 2048
            return SMALL.get(n, 2048)

        def low_part(eng, tensor_tensor, ring, part, n):
            s, _, piece = ring.next()
            m = n // 2
            cs = slice(0, m) if part == "a" else slice(m, n)
            eng.wait_ge(S(f"hi_{part}"), piece + 1)
            tensor_tensor(LO[:, s, cs], raw[:, s % 2, "ab".index(part), 0:m], HI[:, s, cs].bitcast(F32),
                          ALU.subtract).then_inc(S(f"lo_{part}"), 1)

        def rotate(eng, link, work, x, heads, tb, outs):
            r1, r2 = (work[:, u, 0:heads * HD].rearrange("p (a d) -> p a d", d=HD) for u in range(2))
            eng.tensor_tensor(r1, x, cosT[:, tb, :].unsqueeze(1).to_broadcast([P, heads, HD]), ALU.mult)
            eng.tensor_tensor(r2[:, :, 0:32], x[:, :, 32:64], sinT[:, tb, 0:32].unsqueeze(1).to_broadcast([P, heads, 32]),
                              ALU.mult)
            link(eng.tensor_tensor(r2[:, :, 32:64], x[:, :, 0:32],
                                   sinT[:, tb, 32:64].unsqueeze(1).to_broadcast([P, heads, 32]), ALU.mult))
            for o in outs:
                last = eng.tensor_tensor(o, r1, r2, ALU.add)
            return last

        def heads_of(t, tb, c0, heads):
            return t[:, tb, c0:c0 + heads * HD].rearrange("p (a d) -> p a d", d=HD)

        def doubled(tb, c0, heads):
            v = roped[:, tb, c0:c0 + heads * 2 * HD].rearrange("p (a u d) -> p a u d", u=2, d=HD)
            return [v[:, :, u, :] for u in range(2)]

        def turn_table(eng, link, i0, i1, room, L, end):
            e = e_tab[:, i0:i1]
            if L == 1:
                eng.tensor_copy(e[:, :, 0, 1:2], sm5[:, 5, i0:i1].unsqueeze(2))
                link(eng.tensor_copy(e[:, :, 1, 1:2], sm5[:, 4, i0:i1].unsqueeze(2)))
            while L < end:
                n = min(L, end - L)
                er, ei = e[:, :, 0, 1:1 + n], e[:, :, 1, 1:1 + n]
                ur = e[:, :, 0, L:L + 1].to_broadcast([P, i1 - i0, n])
                ui = e[:, :, 1, L:L + 1].to_broadcast([P, i1 - i0, n])
                nr, ni = e[:, :, 0, L + 1:L + 1 + n], e[:, :, 1, L + 1:L + 1 + n]
                tmp = room[:, 0:(i1 - i0) * n].rearrange("p (i t) -> p i t", i=i1 - i0)
                eng.tensor_tensor(nr, er, ur, ALU.mult)
                eng.tensor_tensor(ni, er, ui, ALU.mult)
                link(eng.tensor_tensor(tmp, ei, ui, ALU.mult))
                link(eng.tensor_tensor(nr, nr, tmp, ALU.subtract))
                link(eng.tensor_tensor(tmp, ei, ur, ALU.mult))
                link(eng.tensor_tensor(ni, ni, tmp, ALU.add))
                L *= 2

        @block.gpsimd
        def _(pool):
            ring = Ring()
            steps = Steps(pool, S("pool_step"))
            G = nc.gpsimd
            nc.gpsimd.memset(ones[:, :], 1.0)
            steps.link(G.memset(half[:, :], -0.5))

            def row_rstd(e):
                for tb in range(TB):
                    cs = slice(tb, tb + 1)
                    pool.wait_ge(S("ssq_ready"), 2 * (TB * e + tb) + 2)
                    steps.link(G.tensor_scalar(nv[:, cs], ssq[:, tb, 0:1], ssq[:, tb, 1:2], EPS, ALU.add, ALU.add))
                    G.tensor_tensor(rstd[:, cs], nv[:, cs], half[:, cs], ALU.pow).then_inc(S("rstd_ready"), 1)

            def upto(n):
                while ring.n <= n:
                    low_part(pool, nc.gpsimd.tensor_tensor, ring, "b", size(ring.n))

            def loop(turns, per, first):
                with pool.Fori(0, turns) as i:
                    ring.enter(i, per)
                    for j in range(4 * per):
                        low_part(pool, nc.gpsimd.tensor_tensor, ring, "b", size(first + j))
                ring.leave(turns)

            row_rstd(0)
            pool.wait_ge(S("sin5_ready"), 1)
            turn_table(G, steps.link, E_SPLIT, ST, carve(s5 + 1024 + 5 * P, 3 * P), 1, 64)
            upto(1)
            turn_table(G, steps.link, E_SPLIT, ST, etmp[:, E_SPLIT * P:], 64, SEQ - 1)
            upto(3)
            def turned_sums(i):
                b = i % 2
                pool.wait_ge(S("bu_read"), i + 1)
                G.tensor_tensor(rotA[:, b, 0, :], rotA[:, b, 0, :], rotA[:, b, 1, :], ALU.add).then_inc(S("vr5_ready"), 1)
                G.tensor_tensor(rotB[:, b, 0, :], rotB[:, b, 1, :], rotB[:, b, 0, :], ALU.subtract)\
                    .then_inc(S("vi5_ready"), 1)

            turned_sums(0)
            for i in range(ST):
                b = i % 2
                if i + 1 < ST:
                    turned_sums(i + 1)
                pool.wait_ge(S("z5_ready"), i + 1)
                if i >= 2:
                    pool.wait_ge(S("x5_used"), i - 1)
                G.tensor_tensor(prod_im[:, b, 0, :], zz[:, b, 0, :], e_tab[:, i, 1, :], ALU.mult)
                G.tensor_tensor(prod_im[:, b, 1, :], zz[:, b, 1, :], e_tab[:, i, 0, :], ALU.mult)\
                    .then_inc(S("xi5_ready"), 1)
            upto(6)
            row_rstd(1)
            row_rstd(2)
            upto(8)
            upto(5)
            loop(7, 1, 9)
            upto(P_ATT + 1)
            row_rstd(3)
            row_rstd(4)
            upto(P_ATT + 7)
            for c in range(2):
                pool.wait_ge(S("pj_read"), 3 + c)
                for tb in range(TB):
                    rotate(G, steps.link, rope_q, heads_of(pj, tb, c * 512, 8), 8, tb, [heads_of(roped, tb, c * 512, 8)])\
                        .then_inc(S("q_roped"), 1)
                    pool.wait_ge(S("q_roped"), TB * c + tb + 1)
                upto(P_ATT + 8)
            upto(P_ATT + 14)
            row_rstd(5)
            row_rstd(6)
            upto(P_ATT + 16)
            loop(7, 1, P_ATT + 17)
            upto(P_B2 + 1)
            row_rstd(7)
            row_rstd(8)
            upto(P_SSD + 5)
            with pool.Fori(0, 3) as i:
                ring.enter(i, 2)
                steps.enter(i, 0)
                for j in range(8):
                    low_part(pool, G.tensor_tensor, ring, "b", 2048)
            ring.leave(3)
            upto(P_WOUT2 + 5)
            row_rstd(9)
            upto(P_WOUT2 + 8)
            loop(9, 1, P_WOUT2 + 9)
            upto(P_WOUT2 + 4 + 43)

        def bank2(c):
            return 2 * ((c + (c > 0)) % 2)

        def last2(c):
            return P_B2 + 2 * c + 1 + (c > 0)

        @block.tensor
        def _(pe):
            ring = Ring()
            mm = nc.tensor.matmul

            def arrived():
                s, _, piece = ring.next()
                pe.wait_ge(S("lo_a"), piece + 1)
                pe.wait_ge(S("lo_b"), piece + 1)
                return s

            def used(ins):
                ins.then_inc(S("piece_done"), 1)

            def three(o, lh, ll, rh, rl, start, stop, skip=False):
                mm(o, lh, rh, start=start, stop=False, skip_group_check=skip)
                mm(o, lh, rl, start=False, stop=False, skip_group_check=skip)
                return mm(o, ll, rh, start=False, stop=stop, skip_group_check=skip)

            def ch_major(s, bank, paired=False, norm=None):
                for j in range(2):
                    for k in range(KD):
                        w = (j * KD + k) * P if paired else k * 256 + j * P
                        if norm is not None and j == 0:
                            xT_wait(norm, 1, k)
                        last = three(wk[:, bank, j * SEQ:(j + 1) * SEQ], HI[:, s, w:w + P], LO[:, s, w:w + P],
                                     XH[:, k, :], XL[:, k, :], k == 0, k == KD - 1)
                return last

            def tok_major(s, outs, k0, kt, n, start, stop, norm=None):
                for tb in range(TB):
                    for k in range(kt):
                        ts = slice(tb * P, (tb + 1) * P)
                        if norm is not None:
                            xT_wait(norm, tb, k0 + k)
                        last = three(outs(tb), XH[:, k0 + k, ts], XL[:, k0 + k, ts], HI[:, s, k * n:(k + 1) * n],
                                     LO[:, s, k * n:(k + 1) * n], start and k == 0, stop and k == kt - 1)
                return last

            def clear_acc():
                for q in range(4):
                    mm(accf[:, q * 512:(q + 1) * 512], zero_bf[:, 0:P], zero_bf[:, :], start=True, stop=False,
                       skip_group_check=True)

            def down(s, tiles, last_group, kt=2, first=False, norm=None):
                for tb in range(TB):
                    ts = slice(tb * P, (tb + 1) * P)
                    for kk in range(kt):
                        xh, xl = tiles(kk)
                        if norm is not None:
                            xT_wait(norm[0], tb, norm[1] + kk)
                        stop = last_group and kk == kt - 1
                        for lhs, w, begin, end in ((xh, HI, first and kk == 0, False), (xh, LO, False, False),
                                                   (xl, HI, False, stop)):
                            for n in range(2):
                                c = kk * 1024 + n * 512
                                last = mm(acc[:, tb, n * 512:(n + 1) * 512], lhs[:, ts], w[:, s, c:c + 512],
                                          start=begin, stop=end, skip_group_check=True)
                    if last_group and tb == 0:
                        last.then_inc(S("acc_first"), 1)
                return last

            def norm_transpose(n):
                for q in range(4):
                    tb, b = q // 2, q % 2
                    pe.wait_ge(S("y_ready"), 4 * n + q + 1)
                    for kk in range(4):
                        k = 4 * b + kk
                        last = nc.tensor.transpose(wk[:, q, kk * P:(kk + 1) * P], y[:, tb, k * P:(k + 1) * P], ident)
                    last.then_inc(S("xT_psum"), 1)

            def xT_wait(n, tb, k):
                if k % 4 == 0:
                    pe.wait_ge(S("xT_lo"), 4 * n + 2 * tb + k // 4 + 1)

            def by_halves(o, row):
                for q in range(2):
                    last = mm(o, cst[0:1, C_SEL + q * P:C_SEL + (q + 1) * P], row[:, q::2], start=(q == 0), stop=(q == 1))
                return last

            pe.wait_ge(S("first_in"), 16)
            pe.wait_ge(S("s5_in"), 16 * N_S5)
            nc.tensor.transpose(accf[:, 0:ROWS[0]], rows[0:ROWS[0], 0, :], ident[0:ROWS[0], 0:ROWS[0]])
            by_halves(accf[:, P:P + 16], pair[0:1, 0:32]).then_inc(S("cols_psum"), 1)
            norm_transpose(0)
            for b in range(2):
                s = arrived()
                last = ch_major(s, b, norm=0 if b == 0 else None)
                used(last)
            pe.wait_ge(S("cpad_ready"), 1)
            for r in range(2):
                for q in range(4):
                    last = nc.tensor.transpose(accf[:, 512 + r * 512 + q * P:512 + r * 512 + (q + 1) * P],
                                               cpad[:, r, q, :], ident)
            last.then_inc(S("ct_psum"), 1)
            pe.wait_ge(S("late_in"), 16 * N_LATE)
            by_halves(accf[:, P + 16:P + 32], pair[0:1, 32:64])
            for r, n in enumerate(ROWS[1:]):
                last = nc.tensor.transpose(accf[:, 1536 + r * P:1536 + r * P + n], rows[0:n, 1 + r, :], ident[0:n, 0:n])
            last.then_inc(S("cols_psum"), 1)
            pe.wait_ge(S("bpad_ready"), 1)
            pe.wait_ge(S("u_ready"), 2)
            for r in range(2):
                for q in range(4):
                    last = nc.tensor.transpose(wk[:, 2 + r, q * P:(q + 1) * P],
                                               bpad[:, r, 4 * q:4 * q + 4, :].rearrange("p a b -> p (a b)"), ident)
            last.then_inc(S("bt_psum"), 1)
            pe.wait_ge(S("bt_ready"), 1)
            pe.wait_ge(S("ct_ready"), 1)
            pe.wait_ge(S("cols_ready"), 2)

            def drive(i):
                q, j = i // 4, i % 4
                js = slice(32 * j, 32 * j + 32)
                if i >= 4:
                    pe.wait_ge(S("bu_read"), i - 3)
                for r in range(2):
                    last = mm(wk[:, i % 4, r * SEQ:(r + 1) * SEQ], bt5[js, r, q, :], uT[js, q, :],
                              start=True, stop=True)
                last.then_inc(S("bu_psum"), 1)

            def glu(s, k):
                pe.wait_ge(S("z_lo"), k + 1)
                for b in range(2):
                    for j in range(2):
                        w = k * 512 + (2 * b + j) * P
                        last = three(wk[:, b, j * SEQ:(j + 1) * SEQ], HI[:, s, w:w + P], LO[:, s, w:w + P],
                                     XH[:, k, :], XL[:, k, :], False, k == 3, True)
                    if k == 3 and b == 0:
                        last.then_inc(S("glu_psum"), 1)
                return last

            for i in range(4):
                drive(i)
            for i in range(ST):
                q, j = i // 4, i % 4
                js = slice(32 * j, 32 * j + 32)
                pe.wait_ge(S("xr5_ready"), i + 1)
                pe.wait_ge(S("xi5_ready"), i + 1)
                b = i % 2
                for n, (c, x) in enumerate(((ct5[:, 0, q, js], prod_re[:, b, 0, :]), (ct5n[:, q, js], prod_re[:, b, 1, :]),
                                            (ct5[:, 1, q, js], prod_im[:, b, 0, :]), (ct5[:, 1, q, js], prod_im[:, b, 1, :]))):
                    last = mm(accf[js, q * 512:q * 512 + SEQ], c, x, start=(n == 0), stop=(n == 3))
                last.then_inc(S("x5_used"), 1)
                if i + 4 < ST:
                    drive(i + 4)
                if i == 13:
                    glu_slot = arrived()
                    pe.wait_ge(S("bu_read"), 14)
                    for b in range(2):
                        mm(wk[:, b, :], zero_bf[:, 0:P], zero_bf[:, :], start=True, stop=False, skip_group_check=True)
                if i >= 13:
                    last = glu(glu_slot, i - 13)
            last = glu(glu_slot, 3)
            used(last)
            pe.wait_ge(S("z2_lo"), 2)
            for p in range(2):
                s = arrived()
                used(down(s, lambda kk: (XH[:, 4 + 2 * p + kk, :], XL[:, 4 + 2 * p + kk, :]), p == 1, first=p == 0))

            def mlp(layer):
                norm_transpose(1 + 2 * layer)
                base = layer * MC

                def mlp_up(c, par):
                    if not (isinstance(c, int) and c + base < 2):
                        pe.wait_ge(S("hid_read"), c + base - 1)
                    s = arrived()
                    used(ch_major(s, par, norm=1 + 2 * layer if isinstance(c, int) and c == 0 else None))

                def mlp_down(c, par, end=False):
                    pe.wait_ge(S("hid_lo"), c + base + 1)
                    s = arrived()
                    used(down(s, lambda kk: (HH[:, par, kk, :], HL[:, par, kk, :]), end))

                def turn(c):
                    mlp_up(c + 1, 1)
                    mlp_down(c, 0)
                    mlp_up(c + 2, 0)
                    mlp_down(c + 1, 1)

                mlp_up(0, 0)
                clear_acc()
                turn(0)
                with pe.Fori(0, MC // 2 - 2) as i:
                    ring.enter(i, 1)
                    turn(i * 2 + 2)
                ring.leave(MC // 2 - 2)
                mlp_up(MC - 1, 1)
                mlp_down(MC - 2, 0)
                mlp_down(MC - 1, 1, True)

            mlp(0)

            norm_transpose(2)

            def proj1(e, part):
                if e >= 2 and part == 0:
                    pe.wait_ge(S("pj_read"), e - 1)
                s = arrived()
                used(tok_major(s, lambda tb: wk[:, 2 * (e % 2) + tb, :], 4 * part, 4, 512, part == 0, part == 1,
                               norm=2 if e == 0 else None))

            def tile_transpose(n, blocks):
                if n >= 2:
                    pe.wait_ge(S("qkT_read"), n - 1)
                for b, (tb, c) in enumerate(blocks):
                    last = nc.tensor.transpose(accf[:, (n % 2) * 512 + b * P:(n % 2) * 512 + (b + 1) * P],
                                               roped[:, tb, c:c + P], ident)
                last.then_inc(S("qkT_psum"), 1)

            def row4(tb, c):
                return [(tb, c + b * P) for b in range(4)]

            def index(job):
                tb, h0, nh = IJOBS[job]
                if job >= 2:
                    pe.wait_ge(S("rel_read"), job - 1)
                K = P * (tb + 1)
                for b in range(nh):
                    hd = h0 + 2 * b
                    hs = slice(64 * (hd % 2), 64 * (hd % 2) + 64)
                    o = 1024 + (job % 2) * 512 + b * K
                    last = mm(accf[:, o:o + K], qiT[hs, hd // 2, tb * P:(tb + 1) * P], kiT[hs, 0:K], start=True, stop=True)
                last.then_inc(S("rel_psum"), 1)

            proj1(0, 0)
            proj1(0, 1)
            s = arrived()
            used(tok_major(s, lambda tb: wk[:, 2 + tb, 0:ATT_TAIL], 0, KD, ATT_TAIL, True, True))
            proj1(2, 0)
            pe.wait_ge(S("i_roped"), 2)
            tile_transpose(0, row4(0, 1536))
            tile_transpose(1, row4(1, 1536))
            tile_transpose(2, [(0, 2048), (1, 2048)])
            proj1(2, 1)
            pe.wait_ge(S("qkT_read"), 3)
            index(0)
            index(1)
            proj1(3, 0)
            index(2)
            index(3)
            proj1(3, 1)
            index(4)
            index(5)
            pe.wait_ge(S("q_roped"), 2)
            tile_transpose(3, row4(0, 0))
            tile_transpose(4, row4(1, 0))
            proj1(4, 0)
            proj1(4, 1)
            pe.wait_ge(S("q_roped"), 4)
            tile_transpose(5, row4(0, 512))
            tile_transpose(6, row4(1, 512))
            pe.wait_ge(S("k_roped"), 2)
            tile_transpose(7, row4(0, 1024))
            tile_transpose(8, row4(1, 1024))
            pe.wait_ge(S("qkT_read"), 9)

            def scores1(n):
                tb, h0, nh = JOBS1[n]
                K = P * (tb + 1)
                if n >= 4:
                    pe.wait_ge(S("e1_ready"), n - 3)
                else:
                    pe.wait_ge(S("keep_ready"), 1 + tb)
                for b in range(nh):
                    hd = h0 + 2 * b
                    hs = slice(64 * (hd % 2), 64 * (hd % 2) + 64)
                    o = wk[:, n % 4, b * K:(b + 1) * K]
                    mm(o, id_bf[:, :], keep[:, tb, 0:K], start=True, stop=False, skip_group_check=True)
                    last = mm(o, qT1[hs, hd // 2, tb * P:(tb + 1) * P], kT1[hs, hd // 4, 0:K], start=False, stop=True,
                              skip_group_check=True)
                last.then_inc(S("s1_psum"), 1)

            def transposed1(n):
                pe.wait_ge(S("p1_ready"), n + 1)
                if n >= 2:
                    pe.wait_ge(S("pT1_ready"), n - 1)
                for b in range(4):
                    last = nc.tensor.transpose(accf[:, (n % 2) * 512 + b * P:(n % 2) * 512 + (b + 1) * P],
                                               p1[:, n % 3, b * P:(b + 1) * P], ident)
                last.then_inc(S("pT1_psum"), 1)

            def weighted1(n):
                tb, h0, nh = JOBS1[n]
                pe.wait_ge(S("pT1_ready"), n + 1)
                if n >= 2:
                    pe.wait_ge(S("o1_lo"), n - 1)
                for b in range(nh):
                    hd = h0 + 2 * b
                    o = 1024 + (n % 2) * 512 + b * P
                    for kb in range(tb + 1):
                        last = mm(accf[64 * (hd % 2):64 * (hd % 2) + 64, o:o + P],
                                  pj[:, kb, VOFF + (hd // 4) * 64:VOFF + (hd // 4) * 64 + 64],
                                  pT1[:, n % 2, (b * (tb + 1) + kb) * P:(b * (tb + 1) + kb + 1) * P],
                                  start=(kb == 0), stop=(kb == tb))
                last.then_inc(S("o1_psum"), 1)

            N1 = len(JOBS1)
            for n in range(3):
                scores1(n)
            for n in range(N1 + 1):
                if n + 3 < N1:
                    scores1(n + 3)
                if n < N1:
                    transposed1(n)
                if n >= 1:
                    weighted1(n - 1)
            pe.wait_ge(S("o1_lo"), len(JOBS1))
            for p in range(4):
                s = arrived()
                used(down(s, lambda kk: (XH[:, 2 * p + kk, :], XL[:, 2 * p + kk, :]), p == 3, first=p == 0))

            mlp(1)

            norm_transpose(4)

            def qk_transpose(c):
                j = c if c < 3 else c - 3
                pe.wait_ge(S("qk2_normed"), j + 1)
                for tb in range(TB):
                    n = TB * j + tb
                    if n >= 2:
                        pe.wait_ge(S("qkT2_read"), n - 1)
                    for b in range(4):
                        col = (c % 3) * 512 + b * P
                        last = nc.tensor.transpose(accf[:, (n % 2) * 512 + b * P:(n % 2) * 512 + (b + 1) * P],
                                                   qk2[:, tb, col:col + P], ident)
                    last.then_inc(S("qkT2_psum"), 1)

            for c in range(9):
                if c == 1:
                    pe.wait_ge(S("qk2_normed"), 1)
                elif c == 2:
                    pe.wait_ge(S("dt_read"), 1)
                elif 5 <= c < 8:
                    pe.wait_ge(S("v2_read"), c - 4)
                elif c >= 3:
                    pe.wait_ge(S("qk2_normed"), c - 1 if c < 5 else c - 4)
                for part in range(2):
                    s = arrived()
                    used(tok_major(s, lambda tb: wk[:, bank2(c) + tb, :], 4 * part, 4, 512, part == 0, part == 1,
                                   norm=4 if c == 0 else None))
                if c == 0:
                    s = arrived()
                    used(tok_major(s, lambda tb: wk[:, 2 + tb, 0:SH], 0, KD, SH, True, True))
                if c >= 1 and not 3 <= c - 1 < 6:
                    qk_transpose(c - 1)
            pe.wait_ge(S("a_ready"), 1)
            UU, GT = cst[:, C_UU:C_UU + P], cst[:, C_GT:C_GT + P]
            for n, (lhs, b) in enumerate(((UU, 0), (UU, 1), (GT, 0))):
                last = mm(accf[:, 1024 + n * 32:1024 + (n + 1) * 32], lhs, a_tok[:, b, :], start=True, stop=True)
            last.then_inc(S("cs_psum"), 1)

            gate_slot = [0]

            def gate_half(c, tb):
                if tb == 0:
                    if c >= 1:
                        pe.wait_ge(S("gate_read"), c)
                    gate_slot[0] = arrived()
                s = gate_slot[0]
                for k in range(KD):
                    ts = slice(tb * P, (tb + 1) * P)
                    last = three(accf[:, 1536 + tb * 256:1536 + (tb + 1) * 256], XH[:, k, ts], XL[:, k, ts],
                                 HI[:, s, k * 256:(k + 1) * 256], LO[:, s, k * 256:(k + 1) * 256], k == 0, k == KD - 1)
                if tb == 1:
                    used(last)

            gate_half(0, 0)
            gate_half(0, 1)
            qk_transpose(8)
            pe.wait_ge(S("qkT2_read"), 12)

            def scores2(n):
                hd, tb = JOBS2[n]
                K = P * (tb + 1)
                if n >= 2:
                    pe.wait_ge(S("s2_read"), n - 1)
                hs = slice(64 * (hd % 2), 64 * (hd % 2) + 64)
                for gi in range(3):
                    o = (n % 2) * 1024 + gi * K
                    last = mm(wkf[:, o:o + K], qT2[hs, gi * 4 + hd // 2, tb * P:(tb + 1) * P],
                              kT2[hs, gi * 4 + hd // 2, 0:K], start=True, stop=True)
                last.then_inc(S("s2_psum"), 1)

            def transposed2(n):
                hd, tb = JOBS2[n]
                pe.wait_ge(S("p2_ready"), n + 1)
                if n >= 1:
                    pe.wait_ge(S("pT2_ready"), n)
                for b in range(3 * (tb + 1)):
                    last = nc.tensor.transpose(accf[:, b * P:(b + 1) * P], p2[:, n % 3, b * P:(b + 1) * P], ident)
                last.then_inc(S("pT2_psum"), 1)

            def weighted2(n):
                hd, tb = JOBS2[n]
                nb = 3 * (tb + 1)
                pe.wait_ge(S("pT2_ready"), n + 1)
                if n >= 2 and n % 2 == 0:
                    pe.wait_ge(S("o2_lo"), n // 2)
                elif n == 0:
                    pe.wait_ge(S("cs_read"), 1)
                for b in range(nb):
                    gi, kb = b // (tb + 1), b % (tb + 1)
                    c = gi * 512 + hd * 64
                    last = mm(accf[64 * (hd % 2):64 * (hd % 2) + 64, 1024:1024 + P], v2[:, kb, c:c + 64],
                              pT2[n % 2][:, b * P:(b + 1) * P], start=(b == 0), stop=(b == nb - 1))
                if n % 2:
                    last.then_inc(S("o2_psum"), 1)

            N2 = len(JOBS2)
            scores2(0)
            scores2(1)
            for n in range(N2 + 1):
                if n + 2 < N2:
                    scores2(n + 2)
                if n < N2:
                    transposed2(n)
                if n >= 1:
                    weighted2(n - 1)
                if n < 14:
                    gate_half(1 + n // 2, n % 2)
            pe.wait_ge(S("o2_lo"), 8)
            pe.wait_ge(S("gate_read"), 8)
            for p in range(2):
                s = arrived()
                used(down(s, lambda kk: (OH[:, 2 * p + kk, :], OL[:, 2 * p + kk, :]), p == 1, first=p == 0))
            pe.wait_ge(S("merged_attn"), 1)
            clear_acc()

            def decay_rows(g, par, m):
                gpv, b = gp[:, 1 - par, :], m % 2
                if m >= 2:
                    pe.wait_ge(S("L_read"), g * 4 - 4 + m - 1)
                elif m == 0:
                    pe.wait_ge(S("gp_ready"), g)
                    pe.wait_ge(S("bc_read"), g)
                elif not (isinstance(g, int) and g < 2):
                    pe.wait_ge(S("y_read"), g - 1)
                a0 = gpv[:, G_A + m:G_A + m + 1].to_broadcast([P, P])
                a1 = gpv[:, G_A + 4 + m:G_A + 5 + m].to_broadcast([P, P])
                mm(wk[:, b, 0:P], id_bf[:, :], neg_bf[:, :], start=True, stop=False, skip_group_check=True)
                mm(wk[:, b, 2 * P:3 * P], id_bf[:, :], neg_bf[:, :], start=False, stop=False, skip_group_check=True)
                mm(wk[:, b, 0:P], a0, cst[:, C_UU:C_UU + P], start=False, stop=False, skip_group_check=True)
                mm(wk[:, b, P:3 * P], a1, cst[:, C_UU:C_UU + 2 * P], start=False, stop=True,
                   skip_group_check=True).then_inc(S("L_psum"), 1)

            def xs_transpose(g, par):
                pe.wait_ge(S("xsc_ready"), g)
                for j in range(2):
                    for tb in range(TB):
                        o = tb * 256 + j * P
                        last = nc.tensor.transpose(wk[:, 3, o:o + P], xsc[:, 1 - par, j, tb * P:(tb + 1) * P], ident)
                last.then_inc(S("X_psum"), 1)

            def group_sum(g):
                pe.wait_ge(S("sq_ready"), g - 1)
                for j in range(2):
                    last = mm(wk[:, 3, 0:SEQ], ones[:, :], sq2[:, j, :], start=(j == 0), stop=(j == 1))
                last.then_inc(S("gn_psum"), 1)

            def keys_queries(g, par):
                pe.wait_ge(S("X_read"), g)
                pe.wait_ge(S("bcc_ready"), g)
                bc = bcc[:, 1 - par, :, :]
                mm(wk[:, 3, 0:SEQ], bc[:, 0, 0:P], bc[:, 1, :], start=True, stop=True)
                mm(wk[:, 3, SEQ:SEQ + P], bc[:, 0, P:SEQ], bc[:, 1, P:SEQ], start=True, stop=True)\
                    .then_inc(S("CB_psum"), 1)

            def heads_out(g):
                for m in range(4):
                    pe.wait_ge(S("M_ready"), g * 4 - 4 + m + 1)
                    if m == 0:
                        pe.wait_ge(S("L_read"), g * 4)
                    ps = slice(64 * (m % 2), 64 * (m % 2) + 64)
                    o = (m // 2) * SEQ
                    mm(wk[ps, 1, o:o + SEQ], Xt[:, 0, m * 64:(m + 1) * 64], Lm[:, m, 0:SEQ],
                       start=True, stop=False, skip_group_check=True)
                    last = mm(wk[ps, 1, o + P:o + SEQ], Xt[:, 1, m * 64:(m + 1) * 64], Lm[:, m, SEQ:SEQ + P],
                              start=False, stop=True, skip_group_check=True)
                last.then_inc(S("y_psum"), 1)

            def group_out(g, par, end=False):
                pe.wait_ge(S("Y_lo"), g - 1)
                s = arrived()
                used(down(s, lambda kk: (HH[:, par, kk, :], HL[:, par, kk, :]), end))

            def ssd_step(g, par, ssd, fin):
                if ssd:
                    pe.wait_ge(S("xs_read"), g)
                s = arrived()
                used(ch_major(s, 2))
                if ssd:
                    decay_rows(g, par, 0)
                    if fin:
                        pe.wait_ge(S("CB_read"), g - 1)
                    xs_transpose(g, par)
                pe.wait_ge(S("z_read"), g + 1)
                s = arrived()
                used(ch_major(s, 2))
                if ssd:
                    decay_rows(g, par, 1)
                if fin:
                    pe.wait_ge(S("X_read"), g)
                    group_sum(g)
                if ssd:
                    decay_rows(g, par, 2)
                    decay_rows(g, par, 3)
                    if fin:
                        pe.wait_ge(S("gn_read"), g - 1)
                    keys_queries(g, par)
                    pe.wait_ge(S("L_read"), g * 4 - 1)
                s = arrived()
                used(ch_major(s, 0, True))
                if fin:
                    group_out(g, par)
                if ssd:
                    heads_out(g)

            ssd_step(0, 0, False, False)
            ssd_step(1, 1, True, False)
            with pe.Fori(0, 3) as i:
                ring.enter(i, 2)
                ssd_step(i * 2 + 2, 0, True, True)
                ssd_step(i * 2 + 3, 1, True, True)
            ring.leave(3)
            decay_rows(SG, 0, 0)
            pe.wait_ge(S("CB_read"), SG - 1)
            group_sum(SG)
            decay_rows(SG, 0, 1)
            decay_rows(SG, 0, 2)
            decay_rows(SG, 0, 3)
            pe.wait_ge(S("gn_read"), SG - 1)
            xs_transpose(SG, 0)
            keys_queries(SG, 0)
            heads_out(SG)
            pe.wait_ge(S("CB_read"), SG)
            group_sum(SG + 1)
            group_out(SG, 0)
            group_out(SG + 1, 1, True)
            norm_transpose(5)
            for p in range(4):
                s = arrived()
                used(down(s, lambda kk: (XH[:, 2 * p + kk, :], XL[:, 2 * p + kk, :]), p == 3, first=p == 0,
                          norm=(5, 2 * p)))

            norm_transpose(6)

            def ffn_up(c, par):
                if not (isinstance(c, int) and c < 2):
                    pe.wait_ge(S("gv_read"), c - 1)
                s = arrived()
                used(ch_major(s, par, True, norm=6 if isinstance(c, int) and c == 0 else None))

            def ffn_down(c, par, end=False):
                pe.wait_ge(S("f_lo"), c + 1)
                s = arrived()
                used(down(s, lambda kk: (HH[:, par, kk, :], HL[:, par, kk, :]), end, kt=1))

            def ffn_turn(c):
                ffn_up(c + 1, 1)
                ffn_down(c, 0)
                ffn_up(c + 2, 0)
                ffn_down(c + 1, 1)

            ffn_up(0, 0)
            clear_acc()
            ffn_turn(0)
            with pe.Fori(0, FC // 2 - 2) as i:
                ring.enter(i, 1)
                ffn_turn(i * 2 + 2)
            ring.leave(FC // 2 - 2)
            ffn_up(FC - 1, 1)
            ffn_down(FC - 2, 0)
            ffn_down(FC - 1, 1, True)

        @block.scalar
        def _(act):
            ring = Ring()
            steps = Steps(act, S("act_step"))
            A = nc.scalar.activation

            for dst, src in s5_loads(ins, rows, pair):
                nc.scalar.dma_start(dst, src).then_inc(S("s5_in"), 16)

            def load_gpre(n):
                src = (ins["norm_g"][0, 0], ins["norm_g"][0, 2], ins["norm_g"][1, 0], ins["norm_g"][1, 2],
                       ins["norm1_g_2"][0], ins["norm2_g_2"][0])[n]
                nc.scalar.dma_start(gpre[:, :], src.partition_broadcast(P)).then_inc(S("gpre_in"), 16)

            def load_gpost(j):
                nc.scalar.dma_start(gpost[:, :], ins["norm_g"][j // 2, 2 * (j % 2) + 1].partition_broadcast(P))\
                    .then_inc(S("gpost_in"), 16)

            def hi_next():
                m = size(ring.n) // 2
                s, k, n = ring.next()
                if not isinstance(n, int) or n >= 4:
                    act.wait_ge(S("piece_done"), n - 3)
                for j, part in enumerate("ab"):
                    act.wait_ge(S(f"loaded_{part}{s % 2}"), k * 32 + (16 * (s // 2) + 16))
                    A(HI[:, s, j * m:(j + 1) * m], raw[:, s % 2, j, 0:m], ACT.Copy).then_inc(S(f"hi_{part}"), 1)

            def hi_to(n):
                while ring.n <= n:
                    hi_next()

            def done(n):
                act.wait_ge(S("piece_done"), n + 1)

            squares_done = [0]

            def squares(src, tb, n, sem, count):
                act.wait_ge(S(sem), count)
                if squares_done[0] >= 2:
                    act.wait_ge(S("ssq_ready"), squares_done[0] - 1)
                A(squared[:, n, :], halves(src, tb, n), ACT.Square, scale=D ** -0.5, accum_out=ssq[:, tb, n:n + 1])\
                    .then_inc(S("ssq_ready"), 1)
                squares_done[0] += 1

            def post(n, last_piece):
                for tb, (sem, count) in enumerate((("acc_first", n), ("piece_done", last_piece + 1))):
                    for n in range(2):
                        squares(acc, tb, n, sem, count)

            def pre(j):
                for tb in range(TB):
                    for n in range(2):
                        squares(h, tb, n, "h_ready", 2 * (TB * j + tb) + n + 1)

            def xT_high(n):
                for q in range(4):
                    tb, b = q // 2, q % 2
                    act.wait_ge(S("xT_psum"), 4 * n + q + 1)
                    A(XH[:, 4 * b:4 * b + 4, tb * P:(tb + 1) * P], wk[:, q, :].rearrange("p (k t) -> p k t", k=4),
                      ACT.Copy).then_inc(S("xT_hi"), 1)
                if n < 5:
                    load_gpre(n + 1)
                if 1 <= n < 4:
                    load_gpost(n)

            for n in range(2):
                squares(h, 0, n, "x_in0", 16)
            act.wait_ge(S("cols_psum"), 1)
            A(cols[:, 0, 0:ROWS[0]], accf[:, 0:ROWS[0]], ACT.Copy)
            A(pairb[:, 0:16], accf[:, P:P + 16], ACT.Copy).then_inc(S("cols_ready"), 1)
            act.wait_ge(S("cols_ready"), 1)
            A(sm5[:, 0, :], pairb[:, 0:16], ACT.Exp).then_inc(S("dt5_ready"), 1)
            for n in range(2):
                squares(h, 1, n, "x_in1", 16)
            act.wait_ge(S("ldt5_ready"), 1)
            A(sm5[:, 1, :], sm5[:, 1, :], ACT.Exp).then_inc(S("mag5_ready"), 1)
            act.wait_ge(S("ang5_ready"), 1)
            A(sm5[:, 4, :], sm5[:, 9, :], ACT.Sin)
            A(sm5[:, 5, :], sm5[:, 6, :], ACT.Sin).then_inc(S("sin5_ready"), 1)
            xT_high(0)
            hi_to(1)
            act.wait_ge(S("bc5_in"), 16 * N_BC5)
            for r in range(2):
                for par in range(2):
                    last = A(cpad[:, r, :, 64 * par:64 * par + 64], craw[:, r, :, :], ACT.Copy,
                             scale=cst[:, C_PAR + 2 * r + par:C_PAR + 2 * r + par + 1])
            last.then_inc(S("cpad_ready"), 1)
            hi_to(3)
            for b in range(2):
                done(b)
                A(uT[:, 2 * b:2 * b + 2, :], wk[:, b, :].rearrange("p (j t) -> p j t", j=2), ACT.Copy)\
                    .then_inc(S("u_ready"), 1)
            act.wait_ge(S("ct_psum"), 1)
            for r in range(2):
                A(ct5[:, r, :, :], accf[:, 512 + r * 512:1024 + r * 512].rearrange("p (q n) -> p q n", q=4), ACT.Copy)
            A(ct5n[:, :, :], accf[:, 512:1024].rearrange("p (q n) -> p q n", q=4), ACT.Copy, scale=-1.0)\
                .then_inc(S("ct_ready"), 1)
            act.wait_ge(S("cols_psum"), 2)
            A(pairb[:, 16:32], accf[:, P + 16:P + 32], ACT.Copy)
            for r, n in enumerate(ROWS[1:]):
                last = A(cols[:, 1 + r, 0:n], accf[:, 1536 + r * P:1536 + r * P + n], ACT.Copy)
            last.then_inc(S("cols_ready"), 1)
            act.wait_ge(S("bt_psum"), 1)
            for r in range(2):
                last = A(bt5[:, r, :, :], wk[:, 2 + r, :].rearrange("p (q n) -> p q n", q=4), ACT.Copy)
            last.then_inc(S("bt_ready"), 1)
            L = 128
            act.wait_ge(S("turn_low"), 1)
            for i in range(E_SPLIT):
                for r in range(2):
                    last = A(e_tab[:, i, r, L + 1:SEQ], e_tab[:, i, 0, 1:SEQ - L], ACT.Copy, scale=e_tab[:, i, r, L:L + 1])
                last.then_inc(S("turn_prod"), 1)
            act.wait_ge(S("late_in"), 16 * N_LATE)
            A(alog[:, :], alog[:, :], ACT.Exp).then_inc(S("alog_ready"), 1)
            for q in range(4):
                act.wait_ge(S("yv_ready"), q + 1)
                steps.link(A(zf[:, q, :], yv[:, q, :], ACT.Gelu_apprx_tanh))
                A(XH[:, q, :], zf[:, q, :], ACT.Copy).then_inc(S("z_hi"), 1)
                if q in (1, 2):
                    hi_to(3 + q)
            act.wait_ge(S("glu_psum"), 1)
            for b in range(2):
                if b == 1:
                    done(2)
                A(gt5[:, 2 * b:2 * b + 2, :], wk[:, b, :].rearrange("p (j t) -> p j t", j=2), ACT.Tanh, scale=0.5)\
                    .then_inc(S("gt5_ready"), 1)
            for b in range(2):
                act.wait_ge(S("z2_ready"), b + 1)
                A(XH[:, 4 + 2 * b:6 + 2 * b, :], z2f[:, 2 * b:2 * b + 2, :], ACT.Copy, scale=0.5)\
                    .then_inc(S("z2_hi"), 1)
            hi_to(6)

            post(1, 4)

            def mlp(layer, first):
                pre(2 * layer)
                xT_high(1 + 2 * layer)
                base = layer * MC

                def hidden(c, par, piece):
                    done(piece)
                    if not (isinstance(c, int) and c + base < 2):
                        act.wait_ge(S("hid_lo"), c + base - 1)
                    A(relu_b[:, par, :], wk[:, par, :], ACT.Relu).then_inc(S("hid_read"), 1)
                    act.wait_ge(S("hid_read"), c + base + 1)
                    A(HH[:, par, :, :], relu_b[:, par, :].rearrange("p (j t) -> p j t", j=2), ACT.Square)\
                        .then_inc(S("hid_hi"), 1)

                hi_to(first + 3)
                hidden(0, 0, first)

                def turn(c, piece):
                    hi_next()
                    hidden(c + 1, 1, piece)
                    hi_next()
                    hi_next()
                    hidden(c + 2, 0, piece + 2)
                    hi_next()

                turn(0, first + 1)
                with act.Fori(0, MC // 2 - 2) as i:
                    ring.enter(i, 1)
                    turn(i * 2 + 2, i * 4 + (first + 5))
                ring.leave(MC // 2 - 2)
                hi_to(first + 2 * MC)
                hidden(MC - 1, 1, first + 2 * MC - 3)
                hi_to(first + 2 * MC + 1)
                post(2 + 2 * layer, first + 2 * MC - 1)

            mlp(0, 5)

            pre(1)
            xT_high(2)

            def evac1(e, last_piece):
                done(last_piece)
                c0, w = ((QIOFF, 512), (KIOFF, ATT_TAIL), (0, 512), (512, 512), (1024, 512))[e]
                for tb in range(TB):
                    last = A(pj[:, tb, c0:c0 + w], wk[:, 2 * (e % 2) + tb, 0:w], ACT.Copy)
                last.then_inc(S("pj_read"), 1)

            def tile_evac(n, dst):
                act.wait_ge(S("qkT_psum"), n + 1)
                b, t = dst.shape[1], dst.shape[2]
                A(dst, accf[:, (n % 2) * 512:(n % 2) * 512 + b * t].rearrange("p (b t) -> p b t", b=b), ACT.Copy)\
                    .then_inc(S("qkT_read"), 1)

            def index_relu(job):
                act.wait_ge(S("rel_psum"), job + 1)
                if job >= 2:
                    act.wait_ge(S("rel_used"), job - 1)
                A(rel[:, job % 2, :], accf[:, 1024 + (job % 2) * 512:1536 + (job % 2) * 512], ACT.Relu)\
                    .then_inc(S("rel_read"), 1)

            hi_to(P_ATT + 4)
            evac1(0, P_ATT + 1)
            hi_to(P_ATT + 5)
            evac1(1, P_ATT + 2)
            hi_to(P_ATT + 6)
            tile_evac(0, qiT[:, :, 0:P])
            tile_evac(1, qiT[:, :, P:SEQ])
            tile_evac(2, kiT[:, :].rearrange("p (b t) -> p b t", b=TB))
            hi_to(P_ATT + 7)
            evac1(2, P_ATT + 4)
            index_relu(0)
            index_relu(1)
            hi_to(P_ATT + 8)
            index_relu(2)
            index_relu(3)
            hi_to(P_ATT + 9)
            evac1(3, P_ATT + 6)
            index_relu(4)
            index_relu(5)
            tile_evac(3, qT1[:, 0:4, 0:P])
            tile_evac(4, qT1[:, 0:4, P:SEQ])
            hi_to(P_ATT + 10)
            evac1(4, P_ATT + 8)
            tile_evac(5, qT1[:, 4:8, 0:P])
            tile_evac(6, qT1[:, 4:8, P:SEQ])
            tile_evac(7, kT1[:, :, 0:P])
            tile_evac(8, kT1[:, :, P:SEQ])
            def exps1(n):
                tb, h0, nh = JOBS1[n]
                K = P * (tb + 1)
                act.wait_ge(S("m1_ready"), n + 1)
                if n >= 3:
                    act.wait_ge(S("pT1_psum"), n - 2)
                for b in range(nh):
                    ks = slice(b * K, (b + 1) * K)
                    last = A(p1[:, n % 3, ks], wk[:, n % 4, ks], ACT.Exp, bias=small[:, n % 2, 1, b:b + 1], scale=HD ** -0.5,
                             accum_out=small[:, n % 2, 2, b:b + 1])
                last.then_inc(S("e1_ready"), 1)

            def copies1(n):
                act.wait_ge(S("pT1_psum"), n + 1)
                A(pT1[:, n % 2, :], accf[:, (n % 2) * 512:(n % 2 + 1) * 512], ACT.Copy).then_inc(S("pT1_ready"), 1)

            def o1_high(n):
                tb, h0, nh = JOBS1[n]
                act.wait_ge(S("o1_psum"), n + 1)
                o = 1024 + (n % 2) * 512
                hs = slice(64 * (h0 % 2), 64 * (h0 % 2) + 64)
                A(XH[hs, h0 // 2:h0 // 2 + nh, tb * P:(tb + 1) * P],
                  accf[hs, o:o + nh * P].rearrange("p (a t) -> p a t", t=P), ACT.Copy).then_inc(S("o1_hi"), 1)

            N1 = len(JOBS1)
            exps1(0)
            exps1(1)
            for n in range(N1 + 1):
                if n < N1:
                    copies1(n)
                if n >= 2:
                    o1_high(n - 2)
                if n + 2 < N1:
                    exps1(n + 2)
            o1_high(N1 - 1)
            hi_to(P_ATT + 14)
            post(3, P_ATT + 12)
            mlp(1, P_ATT + 13)

            pre(3)
            xT_high(4)

            def qk_evac(c):
                gcol = pcol(2, R_QG if c < 3 else R_KG)
                dst, t = (qT2 if c < 3 else kT2), c % 3
                for tb in range(TB):
                    n = TB * (c if c < 3 else c - 3) + tb
                    act.wait_ge(S("qkT2_psum"), n + 1)
                    A(dst[:, 4 * t:4 * t + 4, tb * P:(tb + 1) * P],
                      accf[:, (n % 2) * 512:(n % 2 + 1) * 512].rearrange("p (b t) -> p b t", b=4), ACT.Copy,
                      scale=gcol).then_inc(S("qkT2_read"), 1)

            for c in range(9):
                hi_to(last2(c) + 3)
                done(last2(c))
                if 3 <= c < 6:
                    for tb in range(TB):
                        last = A(v2[:, tb, (c - 3) * 512:(c - 2) * 512], wk[:, bank2(c) + tb, :], ACT.Copy)
                    last.then_inc(S("v2_read"), 1)
                else:
                    j = c if c < 3 else c - 3
                    if j >= 2:
                        act.wait_ge(S("qk2_normed"), j - 1)
                    A(sqh[:, j % 2, :], wk[:, bank2(c):bank2(c) + 2, :].rearrange("p b n -> p (b n)"), ACT.Square)\
                        .then_inc(S("qk2_sq"), 1)
                if c == 0:
                    hi_to(last2(1) + 2)
                    act.wait_ge(S("sp_arg"), 1)
                    A(sp2[:, :, :], sp2[:, :, :], ACT.Exp).then_inc(S("sp_exp"), 1)
                elif not 3 <= c - 1 < 6:
                    qk_evac(c - 1)
            act.wait_ge(S("cs_psum"), 1)
            for n in range(3):
                last = A(gpall[:, :, G_NB + 4 * n:G_NB + 4 * n + 4],
                         accf[:, 1024 + n * 32:1024 + (n + 1) * 32].rearrange("p (g m) -> p g m", g=SG),
                         ACT.Copy, scale=(-1.0 if n < 2 else 1.0))
            last.then_inc(S("cs_read"), 1)
            hi_to(P_B2 + 22)

            def exps2(n):
                hd, tb = JOBS2[n]
                act.wait_ge(S("m2_ready"), n + 1)
                s = p2[:, n % 3, 0:3 * P * (tb + 1)]
                A(s, s, ACT.Exp, bias=small[:, n % 2, 1, 0:1], scale=HD ** -0.5,
                  accum_out=small[:, n % 2, 2, 0:1]).then_inc(S("e2_ready"), 1)

            def copies2(n):
                hd, tb = JOBS2[n]
                w = 3 * P * (tb + 1)
                act.wait_ge(S("pT2_psum"), n + 1)
                A(pT2[n % 2][:, 0:w], accf[:, 0:w], ACT.Copy).then_inc(S("pT2_ready"), 1)

            def o2_high(j):
                hd, tb = JOBS2[2 * j + 1]
                act.wait_ge(S("o2_psum"), j + 1)
                A(OH[:, hd // 2, tb * P:(tb + 1) * P], accf[:, 1024:1024 + P], ACT.Copy).then_inc(S("o2_hi"), 1)

            def gate_evac(c):
                done(P_B2 + 19 + c)
                dst = g_ssd if c < 4 else y
                A(dst[:, :, (c % 4) * 256:(c % 4 + 1) * 256],
                  accf[:, 1536:2048].rearrange("p (b n) -> p b n", b=TB), ACT.Tanh, scale=0.5)\
                    .then_inc(S("gate_read"), 1)

            gate_evac(0)
            qk_evac(8)
            N2 = len(JOBS2)
            exps2(0)
            exps2(1)
            for n in range(N2 + 1):
                if n < N2:
                    copies2(n)
                if n + 2 < N2:
                    exps2(n + 2)
                if n >= 1 and n % 2 == 0:
                    o2_high(n // 2 - 1)
                if n < 14 and n % 2 == 0:
                    hi_to(P_B2 + 19 + n // 2 + 4)
                elif n < 14:
                    gate_evac(1 + n // 2)
            hi_to(P_SSD + 1)
            act.wait_ge(S("merged_attn"), 1)
            hi_to(P_SSD + 2)

            def decays(g, par, m):
                gpv = gp[:, 1 - par, :]
                act.wait_ge(S("L_psum"), g * 4 - 4 + m + 1)
                if not (isinstance(g, int) and g < 2):
                    act.wait_ge(S("y_psum"), g - 1)
                for blk, c in ((0, 0), (1, 8), (2, 4)):
                    last = A(Lm[:, m, blk * P:(blk + 1) * P], wk[:, m % 2, blk * P:(blk + 1) * P], ACT.Exp,
                             bias=gpv[:, G_NB + c + m:G_NB + c + m + 1])
                last.then_inc(S("L_read"), 1)

            def bc_tanh(g):
                act.wait_ge(S("bconv_ready"), g)
                if not (isinstance(g, int) and g < 2):
                    act.wait_ge(S("bcc_ready"), g - 1)
                A(btanh[:, :, :], bconv[:, :, :], ACT.Tanh).then_inc(S("btanh_ready"), 1)

            def y_squares(g, par):
                act.wait_ge(S("yz_ready"), g - 1)
                A(sq2[:, :, :], yz[:, par, :, :], ACT.Square).then_inc(S("sq_ready"), 1)

            def y_high(g, par):
                act.wait_ge(S("yn_ready"), g - 1)
                A(HH[:, par, :, :], yn[:, :, :], ACT.Copy).then_inc(S("Y_hi"), 1)

            def ssd_step(g, par, piece, ssd, fin):
                if fin:
                    hi_next()
                done(piece)
                if fin:
                    act.wait_ge(S("yz_ready"), g - 1)
                A(zc[:, par, :, :], wk[:, 2, :].rearrange("p (j t) -> p j t", j=2), ACT.Copy, scale=0.5)\
                    .then_inc(S("z_read"), 1)
                act.wait_ge(S("z_read"), g + 1)
                A(zt[:, par, :, :], zc[:, par, :, :], ACT.Tanh)
                if ssd:
                    bc_tanh(g)
                if fin:
                    y_squares(g, par)
                hi_next()
                if ssd:
                    act.wait_ge(S("gp_ready"), g)
                    decays(g, par, 0)
                done(piece + 1)
                if ssd:
                    act.wait_ge(S("xconv_ready"), g)
                A(xpad[:, :, 3:3 + SEQ], wk[:, 2, :].rearrange("p (j t) -> p j t", j=2), ACT.Copy)\
                    .then_inc(S("xs_read"), 1)
                if ssd:
                    for m in range(1, 4):
                        decays(g, par, m)
                hi_next()
                if fin:
                    y_high(g, par)
                done(piece + 2)
                if ssd:
                    act.wait_ge(S("bconv_ready"), g)
                A(bcpad[:, :, 3:3 + SEQ], wk[:, 0, :].rearrange("p (j t) -> p j t", j=2), ACT.Copy)\
                    .then_inc(S("bc_read"), 1)
                hi_next()
                act.wait_ge(S("xconv_ready"), g + 1)
                if ssd:
                    act.wait_ge(S("xsc_ready"), g)
                A(xtanh[:, :, :], xconv[:, :, :], ACT.Tanh).then_inc(S("xtanh_ready"), 1)

            ssd_step(0, 0, P_SSD, False, False)
            ssd_step(1, 1, P_SSD + 3, True, False)
            with act.Fori(0, 3) as i:
                ring.enter(i, 2)
                ssd_step(i * 2 + 2, 0, i * 8 + (P_SSD + 6), True, True)
                ssd_step(i * 2 + 3, 1, i * 8 + (P_SSD + 10), True, True)
            ring.leave(3)
            act.wait_ge(S("gn_psum"), SG - 2)
            y_squares(SG, 0)
            act.wait_ge(S("gp_ready"), SG)
            decays(SG, 0, 0)
            bc_tanh(SG)
            decays(SG, 0, 1)
            decays(SG, 0, 2)
            decays(SG, 0, 3)
            hi_next()
            act.wait_ge(S("gn_psum"), SG - 1)
            y_squares(SG + 1, 1)
            y_high(SG, 0)
            y_high(SG + 1, 1)
            hi_to(P_WOUT2 + 2)
            xT_high(5)
            first = P_WOUT2 + 4
            hi_to(first + 1)
            pre(4)
            xT_high(6)
            hi_to(first + 2)

            def ffn(c, par, piece):
                done(piece)
                if not (isinstance(c, int) and c < 2):
                    act.wait_ge(S("fconv_ready"), c - 1)
                A(fpad[:, par, :, 2:2 + SEQ], wk[:, par, :].rearrange("p (j t) -> p j t", j=2), ACT.Copy)\
                    .then_inc(S("gv_read"), 1)
                act.wait_ge(S("fconv_ready"), c + 1)
                if not (isinstance(c, int) and c < 2):
                    act.wait_ge(S("fh_ready"), c - 1)
                A(ftanh[:, par, :], fconv[:, par, 0, :], ACT.Tanh).then_inc(S("ftanh_ready"), 1)

            def ffn_hi(c, par):
                act.wait_ge(S("fh_ready"), c + 1)
                A(HH[:, par, 0, :], fhid[:, par, :], ACT.Copy).then_inc(S("f_hi"), 1)

            ffn(0, 0, first)
            ffn_hi(0, 0)

            def ffn_turn(c, piece):
                hi_next()
                ffn(c + 1, 1, piece)
                ffn_hi(c + 1, 1)
                hi_next()
                hi_next()
                ffn(c + 2, 0, piece + 2)
                ffn_hi(c + 2, 0)
                hi_next()

            ffn_turn(0, first + 1)
            with act.Fori(0, FC // 2 - 2) as i:
                ring.enter(i, 1)
                ffn_turn(i * 2 + 2, i * 4 + (first + 5))
            ring.leave(FC // 2 - 2)
            hi_to(first + 2 * FC - 1)
            ffn(FC - 1, 1, first + 2 * FC - 3)
            ffn_hi(FC - 1, 1)

        @block.vector
        def _(dve):
            ring = Ring()
            steps = Steps(dve, S("dve_step"))
            link = steps.link
            V = nc.vector
            TT, TS, STT = V.tensor_tensor, V.tensor_scalar, V.scalar_tensor_tensor

            def lo_next():
                low_part(dve, TT, ring, "a", size(ring.n))

            def lo_to(n):
                while ring.n <= n:
                    lo_next()

            def done(n):
                dve.wait_ge(S("piece_done"), n + 1)

            def rsqrt(v, t, r):
                link(TS(r.bitcast(I32), v.bitcast(I32), -0.5, 1597463007.0, ALU.mult, ALU.add))
                for _ in range(3):
                    link(STT(t, r, -0.5, r, ALU.mult, ALU.mult))
                    link(TT(t, t, v, ALU.mult))
                    link(STT(r, t, 1.5, r, ALU.add, ALU.mult))

            def pre(n, e):
                dve.wait_ge(S("gpre_in"), 16 * (n + 1))
                for tb in range(TB):
                    dve.wait_ge(S("rstd_ready"), TB * e + tb + 1)
                    for b in range(2):
                        STT(halves(y, tb, b), halves(h, tb, b), rstd[:, tb:tb + 1], gpre[:, b * 512:(b + 1) * 512],
                            ALU.mult, ALU.mult).then_inc(S("y_ready"), 1)

            def xT_low(n):
                for q in range(4):
                    tb, b = q // 2, q % 2
                    dve.wait_ge(S("xT_hi"), 4 * n + q + 1)
                    ks, ts = slice(4 * b, 4 * b + 4), slice(tb * P, (tb + 1) * P)
                    TT(XL[:, ks, ts], wk[:, q, :].rearrange("p (k t) -> p k t", k=4), XH[:, ks, ts].bitcast(F32),
                       ALU.subtract).then_inc(S("xT_lo"), 1)

            def post(j, e):
                dve.wait_ge(S("gpost_in"), 16 * (j + 1))
                for tb in range(TB):
                    for n in range(2):
                        dve.wait_ge(S("ssq_ready"), 2 * (TB * e + tb) + n + 1)
                        last = TT(halves(y, tb, n), halves(acc, tb, n), gpost[:, n * 512:(n + 1) * 512], ALU.mult)
                    link(last)
                    dve.wait_ge(S("rstd_ready"), TB * e + tb + 1)
                    for n in range(2):
                        STT(halves(h, tb, n), halves(y, tb, n), rstd[:, tb:tb + 1], halves(h, tb, n), ALU.mult, ALU.add)\
                            .then_inc(S("h_ready"), 1)

            V.memset(zero_bf[:, :], 0.0)
            V.memset(bpad[:, :, :, :], 0.0)
            V.memset(e_tab[:, :, 0, 0:1], 1.0)
            V.memset(e_tab[:, :, 1, 0:1], 0.0)
            dve.wait_ge(S("first_in"), 16)
            V.tensor_copy(id_bf[:, :], ident)
            lr, li = cols[:, 0, R_LR:R_LR + 16], cols[:, 0, R_LI:R_LI + 16]
            v5 = [sm5[:, n, :] for n in range(10)]
            dve.wait_ge(S("dt5_ready"), 1)
            TT(v5[1], lr, v5[0], ALU.mult).then_inc(S("ldt5_ready"), 1)
            link(TT(v5[2], li, v5[0], ALU.mult))
            MAGIC = 12582912.0
            link(TS(v5[3], v5[2], 1.0 / (2 * np.pi), MAGIC, ALU.mult, ALU.add))
            link(TS(v5[3], v5[3], MAGIC, None, ALU.subtract))
            link(STT(v5[9], v5[3], -6.28125, v5[2], ALU.mult, ALU.add))
            link(STT(v5[9], v5[3], -0.0019350051879882812, v5[9], ALU.mult, ALU.add))
            link(STT(v5[9], v5[3], -3.0199160501e-07, v5[9], ALU.mult, ALU.add))
            link(TS(v5[9], v5[9], 3.1415925, -3.1415925, ALU.min, ALU.max))
            link(STT(v5[6], v5[9], -1.0, v5[9], ALU.mult, ALU.max))
            TS(v5[6], v5[6], -1.0, float(np.pi / 2), ALU.mult, ALU.add).then_inc(S("ang5_ready"), 1)
            dve.wait_ge(S("sin5_ready"), 1)
            dve.wait_ge(S("mag5_ready"), 1)
            TT(v5[3], v5[1], v5[5], ALU.mult)
            TT(v5[6], v5[1], v5[4], ALU.mult)
            TT(v5[9], lr, lr, ALU.mult)
            link(TT(v5[0], li, li, ALU.mult))
            TS(v5[3], v5[3], 1.0, None, ALU.subtract)
            link(TT(v5[9], v5[9], v5[0], ALU.add))
            link(V.reciprocal(v5[9], v5[9]))
            TT(v5[7], v5[3], lr, ALU.mult)
            link(TT(v5[0], v5[6], li, ALU.mult))
            link(TT(v5[7], v5[7], v5[0], ALU.add))
            TT(v5[7], v5[7], v5[9], ALU.mult)
            TT(v5[8], v5[6], lr, ALU.mult)
            link(TT(v5[0], v5[3], li, ALU.mult))
            link(TT(v5[8], v5[8], v5[0], ALU.subtract))
            link(TT(v5[8], v5[8], v5[9], ALU.mult))
            pre(0, 0)
            xT_low(0)
            lo_to(1)
            dve.wait_ge(S("bc5_in"), 16 * N_BC5)
            fr = v5[7].unsqueeze(2).to_broadcast([P, 16, 16])
            fi = v5[8].unsqueeze(2).to_broadcast([P, 16, 16])
            bt2 = etmp[:, 0:256].rearrange("p (a b) -> p a b", a=16)
            for r in range(2):
                TT(bq[:, :, :], fr, braw[:, r, :, :], ALU.mult)
                link(TT(bt2[:, :, :], fi, braw[:, 1 - r, :, :], ALU.mult))
                for par in range(2):
                    ps = slice(64 * par, 64 * par + 64)
                    last = TT(bpad[ps, r, :, 16 * par:16 * par + 16], bq[ps, :, :], bt2[ps, :, :],
                              ALU.subtract if r == 0 else ALU.add)
                if r == 0:
                    link(last)
            last.then_inc(S("bpad_ready"), 1)
            dve.wait_ge(S("bpad_ready"), 1)
            turn_table(V, link, 0, E_SPLIT, etmp, 1, 128)
            L = 128
            TS(v5[9][:, 0:E_SPLIT].unsqueeze(2), e_tab[:, 0:E_SPLIT, 1, L:L + 1], -1.0, None, ALU.mult)\
                .then_inc(S("turn_low"), 1)
            dve.wait_ge(S("turn_low"), 1)
            for i in range(E_SPLIT):
                dve.wait_ge(S("turn_prod"), i + 1)
                for r, f in ((0, v5[9][:, i:i + 1]), (1, e_tab[:, i, 0, L:L + 1])):
                    high = e_tab[:, i, r, L + 1:SEQ]
                    last = STT(high, e_tab[:, i, 1, 1:SEQ - L], f, high, ALU.mult, ALU.add)
            link(last)
            def turned(i):
                dve.wait_ge(S("bu_psum"), i + 1)
                b = i % 2
                bu = wk[:, i % 4, :].rearrange("p (r t) -> p r t", r=2)
                TT(rotA[:, b, :, :], bu, e_tab[:, i, :, :], ALU.mult)
                TT(rotB[:, b, 0, :], bu[:, 0, :], e_tab[:, i, 1, :], ALU.mult)
                TT(rotB[:, b, 1, :], bu[:, 1, :], e_tab[:, i, 0, :], ALU.mult).then_inc(S("bu_read"), 1)

            def scan(i):
                b = i % 2
                dve.wait_ge(S("vr5_ready"), i + 1)
                if i >= 2:
                    dve.wait_ge(S("xi5_ready"), i - 1)
                mag = v5[1][:, i:i + 1].to_broadcast([P, SEQ])
                V.tensor_tensor_scan(zz[:, b, 0, :], mag, rotA[:, b, 0, :], 0.0, ALU.mult, ALU.add)
                dve.wait_ge(S("vi5_ready"), i + 1)
                V.tensor_tensor_scan(zz[:, b, 1, :], mag, rotB[:, b, 0, :], 0.0, ALU.mult, ALU.add)\
                    .then_inc(S("z5_ready"), 1)
                dve.wait_ge(S("z5_ready"), i + 1)
                if i >= 2:
                    dve.wait_ge(S("x5_used"), i - 1)
                TT(prod_re[:, b, :, :], zz[:, b, :, :], e_tab[:, i, :, :], ALU.mult).then_inc(S("xr5_ready"), 1)

            def skip(q):
                dve.wait_ge(S("x5_used"), 4 * q + 4)
                STT(yv[:, q, :], uT[:, q, :], pcol(0, R_D + q), accf[:, q * 512:q * 512 + SEQ],
                    ALU.mult, ALU.add).then_inc(S("yv_ready"), 1)

            def z_low(q):
                dve.wait_ge(S("z_hi"), q + 1)
                TT(XL[:, q, :], zf[:, q, :], XH[:, q, :].bitcast(F32), ALU.subtract).then_inc(S("z_lo"), 1)

            dve.wait_ge(S("cols_ready"), 2)
            turned(0)
            for i in range(ST):
                if i + 1 < ST:
                    if i + 1 == E_SPLIT:
                        dve.wait_ge(S("vi5_ready"), 1)
                    turned(i + 1)
                scan(i)
                if i % 4 == 1 and i > 4:
                    skip(i // 4 - 1)
                if i % 4 == 3 and i > 4:
                    z_low(i // 4 - 1)
                if i == 6 or i == 10:
                    lo_next()
            skip(3)
            z_low(3)
            lo_to(5)
            for b in range(2):
                bs = slice(2 * b, 2 * b + 2)
                dve.wait_ge(S("gt5_ready"), b + 1)
                STT(z2f[:, bs, :], gt5[:, bs, :], 1.0, zf[:, bs, :], ALU.add, ALU.mult).then_inc(S("z2_ready"), 1)
            for b in range(2):
                bs, bo = slice(2 * b, 2 * b + 2), slice(4 + 2 * b, 6 + 2 * b)
                dve.wait_ge(S("z2_hi"), b + 1)
                STT(XL[:, bo, :], z2f[:, bs, :], 0.5, XH[:, bo, :].bitcast(F32), ALU.mult, ALU.subtract)\
                    .then_inc(S("z2_lo"), 1)
            dve.wait_ge(S("consts_in"), 16)
            V.tensor_copy(neg_bf[:, :], cst[:, C_NEGT:C_NEGT + P])
            cw = cols[:, 1, :].rearrange("p (k t) -> p k t", k=4)
            for j in range(2):
                TS(gpall[:, :, G_WX + j:G_WX + 8:2], cw[:, :, j:16:2].rearrange("p k g -> p g k"), 0.5, None, ALU.mult)
                TS(gpall[:, :, G_BX + j], cols[:, 2, R_CB + j:R_CB + 16:2], 0.5, None, ALU.mult)
                V.tensor_copy(gpall[:, :, G_NG + j], cols[:, 2, R_SN + j:R_SN + 16:2])
                V.tensor_copy(gpall[:, :, G_D + j], pairb[:, 16 + j:32:2])
            TS(gpall[:, :, G_WB:G_WB + 4], cw[:, :, 16:24].rearrange("p k g -> p g k"), 0.5, None, ALU.mult)
            TS(gpall[:, :, G_WC:G_WC + 4], cw[:, :, 24:32].rearrange("p k g -> p g k"), 0.5, None, ALU.mult)
            TS(gpall[:, :, G_BB], cols[:, 2, R_CB + 16:R_CB + 24], 0.5, None, ALU.mult)
            TS(gpall[:, :, G_BC], cols[:, 2, R_CB + 24:R_CB + 32], 0.5, None, ALU.mult)
            for j, f in enumerate((0.5, 1.0)):
                for k in range(3):
                    blk, at = (3, k * 44) if k < 2 else (4, 0)
                    TS(fpall[:, :, 4 * j + k], cols[:, blk, at + FC * j:at + FC * (j + 1)], f, None, ALU.mult)
                last = TS(fpall[:, :, 4 * j + 3], cols[:, 2, R_FB + FC * j:R_FB + FC * (j + 1)], f, None, ALU.mult)
            link(last)
            lo_to(6)
            post(0, 1)

            def mlp(layer, first):
                pre(1 + 2 * layer, 2 + 4 * layer)
                xT_low(1 + 2 * layer)
                base = layer * MC

                def hidden(c, par):
                    dve.wait_ge(S("hid_read"), c + base + 1)
                    link(TT(sq_b[:, par, :], relu_b[:, par, :], relu_b[:, par, :], ALU.mult))
                    dve.wait_ge(S("hid_hi"), c + base + 1)
                    TT(HL[:, par, :, :], sq_b[:, par, :].rearrange("p (j t) -> p j t", j=2),
                       HH[:, par, :, :].bitcast(F32), ALU.subtract).then_inc(S("hid_lo"), 1)

                lo_to(first + 3)
                hidden(0, 0)
                with dve.Fori(0, (MC - 2) // 2) as i:
                    ring.enter(i, 1)
                    steps.enter(i, 2)
                    lo_next()
                    hidden(i * 2 + 1, 1)
                    lo_next()
                    lo_next()
                    hidden(i * 2 + 2, 0)
                    lo_next()
                ring.leave((MC - 2) // 2)
                steps.leave((MC - 2) // 2)
                lo_to(first + 2 * MC)
                hidden(MC - 1, 1)
                lo_to(first + 2 * MC + 1)
                post(2 * layer + 1, 3 + 4 * layer)

            mlp(0, 5)

            pre(2, 4)
            xT_low(2)
            lo_to(P_ATT + 4)
            dve.wait_ge(S("pj_read"), 1)
            for tb in range(TB):
                link(rotate(V, link, rope_i, heads_of(pj, tb, QIOFF, IH), IH, tb, [heads_of(roped, tb, 1536, IH)]))
            lo_to(P_ATT + 5)
            dve.wait_ge(S("pj_read"), 2)
            for tb in range(TB):
                rotate(V, link, rope_i, heads_of(pj, tb, KIOFF, 1), 1, tb, doubled(tb, 2048, 1)).then_inc(S("i_roped"), 1)
                dve.wait_ge(S("i_roped"), tb + 1)
            link(TS(wi_s[:, :, :], pj[:, :, WIOFF:WIOFF + IH], (IH ** -0.5) * (HD ** -0.5), None, ALU.mult))
            lo_to(P_ATT + 7)

            def rotate_keys():
                dve.wait_ge(S("pj_read"), 5)
                for tb in range(TB):
                    rotate(V, link, rope_k, heads_of(pj, tb, QW, NKV), NKV, tb, doubled(tb, QW, NKV))\
                        .then_inc(S("k_roped"), 1)
                    dve.wait_ge(S("k_roped"), tb + 1)

            caus = cst[:, C_CAUS:C_CAUS + P]
            for tb in range(TB):
                K = P * (tb + 1)
                sc, lf, kp = score[:, tb, 0:K], left[:, tb, 0:K], keep[:, tb, 0:K]
                for job, (jtb, h0, nh) in enumerate(IJOBS):
                    if jtb != tb:
                        continue
                    dve.wait_ge(S("rel_read"), job + 1)
                    for b in range(nh):
                        hd = h0 + 2 * b
                        r = rel[:, job % 2, b * K:(b + 1) * K]
                        w = wi_s[:, tb, hd:hd + 1]
                        ins_ = TS(sc, r, w, None, ALU.mult) if hd == 0 else STT(sc, r, w, sc, ALU.mult, ALU.add)
                        if b < nh - 1:
                            link(ins_)
                    ins_.then_inc(S("rel_used"), 1)
                    dve.wait_ge(S("rel_used"), job + 1)
                    if job == 3:
                        lo_to(P_ATT + 8)
                link(TT(sc[:, K - P:K], sc[:, K - P:K], caus, ALU.add))
                src = sc
                for turn in range(TOPK // 8):
                    link(V.max(top8[:, :], src))
                    link(V.match_replace(lf, top8[:, :], src, TAKEN))
                    src = lf
                    if tb == 1 and turn == 6:
                        rotate_keys()
                link(TS(kp, lf, -2e38, NEG, ALU.is_gt, ALU.mult))
                TT(kp[:, K - P:K], kp[:, K - P:K], caus, ALU.add).then_inc(S("keep_ready"), 1)

            def largest1(n):
                tb, h0, nh = JOBS1[n]
                dve.wait_ge(S("s1_psum"), n + 1)
                link(V.tensor_reduce(small[:, n % 2, 0, 0:nh], wk[:, n % 4, :].rearrange("p (a k) -> p a k", a=nh),
                                     AXIS.X, ALU.max))
                TS(small[:, n % 2, 1, 0:nh], small[:, n % 2, 0, 0:nh], -HD ** -0.5, None, ALU.mult)\
                    .then_inc(S("m1_ready"), 1)

            def normed1(n):
                tb, h0, nh = JOBS1[n]
                K = P * (tb + 1)
                dve.wait_ge(S("e1_ready"), n + 1)
                link(V.reciprocal(small[:, n % 2, 3, 0:nh], small[:, n % 2, 2, 0:nh]))
                s = p1[:, n % 3, :].rearrange("p (a k) -> p a k", a=nh)
                TT(s, s, small[:, n % 2, 3, 0:nh].unsqueeze(2).to_broadcast([P, nh, K]), ALU.mult)\
                    .then_inc(S("p1_ready"), 1)

            def o1_low(n):
                tb, h0, nh = JOBS1[n]
                dve.wait_ge(S("o1_hi"), n + 1)
                o = 1024 + (n % 2) * 512
                ts = slice(tb * P, (tb + 1) * P)
                hs = slice(64 * (h0 % 2), 64 * (h0 % 2) + 64)
                TT(XL[hs, h0 // 2:h0 // 2 + nh, ts], accf[hs, o:o + nh * P].rearrange("p (a t) -> p a t", t=P),
                   XH[hs, h0 // 2:h0 // 2 + nh, ts].bitcast(F32), ALU.subtract).then_inc(S("o1_lo"), 1)

            N1 = len(JOBS1)
            largest1(0)
            largest1(1)
            normed1(0)
            for n in range(N1 + 1):
                if n + 2 < N1:
                    largest1(n + 2)
                if n in (N1 - 2, N1 - 1):
                    lo_next()
                if n + 1 < N1:
                    normed1(n + 1)
                if n >= 2:
                    o1_low(n - 2)
            o1_low(N1 - 1)
            lo_to(P_ATT + 14)
            post(2, 5)
            mlp(1, P_ATT + 13)

            pre(4, 8)
            xT_low(4)
            def softplus():
                done(P_B2 + 2)
                for tb in range(TB):
                    last = TT(sp1[:, tb, :], wk[:, 2 + tb, 0:SH], dtb[:, :], ALU.add)
                last.then_inc(S("dt_read"), 1)
                dve.wait_ge(S("dt_read"), 1)
                link(STT(sp2[:, :, :], sp1[:, :, :], -1.0, sp1[:, :, :], ALU.mult, ALU.min))
                TS(sp1[:, :, :], sp1[:, :, :], 0.0, None, ALU.max).then_inc(S("sp_arg"), 1)
                dve.wait_ge(S("sp_exp"), 1)
                link(TS(sp3[:, :, :], sp2[:, :, :], 2.0, None, ALU.add))
                link(V.reciprocal(sp3[:, :, :], sp3[:, :, :]))
                link(TT(sp2[:, :, :], sp2[:, :, :], sp3[:, :, :], ALU.mult))
                link(TT(sp3[:, :, :], sp2[:, :, :], sp2[:, :, :], ALU.mult))
                link(TS(dt_tok[:, :, :], sp3[:, :, :], 2.0 / 17, 2.0 / 15, ALU.mult, ALU.add))
                for n in (13, 11, 9, 7, 5, 3, 1):
                    link(TT(dt_tok[:, :, :], dt_tok[:, :, :], sp3[:, :, :], ALU.mult))
                    link(TS(dt_tok[:, :, :], dt_tok[:, :, :], 2.0 / n, None, ALU.add))
                link(TT(dt_tok[:, :, :], dt_tok[:, :, :], sp2[:, :, :], ALU.mult))
                link(TT(dt_tok[:, :, :], dt_tok[:, :, :], sp1[:, :, :], ALU.add))
                dve.wait_ge(S("alog_ready"), 1)
                for tb in range(TB):
                    last = STT(a_tok[:, tb, :], dt_tok[:, tb, :], -1.0, alog[:, :], ALU.mult, ALU.mult)
                last.then_inc(S("a_ready"), 1)
                dve.wait_ge(S("a_ready"), 1)
                for tb in range(TB):
                    for at, t in ((G_DT, dt_tok), (G_A, a_tok)):
                        last = V.tensor_copy(gpall[:, :, at + 4 * tb:at + 4 * tb + 4],
                                             t[:, tb, :].rearrange("p (g m) -> p g m", g=SG))
                link(last)

            def head_norm(c):
                j, t = (c if c < 3 else c - 3), c % 3
                dve.wait_ge(S("qk2_sq"), j + 1)
                link(V.tensor_reduce(hv2[:, :], sqh[:, j % 2, :].rearrange("p (a d) -> p a d", d=HD), AXIS.X, ALU.add))
                link(TS(hv2[:, :], hv2[:, :], 1.0 / HD, EPS, ALU.mult, ALU.add))
                rsqrt(hv2[:, :], ht2[:, :], hr2[:, :])
                for tb in range(TB):
                    last = TT(qk2[:, tb, t * 512:(t + 1) * 512].rearrange("p (a d) -> p a d", d=HD),
                              wk[:, bank2(c) + tb, :].rearrange("p (a d) -> p a d", d=HD),
                              hr2[:, 8 * tb:8 * tb + 8].unsqueeze(2).to_broadcast([P, 8, HD]), ALU.mult)
                last.then_inc(S("qk2_normed"), 1)

            for c in range(9):
                lo_to(last2(c) + 3)
                if not 3 <= c < 6:
                    head_norm(c)
                if c == 0:
                    softplus()
            lo_to(P_B2 + 22)

            def masked2(n):
                hd, tb = JOBS2[n]
                K = P * (tb + 1)
                dve.wait_ge(S("s2_psum"), n + 1)
                if n >= 3:
                    dve.wait_ge(S("pT2_psum"), n - 2)
                s = p2[:, n % 3, 0:3 * K]
                o = (n % 2) * 1024
                TT(s.rearrange("p (g k) -> p g k", g=3), wkf[:, o:o + 3 * K].rearrange("p (g k) -> p g k", g=3),
                   dilm[:, :, SEQ - K:SEQ], ALU.add).then_inc(S("s2_read"), 1)
                dve.wait_ge(S("s2_read"), n + 1)
                link(V.tensor_reduce(small[:, n % 2, 0, 0:1], s, AXIS.X, ALU.max))
                TS(small[:, n % 2, 1, 0:1], small[:, n % 2, 0, 0:1], -HD ** -0.5, None, ALU.mult)\
                    .then_inc(S("m2_ready"), 1)

            def normed2(n):
                hd, tb = JOBS2[n]
                dve.wait_ge(S("e2_ready"), n + 1)
                link(V.reciprocal(small[:, n % 2, 3, 0:1], small[:, n % 2, 2, 0:1]))
                s = p2[:, n % 3, 0:3 * P * (tb + 1)]
                TS(s, s, small[:, n % 2, 3, 0:1], None, ALU.mult).then_inc(S("p2_ready"), 1)

            def o2_low(j):
                hd, tb = JOBS2[2 * j + 1]
                ts = slice(tb * P, (tb + 1) * P)
                dve.wait_ge(S("o2_hi"), j + 1)
                TT(OL[:, hd // 2, ts], accf[:, 1024:1024 + P], OH[:, hd // 2, ts].bitcast(F32), ALU.subtract)\
                    .then_inc(S("o2_lo"), 1)

            N2 = len(JOBS2)
            masked2(0)
            masked2(1)
            normed2(0)
            for n in range(N2 + 1):
                if n + 1 < N2:
                    normed2(n + 1)
                if n + 2 < N2:
                    masked2(n + 2)
                if n >= 1 and n % 2 == 0:
                    o2_low(n // 2 - 1)
                if n < 14 and n % 2 == 0:
                    lo_to(P_B2 + 19 + n // 2 + 4)
            lo_to(P_SSD + 1)
            dve.wait_ge(S("gate_read"), 8)
            TS(yf, yf, 0.5, 0.5, ALU.mult, ALU.add)
            link(TS(g_ssd[:, :, :], g_ssd[:, :, :], 0.5, 0.5, ALU.mult, ALU.add))
            done(P_SSD - 1)
            for tb in range(TB):
                last = TT(y[:, tb, :], y[:, tb, :], acc[:, tb, :], ALU.mult)
            V.memset(xpad[:, :, 0:3], 0.0)
            V.memset(bcpad[:, :, 0:3], 0.0).then_inc(S("merged_attn"), 1)
            dve.wait_ge(S("merged_attn"), 1)
            lo_to(P_SSD + 2)

            def conv4(dst, src, taps, biases):
                for k in range(4):
                    for j in range(2):
                        o, x = dst[:, j, :], src[:, j, k:k + SEQ]
                        last = TS(o, x, taps[j][0], biases[j], ALU.mult, ALU.add) if k == 0 else \
                            STT(o, x, taps[j][k], o, ALU.mult, ALU.add)
                    if k < 3:
                        link(last)
                return last

            def one(v, at):
                return v[:, at:at + 1]

            def keys_silu(g, par):
                dve.wait_ge(S("btanh_ready"), g)
                STT(bcc[:, 1 - par, :, :], btanh[:, :, :], 1.0, bconv[:, :, :], ALU.add, ALU.mult)\
                    .then_inc(S("bcc_ready"), 1)

            def xs_dt(g, par):
                gpv = gp[:, 1 - par, :]
                dve.wait_ge(S("X_psum"), g)
                if not (isinstance(g, int) and g < 2):
                    dve.wait_ge(S("y_psum"), g - 1)
                for tb in range(TB):
                    last = TT(Xt[:, tb, :].rearrange("p (m d) -> p m d", m=4),
                              wk[:, 3, tb * SEQ:(tb + 1) * SEQ].rearrange("p (m d) -> p m d", m=4),
                              gpv[:, G_DT + 4 * tb:G_DT + 4 * tb + 4].unsqueeze(2).to_broadcast([P, 4, HD]), ALU.mult)
                last.then_inc(S("X_read"), 1)

            def group_mean(g):
                dve.wait_ge(S("gn_psum"), g - 1)
                TS(gv_[:, :], wk[:, 3, 0:SEQ], 1.0 / 256, EPS, ALU.mult, ALU.add).then_inc(S("gn_read"), 1)

            def group_norm(g, par):
                dve.wait_ge(S("gn_read"), g - 1)
                rsqrt(gv_[:, :], gt_[:, :], gr_[:, :])
                for j in range(2):
                    last = STT(yn[:, j, :], yz[:, par, j, :], one(gp[:, par, :], G_NG + j), gr_[:, :], ALU.mult, ALU.mult)
                last.then_inc(S("yn_ready"), 1)
                dve.wait_ge(S("yn_ready"), g - 1)

            def y_low(g, par):
                dve.wait_ge(S("Y_hi"), g - 1)
                TT(HL[:, par, :, :], yn[:, :, :], HH[:, par, :, :].bitcast(F32), ALU.subtract).then_inc(S("Y_lo"), 1)

            def decayed(g):
                dve.wait_ge(S("CB_psum"), g)
                V.tensor_copy(cbs[:, :], wk[:, 3, 0:384]).then_inc(S("CB_read"), 1)
                dve.wait_ge(S("CB_read"), g)
                for m in range(4):
                    dve.wait_ge(S("L_read"), g * 4 - 4 + m + 1)
                    TT(Lm[:, m, :], Lm[:, m, :], cbs[:, :], ALU.mult).then_inc(S("M_ready"), 1)

            def gated(g, par):
                u = 1 - par
                link(STT(zt[:, u, :, :], zt[:, u, :, :], 1.0, zc[:, u, :, :], ALU.add, ALU.mult))
                dve.wait_ge(S("y_psum"), g)
                for j in range(2):
                    last = STT(yz[:, u, j, :], xsc[:, u, j, :], one(gp[:, u, :], G_D + j), wk[:, 1, j * SEQ:(j + 1) * SEQ],
                               ALU.mult, ALU.add)
                last.then_inc(S("y_read"), 1)
                dve.wait_ge(S("y_read"), g)
                TT(yz[:, u, :, :], yz[:, u, :, :], zt[:, u, :, :], ALU.mult).then_inc(S("yz_ready"), 1)

            def ssd_step(g, par, ssd, fin):
                gpn = gp[:, par, :]
                if fin:
                    lo_next()
                if ssd:
                    keys_silu(g, par)
                    xs_dt(g, par)
                lo_next()
                if fin:
                    group_mean(g)
                    group_norm(g, par)
                V.tensor_copy(gpn, gpall[:, bass.ds(g, 1), :].rearrange("p a n -> p (a n)")).then_inc(S("gp_ready"), 1)
                dve.wait_ge(S("gp_ready"), g + 1)
                if fin:
                    y_low(g, par)
                if ssd:
                    decayed(g)
                lo_next()
                dve.wait_ge(S("xs_read"), g + 1)
                if ssd:
                    dve.wait_ge(S("xtanh_ready"), g)
                conv4(xconv, xpad, [[one(gpn, G_WX + 2 * k + j) for k in range(4)] for j in range(2)],
                      [one(gpn, G_BX + j) for j in range(2)]).then_inc(S("xconv_ready"), 1)
                lo_next()
                dve.wait_ge(S("xtanh_ready"), g + 1)
                STT(xsc[:, par, :, :], xtanh[:, :, :], 1.0, xconv[:, :, :], ALU.add, ALU.mult).then_inc(S("xsc_ready"), 1)
                if ssd:
                    gated(g, par)
                dve.wait_ge(S("bc_read"), g + 1)
                dve.wait_ge(S("xsc_ready"), g + 1)
                conv4(bconv, bcpad, [[one(gpn, w + k) for k in range(4)] for w in (G_WB, G_WC)],
                      [one(gpn, b) for b in (G_BB, G_BC)]).then_inc(S("bconv_ready"), 1)

            ssd_step(0, 0, False, False)
            ssd_step(1, 1, True, False)
            with dve.Fori(0, 3) as i:
                ring.enter(i, 2)
                steps.enter(i, 2 * (10 + 2 * 3 + 1))
                ssd_step(i * 2 + 2, 0, True, True)
                ssd_step(i * 2 + 3, 1, True, True)
            ring.leave(3)
            steps.leave(3)
            group_mean(SG)
            keys_silu(SG, 0)
            xs_dt(SG, 0)
            decayed(SG)
            gated(SG, 0)
            group_norm(SG, 0)
            group_mean(SG + 1)
            y_low(SG, 0)
            group_norm(SG + 1, 1)
            lo_next()
            y_low(SG + 1, 1)
            lo_to(P_WOUT2 + 1)
            for tb in range(TB):
                if tb == 0:
                    dve.wait_ge(S("acc_first"), 6)
                else:
                    done(P_WOUT2 - 1)
                for n in range(2):
                    last = TT(halves(g_ssd, tb, n), halves(g_ssd, tb, n), halves(acc, tb, n), ALU.mult)
                link(last)
                for n in range(2):
                    TT(halves(y, tb, n), halves(y, tb, n), halves(g_ssd, tb, n), ALU.add).then_inc(S("y_ready"), 1)
            xT_low(5)
            lo_to(P_WOUT2 + 2)
            first = P_WOUT2 + 4
            lo_to(first + 1)
            link(V.memset(fpad[:, :, :, 0:2], 0.0))
            for tb in range(TB):
                if tb == 0:
                    dve.wait_ge(S("acc_first"), 7)
                else:
                    done(first - 1)
                for n in range(2):
                    TT(halves(h, tb, n), halves(h, tb, n), halves(acc, tb, n), ALU.add).then_inc(S("h_ready"), 1)
            pre(5, 9)
            xT_low(6)
            lo_to(first + 2)

            def ffn(c, par):
                V.tensor_copy(fp[:, par, :], fpall[:, bass.ds(c, 1), :].rearrange("p a n -> p (a n)"))\
                    .then_inc(S("fp_ready"), 1)
                dve.wait_ge(S("fp_ready"), c + 1)
                dve.wait_ge(S("gv_read"), c + 1)
                for k in range(3):
                    for j in range(2):
                        o, s, w = fconv[:, par, j, :], fpad[:, par, j, k:k + SEQ], [fp[:, par, 4 * j + n:4 * j + n + 1] for n in range(4)]
                        last = TS(o, s, w[0], w[3], ALU.mult, ALU.add) if k == 0 else STT(o, s, w[k], o, ALU.mult, ALU.add)
                    if k < 2:
                        link(last)
                last.then_inc(S("fconv_ready"), 1)
                dve.wait_ge(S("ftanh_ready"), c + 1)
                link(STT(fhid[:, par, :], ftanh[:, par, :], 1.0, fconv[:, par, 0, :], ALU.add, ALU.mult))
                TT(fhid[:, par, :], fhid[:, par, :], fconv[:, par, 1, :], ALU.mult).then_inc(S("fh_ready"), 1)
                dve.wait_ge(S("f_hi"), c + 1)
                TT(HL[:, par, 0, :], fhid[:, par, :], HH[:, par, 0, :].bitcast(F32), ALU.subtract)\
                    .then_inc(S("f_lo"), 1)

            ffn(0, 0)
            with dve.Fori(0, (FC - 2) // 2) as i:
                ring.enter(i, 1)
                steps.enter(i, 6)
                lo_next()
                ffn(i * 2 + 1, 1)
                lo_next()
                lo_next()
                ffn(i * 2 + 2, 0)
                lo_next()
            ring.leave((FC - 2) // 2)
            steps.leave((FC - 2) // 2)
            lo_to(first + 2 * FC - 1)
            ffn(FC - 1, 1)
            for tb in range(TB):
                if tb == 0:
                    dve.wait_ge(S("acc_first"), 8)
                else:
                    done(first + 2 * FC - 1)
                for n in range(2):
                    TT(halves(y, tb, n), halves(h, tb, n), halves(acc, tb, n), ALU.add).then_inc(S("out_ready"), 1)


def r128(ap):
    return ap.rearrange("(r c) -> r c", c=P)


def s5_loads(ins, rows, pair):
    return [
        (rows[R_LR:R_LR + 16, 0, :], ins["ssm_lam_re"][0].rearrange("(i q) s -> i (q s)", q=2)),
        (rows[R_LI:R_LI + 16, 0, :], ins["ssm_lam_im"][0].rearrange("(i q) s -> i (q s)", q=2)),
        (rows[R_D:R_D + 4, 0, :], ins["ssm_d"][0].rearrange("(q a) c -> q (a c)", q=4)),
        (pair[:, 0:32], ins["ssm_log_dt"]),
    ]


def bc5_loads(ins, braw, craw):
    loads = []
    for r, (b, c) in enumerate((("ssm_b_re", "ssm_c_re"), ("ssm_b_im", "ssm_c_im"))):
        loads.append((braw[:, r, :, :], ins[b][0].rearrange("(i q) s c -> (q s) i c", q=2)))
        loads.append((craw[:, r, :, :], ins[c][0].rearrange("(t a) c s -> (a c) t s", t=4)))
    return loads


def late_loads(ins, rows, pair, alog, dtb):
    loads = [
        (rows[R_SN:R_SN + 16, 2, :], r128(ins["ssd_norm_g_2"][0])),
        (rows[0:128, 1, :], ins["ssd_conv_w_2"][0].rearrange("k (t c) -> (k t) c", c=P)),
        (rows[R_CB:R_CB + 32, 2, :], r128(ins["ssd_conv_b_2"][0])),
        (rows[R_FB:R_FB + 44, 2, :], r128(ins["ffn_conv_b_2"][0])),
        (rows[0:88, 3, :], ins["ffn_conv_w_2"][0, 0:2].rearrange("k (t c) -> (k t) c", c=P)),
        (rows[0:44, 4, :], r128(ins["ffn_conv_w_2"][0, 2])),
        (pair[:, 32:64], ins["d_skip_2"]),
        (alog[:, :], ins["a_log_2"][0].partition_broadcast(P)),
        (dtb[:, :], ins["dt_bias_2"][0].partition_broadcast(P)),
    ]
    for at, name in ((R_QG, "q_norm_g_2"), (R_KG, "k_norm_g_2")):
        for part in range(2):
            loads.append((rows[at:at + 1, 2, 64 * part:64 * part + 64], ins[name]))
    return loads


def constants():
    c = np.zeros((P, C_END), np.float32)
    i, j = np.arange(P)[:, None], np.arange(P)[None, :]
    c[:, C_ID:C_ID + P] = i == j
    c[:, C_UU:C_UU + 2 * P] = np.tile(i <= j, 2)
    c[:, C_GT:C_GT + P] = i > j
    c[:, C_NEGT:C_NEGT + P] = np.where(j < i, NEG, 0)
    c[:, C_CAUS:C_CAUS + P] = np.where(j > i, NEG, 0)
    for g, (window, dil) in enumerate(((128, 1), (512, 4), (2048, 16))):
        dist = np.concatenate([P + i - j, i - j], axis=1)
        ok = (dist >= 0) & (dist <= window) & (dist % dil == 0)
        c[:, C_DIL + g * SEQ:C_DIL + (g + 1) * SEQ] = np.where(ok, 0, NEG)
    half = HD // 2
    freq = np.float32(10000.0) ** (-np.arange(half, dtype=np.float32) * np.float32(2.0) / np.float32(HD))
    ang = (np.arange(SEQ, dtype=np.float32)[:, None] * freq[None, :].astype(np.float32)).astype(np.float32)
    cos, sin = np.cos(ang), np.sin(ang)
    for b in range(TB):
        ts = slice(b * P, (b + 1) * P)
        c[:, C_COS + b * HD:C_COS + (b + 1) * HD] = np.concatenate([cos[ts], cos[ts]], axis=1)
        c[:, C_SIN + b * HD:C_SIN + (b + 1) * HD] = np.concatenate([-sin[ts], sin[ts]], axis=1)
    c[0, C_SEL:C_SEL + 64] = 1
    c[0, C_SEL + P + 64:C_SEL + 2 * P] = 1
    odd = (np.arange(P) // CH) % 2
    c[:, C_PAR], c[:, C_PAR + 1], c[:, C_PAR + 2], c[:, C_PAR + 3] = 1 - odd, odd, odd - 1, -odd
    return c


_INS = ["x", "norm_g", "mlp_w1", "mlp_w2", "ssm_w_in", "ssm_lam_re", "ssm_lam_im", "ssm_log_dt", "ssm_b_re",
        "ssm_b_im", "ssm_c_re", "ssm_c_im", "ssm_d", "ssm_w_glu", "ssm_w_out", "att_w_in", "att_w_out", "norm1_g_2",
        "w_in_2", "ssd_conv_w_2", "ssd_conv_b_2", "dt_bias_2", "a_log_2", "d_skip_2", "ssd_norm_g_2",
        "w_ssd_proj_2", "q_norm_g_2", "k_norm_g_2", "w_attn_proj_2", "w_out_2", "norm2_g_2", "w_up_2",
        "ffn_conv_w_2", "ffn_conv_b_2", "w_down_2"]


def kernel(**inputs):
    import concourse.bacc as bacc
    from concourse.bass_utils import run_bass_kernel_spmd

    nc = bacc.Bacc("TRN2", target_bir_lowering=False, num_devices=1)
    arrays, aps = {}, {}
    for name in _INS:
        a = np.ascontiguousarray(inputs[name])
        arrays[f"in_{name}"] = a
        aps[name] = nc.dram_tensor(f"in_{name}", a.shape, mybir.dt.from_np(a.dtype), kind="ExternalInput").ap()
    arrays["consts"] = constants()
    aps["consts"] = nc.dram_tensor("consts", (P, C_END), F32, kind="ExternalInput").ap()
    out = nc.dram_tensor("out", (1, SEQ, D), F32, kind="ExternalOutput").ap()
    build(nc, aps, out)
    r = run_bass_kernel_spmd(nc, [arrays], core_ids=[0])
    return r.results[0]["out"]
```
